# Optimizing a Trainium2 kernel written in Bass

```python
import math
import jax, jax.numpy as jnp
from jax import lax
import numpy as np
import jax
import jax.numpy as jnp

D_MODEL = 1024
BATCH = 1
SEQ = 256
DEPTH = 1

CHUNK = 64
Q_BLOCK = 128
SB_HEAD_DIM = 64
SB_HEADS = D_MODEL // 128
SB_WIDTH = SB_HEADS * SB_HEAD_DIM
SSM_WIDTH = D_MODEL // 2
SSM_GROUP = 16
SSM_GROUPS = SSM_WIDTH // SSM_GROUP
SSM_STATE = 64
N_MEM = 256
XA_HEADS = 4
XA_HEAD_DIM = D_MODEL // XA_HEADS
D_FF = 11 * D_MODEL // 4
CONV_WIDTH = 3
RMS_EPS = 1e-6
IN_WIDTH = 3 * SB_WIDTH + SSM_WIDTH + 2 * D_MODEL


def rms_norm(x, gain):
    xf = x.astype(jnp.float32)
    y = xf * lax.rsqrt(jnp.mean(xf * xf, axis=-1, keepdims=True) + RMS_EPS)
    return (y * gain.astype(jnp.float32)).astype(x.dtype)

def stick_breaking_attention(q, k, v):
    b, s, _ = q.shape
    n_blk = s // Q_BLOCK
    qh = q.reshape(b, n_blk, Q_BLOCK, SB_HEADS, SB_HEAD_DIM).transpose(1, 0, 3, 2, 4)
    kh = k.reshape(b, s, SB_HEADS, SB_HEAD_DIM).transpose(0, 2, 1, 3)
    vh = v.reshape(b, s, SB_HEADS, SB_HEAD_DIM).transpose(0, 2, 1, 3)
    key_pos = jnp.arange(s, dtype=jnp.int32)
    scale = SB_HEAD_DIM ** -0.5

    def one_block(args):
        q_blk, blk = args
        z = jnp.einsum('bhqd,bhkd->bhqk', q_blk, kh).astype(jnp.float32) * scale
        q_pos = blk * Q_BLOCK + jnp.arange(Q_BLOCK, dtype=jnp.int32)
        causal = key_pos[None, :] < q_pos[:, None]
        log_fail = jnp.where(causal, jax.nn.log_sigmoid(-z), 0.0)
        log_remain = lax.cumsum(log_fail, axis=3, reverse=True) - log_fail
        w = jnp.where(causal, jnp.exp(jax.nn.log_sigmoid(z) + log_remain), 0.0)
        return jnp.einsum('bhqk,bhkd->bhqd', w.astype(vh.dtype), vh)

    out = lax.map(one_block, (qh, jnp.arange(n_blk, dtype=jnp.int32)))
    return out.transpose(1, 0, 3, 2, 4).reshape(b, s, SB_WIDTH)

def _linear_recurrence_combine(e_i, e_j):
    a_i, b_i = e_i
    a_j, b_j = e_j
    return a_j * a_i, a_j * b_i + b_j

def s5_branch(u, a_re, a_im, log_dt, b_re, b_im, c_re, c_im, d_skip, w_glu, b_glu):
    b, s, _ = u.shape
    f32 = jnp.float32
    ug = u.astype(f32).reshape(b, s, SSM_GROUPS, SSM_GROUP)
    lam = lax.complex(a_re.astype(f32), a_im.astype(f32))
    dt = jnp.exp(log_dt.astype(f32))[:, None]
    lam_bar = jnp.exp(lam * dt)
    b_mat = lax.complex(b_re.astype(f32), b_im.astype(f32))
    b_bar = ((lam_bar - 1.0) / lam)[:, :, None] * b_mat
    bu = jnp.einsum('gpc,bsgc->bsgp', b_bar, ug.astype(jnp.complex64))
    decay = jnp.broadcast_to(lam_bar, (1, s, SSM_GROUPS, SSM_STATE))
    _, states = lax.associative_scan(_linear_recurrence_combine, (decay, bu), axis=1)
    c_mat = lax.complex(c_re.astype(f32), c_im.astype(f32))
    y = jnp.einsum('gcp,bsgp->bsgc', c_mat, states).real
    y = y + d_skip.astype(f32).reshape(SSM_GROUPS, SSM_GROUP) * ug
    y = jax.nn.gelu(y.reshape(b, s, SSM_WIDTH)).astype(u.dtype)
    return y * jax.nn.sigmoid(y @ w_glu + b_glu)

def memory_cross_attention(h, mem_n, wq, wk, wv, wo):
    b, s, _ = h.shape
    m = mem_n.shape[1]
    q = (h @ wq).reshape(b, s, XA_HEADS, XA_HEAD_DIM)
    k = (mem_n @ wk).reshape(b, m, XA_HEADS, XA_HEAD_DIM)
    v = (mem_n @ wv).reshape(b, m, XA_HEADS, XA_HEAD_DIM)
    scores = jnp.einsum('bqhd,bmhd->bhqm', q, k).astype(jnp.float32) * (XA_HEAD_DIM ** -0.5)
    p = jax.nn.softmax(scores, axis=-1).astype(v.dtype)
    o = jnp.einsum('bhqm,bmhd->bqhd', p, v).reshape(b, s, D_MODEL)
    return o @ wo

def conv_ffn(h, w_up, conv_w, conv_b, w_down):
    up = h @ w_up
    up = lax.conv_general_dilated(
        up, conv_w[:, None, :].astype(up.dtype), window_strides=(1,),
        padding=[(CONV_WIDTH - 1, 0)], dimension_numbers=('NWC', 'WIO', 'NWC'),
        feature_group_count=2 * D_FF) + conv_b
    gate, val = jnp.split(up, 2, axis=-1)
    return (jax.nn.gelu(gate) * val) @ w_down

def _normal(key, shape, scale):
    return jax.random.normal(key, shape, jnp.float32) * scale

def first_inputs(seed: int = 0) -> dict:
    key = jax.random.key(seed)
    ks = jax.random.split(key, 32)
    L, D, G, P, C = DEPTH, D_MODEL, SSM_GROUPS, SSM_STATE, SSM_GROUP
    gain = lambda k: 1.0 + _normal(k, (L, D), 0.05)
    return {
        "x": _normal(ks[0], (BATCH, SEQ, D), 1.0),
        "mem": _normal(ks[1], (BATCH, N_MEM, D), 1.0),
        "norm_mix_pre": gain(ks[2]),
        "norm_mix_post": gain(ks[3]),
        "w_in": _normal(ks[4], (L, D, IN_WIDTH), D ** -0.5),
        "b_gate": _normal(ks[5], (L, 2 * D), 0.01),
        "ssm_a_re": -0.5 + _normal(ks[6], (L, G, P), 0.01),
        "ssm_a_im": jnp.pi * jnp.arange(P, dtype=jnp.float32)[None, None, :] + _normal(ks[7], (L, G, P), 0.01),
        "ssm_log_dt": jax.random.uniform(ks[8], (L, G), jnp.float32, math.log(1e-3), math.log(1e-1)),
        "ssm_b_re": _normal(ks[9], (L, G, P, C), (2 * C) ** -0.5),
        "ssm_b_im": _normal(ks[10], (L, G, P, C), (2 * C) ** -0.5),
        "ssm_c_re": _normal(ks[11], (L, G, C, P), (2 * P) ** -0.5),
        "ssm_c_im": _normal(ks[12], (L, G, C, P), (2 * P) ** -0.5),
        "ssm_d": _normal(ks[13], (L, SSM_WIDTH), 1.0),
        "ssm_w_glu": _normal(ks[14], (L, SSM_WIDTH, SSM_WIDTH), SSM_WIDTH ** -0.5),
        "ssm_b_glu": _normal(ks[15], (L, SSM_WIDTH), 0.01),
        "w_branch_attn": _normal(ks[16], (L, SB_WIDTH, D), SB_WIDTH ** -0.5),
        "w_branch_ssm": _normal(ks[17], (L, SSM_WIDTH, D), SSM_WIDTH ** -0.5),
        "w_out": _normal(ks[18], (L, D, D), D ** -0.5),
        "norm_xa_pre": gain(ks[19]),
        "norm_xa_post": gain(ks[20]),
        "norm_mem": gain(ks[21]),
        "xa_wq": _normal(ks[22], (L, D, D), D ** -0.5),
        "xa_wk": _normal(ks[23], (L, D, D), D ** -0.5),
        "xa_wv": _normal(ks[24], (L, D, D), D ** -0.5),
        "xa_wo": _normal(ks[25], (L, D, D), D ** -0.5),
        "norm_ffn_pre": gain(ks[26]),
        "norm_ffn_post": gain(ks[27]),
        "ffn_w_up": _normal(ks[28], (L, D, 2 * D_FF), D ** -0.5),
        "ffn_conv_w": _normal(ks[29], (L, CONV_WIDTH, 2 * D_FF), CONV_WIDTH ** -0.5),
        "ffn_conv_b": _normal(ks[30], (L, 2 * D_FF), 0.01),
        "ffn_w_down": _normal(ks[31], (L, D_FF, D), D_FF ** -0.5),
    }

def first_block(x, mem, norm_mix_pre, norm_mix_post, w_in, b_gate,
              ssm_a_re, ssm_a_im, ssm_log_dt, ssm_b_re, ssm_b_im, ssm_c_re, ssm_c_im,
              ssm_d, ssm_w_glu, ssm_b_glu, w_branch_attn, w_branch_ssm, w_out,
              norm_xa_pre, norm_xa_post, norm_mem, xa_wq, xa_wk, xa_wv, xa_wo,
              norm_ffn_pre, norm_ffn_post, ffn_w_up, ffn_conv_w, ffn_conv_b, ffn_w_down):
    splits = (SB_WIDTH, 2 * SB_WIDTH, 3 * SB_WIDTH, 3 * SB_WIDTH + SSM_WIDTH)
    for l in range(DEPTH):
        h = rms_norm(x, norm_mix_pre[l])
        proj = h @ w_in[l]
        q, k, v, u, gate_logits = jnp.split(proj, splits, axis=-1)
        gate_attn, gate_ssm = jnp.split(jax.nn.sigmoid(gate_logits + b_gate[l]), 2, axis=-1)
        o_attn = stick_breaking_attention(q, k, v)
        o_ssm = s5_branch(u, ssm_a_re[l], ssm_a_im[l], ssm_log_dt[l], ssm_b_re[l], ssm_b_im[l],
                          ssm_c_re[l], ssm_c_im[l], ssm_d[l], ssm_w_glu[l], ssm_b_glu[l])
        merged = gate_attn * (o_attn @ w_branch_attn[l]) + gate_ssm * (o_ssm @ w_branch_ssm[l])
        x = x + rms_norm(merged @ w_out[l], norm_mix_post[l])
        h = rms_norm(x, norm_xa_pre[l])
        mem_n = rms_norm(mem, norm_mem[l])
        xa = memory_cross_attention(h, mem_n, xa_wq[l], xa_wk[l], xa_wv[l], xa_wo[l])
        x = x + rms_norm(xa, norm_xa_post[l])
        h = rms_norm(x, norm_ffn_pre[l])
        f = conv_ffn(h, ffn_w_up[l], ffn_conv_w[l], ffn_conv_b[l], ffn_w_down[l])
        x = x + rms_norm(f, norm_ffn_post[l])
    return x


DEPTH_2 = 2

GRID_W = 64
CTX_LEN = 256
N_MIXERS = 2
N_HEADS = 8
HEAD_DIM = D_MODEL // N_HEADS
N_GROUPS = 4
EXPERTS_PER_GROUP = 8
N_EXPERTS = N_GROUPS * EXPERTS_PER_GROUP
TOP_K = 2
D_EXPERT = D_MODEL // 2
MOE_BLOCK = 128
N_MOD = 6
EPS = 1e-6


def rmsnorm(x, g):
    xf = x.astype(jnp.float32)
    y = xf * lax.rsqrt(jnp.mean(xf * xf, axis=-1, keepdims=True) + EPS)
    return (y * g.astype(jnp.float32)).astype(x.dtype)

def modulate(x, g, shift, scale):
    return rmsnorm(x, g) * (1 + scale) + shift

def ada_params(cond, w, b):
    m = jax.nn.silu(cond) @ w + b
    return jnp.split(m[..., None, :], N_MOD, axis=-1)

def conv3_seq(x, w):
    xp = jnp.pad(x, ((0, 0), (1, 1), (0, 0)))
    return xp[:, :-2] * w[0] + xp[:, 1:-1] * w[1] + xp[:, 2:] * w[2]

def conv3_grid(x, w, rows):
    b, s, ch = x.shape
    half = ch // 2
    g = x.reshape(b, rows, GRID_W, ch)
    wh, wv = w[:, :half], w[:, half:]
    ph = jnp.pad(g[..., :half], ((0, 0), (0, 0), (1, 1), (0, 0)))
    yh = ph[:, :, :-2] * wh[0] + ph[:, :, 1:-1] * wh[1] + ph[:, :, 2:] * wh[2]
    pv = jnp.pad(g[..., half:], ((0, 0), (1, 1), (0, 0), (0, 0)))
    yv = pv[:, :-2] * wv[0] + pv[:, 1:-1] * wv[1] + pv[:, 2:] * wv[2]
    return jnp.concatenate([yh, yv], axis=-1).reshape(b, s, ch)

def l2norm(t):
    return t * lax.rsqrt(jnp.sum(t * t, axis=-1, keepdims=True) + EPS)

def to_chunks(t):
    b, l, h = t.shape[:3]
    t = t.reshape(b, l // CHUNK, CHUNK, h, *t.shape[3:])
    return jnp.moveaxis(t, (1, 3), (0, 2))

def from_chunks(t):
    t = jnp.moveaxis(t, (0, 2), (1, 3))
    b, n, c, h, d = t.shape
    return t.reshape(b, n * c, h, d)

def gated_delta_scan(q, k, v, g, beta, s0, with_output):
    qc, kc, vc = to_chunks(q), to_chunks(k), to_chunks(v)
    gc = jnp.cumsum(to_chunks(g), axis=-1)
    bc = to_chunks(beta)
    pos = jnp.arange(CHUNK)
    incl = pos[:, None] >= pos[None, :]
    decay = jnp.exp(jnp.where(incl, gc[..., :, None] - gc[..., None, :], -jnp.inf))
    kb = kc * bc[..., None]
    lmat = jnp.where(pos[:, None] > pos[None, :],
                     jnp.einsum('nbhid,nbhjd->nbhij', kb, kc) * decay, 0.0)
    rhs = jnp.concatenate([vc * bc[..., None], kb * jnp.exp(gc)[..., None]], axis=-1)
    sol = lax.linalg.triangular_solve(lmat, rhs, left_side=True, lower=True, unit_diagonal=True)
    dv = vc.shape[-1]
    u, w = sol[..., :dv], sol[..., dv:]
    k_dec = kc * jnp.exp(gc[..., -1:] - gc)[..., None]
    g_last = jnp.exp(gc[..., -1])
    xs = (u, w, k_dec, g_last)
    if with_output:
        xs = xs + (qc * jnp.exp(gc)[..., None], jnp.einsum('nbhid,nbhjd->nbhij', qc, kc) * decay)

    def step(s, inp):
        u_i, w_i, kd_i, gl_i = inp[:4]
        v_new = u_i - jnp.einsum('bhcd,bhde->bhce', w_i, s)
        s_next = s * gl_i[..., None, None] + jnp.einsum('bhcd,bhce->bhde', kd_i, v_new)
        if with_output:
            qd_i, qk_i = inp[4:]
            o = jnp.einsum('bhcd,bhde->bhce', qd_i, s) + jnp.einsum('bhij,bhje->bhie', qk_i, v_new)
            return s_next, o
        return s_next, None

    s_final, o = lax.scan(step, s0, xs)
    return s_final, (from_chunks(o) if with_output else None)

def deltanet_mixer(h_lat, h_ctx, w_in, conv_w, a_log, dt_bias, onorm, w_out, ctx_out):
    d, nh, f32 = D_MODEL, N_HEADS, jnp.float32

    def project(h):
        b, l, _ = h.shape
        p = h @ w_in
        qkv = jax.nn.silu(conv3_seq(p[..., :3 * d], conv_w))
        q, k, v = (t.reshape(b, l, nh, HEAD_DIM).astype(f32) for t in jnp.split(qkv, 3, axis=-1))
        q = l2norm(q) * HEAD_DIM ** -0.5
        k = l2norm(k)
        z = p[..., 3 * d:4 * d]
        beta = jax.nn.sigmoid(p[..., 4 * d:4 * d + 2 * nh].astype(f32)).reshape(b, l, 2, nh)
        a_in = p[..., 4 * d + 2 * nh:].astype(f32).reshape(b, l, 2, nh)
        g = -jnp.exp(a_log.astype(f32)) * jax.nn.softplus(a_in + dt_bias.astype(f32))
        return q, k, v, z, beta, g

    def bidir(q, k, v, beta, g, s_f, s_b, with_output):
        flip = lambda t: t[:, ::-1]
        rf = gated_delta_scan(q, k, v, g[:, :, 0], beta[:, :, 0], s_f, with_output)
        rb = gated_delta_scan(flip(q), flip(k), flip(v), flip(g[:, :, 1]), flip(beta[:, :, 1]),
                              s_b, with_output)
        return rf, rb

    def finish(o, z):
        b, l = z.shape[:2]
        o = o * lax.rsqrt(jnp.mean(o * o, axis=-1, keepdims=True) + EPS) * onorm.astype(f32)
        y = o.astype(z.dtype) * jax.nn.silu(z).reshape(b, l, nh, HEAD_DIM)
        return y.reshape(b, l, d) @ w_out

    qc, kc, vc, zc, bc, gc = project(h_ctx)
    s_zero = jnp.zeros((h_ctx.shape[0], nh, HEAD_DIM, HEAD_DIM), f32)
    (sf, ocf), (sb, ocb) = bidir(qc, kc, vc, bc, gc, s_zero, s_zero, ctx_out)
    y_ctx = finish(ocf + ocb[:, ::-1], zc) if ctx_out else None
    ql, kl, vl, zl, bl, gl = project(h_lat)
    (_, olf), (_, olb) = bidir(ql, kl, vl, bl, gl, sf, sb, True)
    y_lat = finish(olf + olb[:, ::-1], zl)
    return y_lat, y_ctx

def shortconv_mixer(h, w_in, conv_w, w_out, rows):
    gate_b, gate_c, hx = jnp.split(h @ w_in, 3, axis=-1)
    u = gate_c * hx
    y = conv3_grid(u, conv_w, rows) if rows is not None else conv3_seq(u, conv_w)
    return (gate_b * y) @ w_out

def hier_moe(h, router_g, router_e, w1, w3, w2):
    f32 = jnp.float32
    t, d = h.shape
    hf = h.astype(f32)
    pg = jax.nn.softmax(hf @ router_g.astype(f32), axis=-1)
    gi = jnp.argmax(pg, axis=-1).astype(jnp.int32)
    pg_sel = jnp.take_along_axis(pg, gi[:, None], axis=-1)
    le = (hf @ router_e.astype(f32)).reshape(t, N_GROUPS, EXPERTS_PER_GROUP)
    le_sel = jnp.take_along_axis(le, gi[:, None, None], axis=1)[:, 0]
    pk, ik = lax.top_k(jax.nn.softmax(le_sel, axis=-1), TOP_K)
    wts = pg_sel * pk / jnp.sum(pk, axis=-1, keepdims=True)
    eid = gi[:, None] * EXPERTS_PER_GROUP + ik.astype(jnp.int32)

    n = t * TOP_K
    n_blocks = -(-n // MOE_BLOCK) + N_EXPERTS
    cap = n_blocks * MOE_BLOCK
    flat_e = eid.reshape(-1)
    flat_tok = jnp.repeat(jnp.arange(t, dtype=jnp.int32), TOP_K)
    flat_w = wts.reshape(-1)
    order = jnp.argsort(flat_e)
    se = flat_e[order]
    counts = jnp.zeros((N_EXPERTS,), jnp.int32).at[flat_e].add(1)
    padded = (counts + MOE_BLOCK - 1) // MOE_BLOCK * MOE_BLOCK
    ends_pad = jnp.cumsum(padded)
    start_pad = ends_pad - padded
    start_raw = jnp.cumsum(counts) - counts
    dest = start_pad[se] + jnp.arange(n, dtype=jnp.int32) - start_raw[se]
    buf_tok = jnp.full((cap,), t, jnp.int32).at[dest].set(flat_tok[order])
    buf_w = jnp.zeros((cap,), f32).at[dest].set(flat_w[order])
    block_e = jnp.minimum(
        jnp.searchsorted(ends_pad, jnp.arange(n_blocks, dtype=jnp.int32) * MOE_BLOCK, side='right'),
        N_EXPERTS - 1).astype(jnp.int32)
    h_pad = jnp.concatenate([h, jnp.zeros((1, d), h.dtype)], axis=0)
    xb = h_pad[buf_tok].reshape(n_blocks, MOE_BLOCK, d)

    def expert_block(args):
        xi, e = args
        return (jax.nn.silu(xi @ w1[e]) * (xi @ w3[e])) @ w2[e]

    yb = lax.map(expert_block, (xb, block_e)).reshape(cap, d)
    y = jax.ops.segment_sum(yb * buf_w[:, None].astype(yb.dtype), buf_tok, num_segments=t + 1)
    return y[:t]

def second_inputs(seed: int = 0) -> dict:
    key = jax.random.key(seed)
    ks = jax.random.split(key, 24)
    d, nh, f32 = D_MODEL, N_HEADS, jnp.float32
    n_a = (DEPTH_2 + N_MIXERS - 1) // N_MIXERS
    n_b = DEPTH_2 // N_MIXERS

    def nrm(k, shape, scale):
        return jax.random.normal(k, shape, f32) * scale

    dt = jnp.exp(jax.random.uniform(ks[10], (n_a, 2, nh), f32, math.log(1e-3), math.log(1e-1)))
    return {
        'x': nrm(ks[0], (BATCH, SEQ, d), 1.0),
        'c': nrm(ks[1], (BATCH, d), 1.0),
        'ctx': nrm(ks[2], (BATCH, CTX_LEN, d), 1.0),
        'c_ctx': nrm(ks[3], (d,), 1.0),
        'ada_w': nrm(ks[4], (DEPTH_2, d, N_MOD * d), 0.5 * d ** -0.5),
        'ada_b': nrm(ks[5], (DEPTH_2, N_MOD * d), 0.02),
        'norm_mix': 1.0 + nrm(ks[6], (DEPTH_2, d), 0.05),
        'norm_ffn': 1.0 + nrm(ks[7], (DEPTH_2, d), 0.05),
        'w_in_a': nrm(ks[8], (n_a, d, 4 * d + 4 * nh), d ** -0.5),
        'conv_a': nrm(ks[9], (n_a, 3, 3 * d), 3 ** -0.5),
        'a_log_a': jnp.log(jax.random.uniform(ks[11], (n_a, 2, nh), f32, 1.0, 16.0)),
        'dt_bias_a': dt + jnp.log(-jnp.expm1(-dt)),
        'onorm_a': 1.0 + nrm(ks[12], (n_a, HEAD_DIM), 0.05),
        'w_out_a': nrm(ks[13], (n_a, d, d), d ** -0.5),
        'w_in_b': nrm(ks[14], (n_b, d, 3 * d), d ** -0.5),
        'conv_b': nrm(ks[15], (n_b, 3, d), 3 ** -0.5),
        'w_out_b': nrm(ks[16], (n_b, d, d), d ** -0.5),
        'router_g': nrm(ks[17], (DEPTH_2, d, N_GROUPS), d ** -0.5),
        'router_e': nrm(ks[18], (DEPTH_2, d, N_EXPERTS), d ** -0.5),
        'w1': nrm(ks[19], (DEPTH_2, N_EXPERTS, d, D_EXPERT), d ** -0.5),
        'w3': nrm(ks[20], (DEPTH_2, N_EXPERTS, d, D_EXPERT), d ** -0.5),
        'w2': nrm(ks[21], (DEPTH_2, N_EXPERTS, D_EXPERT, d), D_EXPERT ** -0.5),
        'final_norm': 1.0 + nrm(ks[22], (d,), 0.05),
    }

def second_block(x, c, ctx, c_ctx, ada_w, ada_b, norm_mix, norm_ffn,
              w_in_a, conv_a, a_log_a, dt_bias_a, onorm_a, w_out_a,
              w_in_b, conv_b, w_out_b, router_g, router_e, w1, w3, w2, final_norm):
    b, s, d = x.shape
    rows = s // GRID_W
    kinds = [i % N_MIXERS for i in range(DEPTH_2)]
    for i in range(DEPTH_2):
        kind, j = kinds[i], i // N_MIXERS
        ctx_live = 0 in kinds[i + 1:]
        sh_m, sc_m, gt_m, sh_f, sc_f, gt_f = ada_params(c, ada_w[i], ada_b[i])
        if kind == 0 or ctx_live:
            csh_m, csc_m, cgt_m, csh_f, csc_f, cgt_f = ada_params(c_ctx, ada_w[i], ada_b[i])
            hc = modulate(ctx, norm_mix[i], csh_m, csc_m)
        h = modulate(x, norm_mix[i], sh_m, sc_m)
        if kind == 0:
            y, yc = deltanet_mixer(h, hc, w_in_a[j], conv_a[j], a_log_a[j], dt_bias_a[j],
                                   onorm_a[j], w_out_a[j], ctx_live)
        else:
            y = shortconv_mixer(h, w_in_b[j], conv_b[j], w_out_b[j], rows)
            yc = shortconv_mixer(hc, w_in_b[j], conv_b[j], w_out_b[j], None) if ctx_live else None
        x = x + gt_m * y
        hf = modulate(x, norm_ffn[i], sh_f, sc_f).reshape(b * s, d)
        if ctx_live:
            ctx = ctx + cgt_m * yc
            hcf = modulate(ctx, norm_ffn[i], csh_f, csc_f).reshape(-1, d)
            out = hier_moe(jnp.concatenate([hf, hcf], axis=0), router_g[i], router_e[i],
                           w1[i], w3[i], w2[i])
            x = x + gt_f * out[:b * s].reshape(b, s, d)
            ctx = ctx + cgt_f * out[b * s:].reshape(ctx.shape)
        else:
            x = x + gt_f * hier_moe(hf, router_g[i], router_e[i], w1[i], w3[i], w2[i]).reshape(b, s, d)
    return rmsnorm(x, final_norm)


def setup_inputs(seed=0):
    out = dict(first_inputs(seed))
    for name, value in second_inputs(seed + 1).items():
        if name != "x":
            out[name + "_2"] = value
    return out


def reference(
    x, mem, norm_mix_pre, norm_mix_post, w_in, b_gate, ssm_a_re, ssm_a_im, ssm_log_dt, ssm_b_re,
    ssm_b_im, ssm_c_re, ssm_c_im, ssm_d, ssm_w_glu, ssm_b_glu, w_branch_attn, w_branch_ssm,
    w_out, norm_xa_pre, norm_xa_post, norm_mem, xa_wq, xa_wk, xa_wv, xa_wo, norm_ffn_pre,
    norm_ffn_post, ffn_w_up, ffn_conv_w, ffn_conv_b, ffn_w_down, c_2, ctx_2, c_ctx_2, ada_w_2,
    ada_b_2, norm_mix_2, norm_ffn_2, w_in_a_2, conv_a_2, a_log_a_2, dt_bias_a_2, onorm_a_2,
    w_out_a_2, w_in_b_2, conv_b_2, w_out_b_2, router_g_2, router_e_2, w1_2, w3_2, w2_2,
    final_norm_2,
):
    x = first_block(
        x, mem, norm_mix_pre, norm_mix_post, w_in, b_gate, ssm_a_re, ssm_a_im, ssm_log_dt,
        ssm_b_re, ssm_b_im, ssm_c_re, ssm_c_im, ssm_d, ssm_w_glu, ssm_b_glu, w_branch_attn,
        w_branch_ssm, w_out, norm_xa_pre, norm_xa_post, norm_mem, xa_wq, xa_wk, xa_wv, xa_wo,
        norm_ffn_pre, norm_ffn_post, ffn_w_up, ffn_conv_w, ffn_conv_b, ffn_w_down,
    )
    return second_block(
        x, c_2, ctx_2, c_ctx_2, ada_w_2, ada_b_2, norm_mix_2, norm_ffn_2, w_in_a_2, conv_a_2,
        a_log_a_2, dt_bias_a_2, onorm_a_2, w_out_a_2, w_in_b_2, conv_b_2, w_out_b_2, router_g_2,
        router_e_2, w1_2, w3_2, w2_2, final_norm_2,
    )


_drawn_inputs = setup_inputs


def setup_inputs(seed=0):
    import zlib

    import numpy as np

    out = dict(_drawn_inputs(seed))
    spreads = {}
    factors = {'b_gate': 8.0,
     'ssm_a_re': 8.0,
     'ssm_b_re': 3.762,
     'ssm_b_im': 3.493,
     'ssm_c_re': 3.444,
     'ssm_c_im': 3.526,
     'ssm_b_glu': 8.0,
     'ffn_conv_b': 6.322,
     'ctx_2': 3.96,
     'c_ctx_2': 5.771,
     'ada_b_2': 2.747,
     'norm_mix_2': 3.159,
     'norm_ffn_2': 3.941,
     'onorm_a_2': 8.0}
    for name, (base, spread) in spreads.items():
        noise = np.random.default_rng([zlib.crc32(name.encode()), seed]).standard_normal(out[name].shape)
        drawn = base * np.exp(spread * noise) if base else spread * noise
        out[name] = jnp.asarray(drawn.astype(out[name].dtype))
    for name, factor in factors.items():
        out[name] = (out[name] * factor).astype(out[name].dtype)
    return out
```

```python
from contextlib import ExitStack

import concourse.bass as bass
from concourse import mybir
from concourse.alu_op_type import AluOpType as ALU

F32 = mybir.dt.float32
U32 = mybir.dt.uint32
I32 = mybir.dt.int32
ACT = mybir.ActivationFunctionType
AX = mybir.AxisListType

P = 128
T = 256
TT = T // P
D = 1024
KC = D // P
RING = 4
SLOT = 4096
EPS = 1e-6
PI = 3.141592653589793
ROUND = 12582912.0
BIG = 1.0e30

SB_HEADS, SB_DIM = 8, 64
SB_W = SB_HEADS * SB_DIM
SSM_W, SSM_G, SSM_C, SSM_S = 512, 32, 16, 64
ST = SSM_G * SSM_S // P
XA_HEADS = 4
D_FF = 2816
FC = D_FF // P
NH = 8
N_EXP, N_GRP, E_GRP = 32, 4, 8
D_EXP = 512
GRID_W = 64


class Counter:

    def __init__(self, sem, step=1):
        self.sem, self.step, self.count, self.base = sem, step, 0, 0

    def tick(self):
        self.count += self.step
        return self.step

    def at(self, k):
        return self.base + self.step * k


class Kit:

    def __init__(self, nc, ctx, io):
        self.nc, self.ctx, self.io = nc, ctx, io
        self.counters, self.names = {}, {}
        self.tiles, self.issued, self.used = [], 0, 0
        self.landed = [ctx.enter_context(nc.semaphore(f"slot{i}_landed")) for i in range(RING)]
        self.landed_count, self.queued = [0] * RING, [0] * RING
        self.need = []
        self.products = self.counter("products")
        self.done_at = {}
        self.own = {n: Counter(ctx.enter_context(nc.semaphore(f"{n}_own_step"))) for n in ("dve", "act", "pool")}
        self.ring = [self.sb(f"ring{i}", [P, SLOT]) for i in range(RING)]

    def unique(self, name):
        n = self.names[name] = self.names.get(name, 0) + 1
        return name if n == 1 else f"{name}_{n}"

    def sb(self, name, shape, dt=F32, ctx=None):
        return (ctx or self.ctx).enter_context(self.nc.sbuf_tensor(self.unique(name), shape, dt))

    def ps(self, name, shape, ctx, dt=F32):
        return ctx.enter_context(self.nc.psum_tensor(self.unique(name), shape, dt))

    def counter(self, name, step=1):
        if name not in self.counters:
            self.counters[name] = Counter(self.ctx.enter_context(self.nc.semaphore(name)), step)
        return self.counters[name]

    def stage(self):
        for s in self.counters.values():
            s.base = s.count
        return ExitStack()

    def queue(self, *parts):
        slot = len(self.tiles) % RING
        self.queued[slot] += 16 * len(parts)
        self.tiles.append(parts)
        self.need.append(self.queued[slot])

    def issue(self, sp, upto):
        for g in range(self.issued, min(upto, len(self.tiles))):
            if g >= RING:
                sp.wait_ge(self.products.sem, self.done_at[g - RING])
            for off, shape, src in self.tiles[g]:
                n = shape[0] * shape[1]
                dst = self.ring[g % RING][:, off:off + n].rearrange("p (a n) -> p a n", a=shape[0])
                sp.dma_start(dst, src).then_inc(self.landed[g % RING], 16)
                self.landed_count[g % RING] += 16
        self.issued = max(self.issued, min(upto, len(self.tiles)))

    def tile(self, eng, g, a):
        eng.wait_ge(self.landed[g % RING], self.need[g])
        words = sum(s[0] * s[1] for _, s, _ in self.tiles[g])
        return self.ring[g % RING][:, 0:words].rearrange("p (a n) -> p a n", a=a)

    def col(self, name, i=0):
        return self.params[:, self.cols[name] + i:self.cols[name] + i + 1]


def rows_of(w, c0, n):
    return w.rearrange("(k p) n -> p k n", p=P)[:, :, c0:c0 + n]


def queue_columns(K, w, n_total, n=512):
    for c in range(0, n_total, n):
        K.queue((0, (w.shape[0] // P, n), rows_of(w, c, n)))


def vector_rows(K):
    io = K.io
    vec = lambda a: a.rearrange("(c p) -> c p", p=P)
    out = []
    for n in ("norm_mix_pre", "norm_mix_post", "norm_xa_pre", "norm_xa_post", "norm_mem",
              "norm_ffn_pre", "norm_ffn_post", "b_gate", "ssm_b_glu", "ssm_d", "ffn_conv_b"):
        out.append((n, vec(io[n][0])))
    for j in range(3):
        out.append((f"ffn_conv_w{j}", vec(io["ffn_conv_w"][0, j])))
    out.append(("ssm_a_re", io["ssm_a_re"][0].rearrange("(i h) s -> i (h s)", h=2)))
    out.append(("ssm_a_im", io["ssm_a_im"][0].rearrange("(i h) s -> i (h s)", h=2)))
    out.append(("c", vec(io["c_2"][0])))
    out.append(("c_ctx", vec(io["c_ctx_2"])))
    for l in range(2):
        out.append((f"ada_b{l}", vec(io["ada_b_2"][l])))
        out.append((f"norm_mix{l}", vec(io["norm_mix_2"][l])))
        out.append((f"norm_ffn{l}", vec(io["norm_ffn_2"][l])))
    for j in range(3):
        out.append((f"conv_a{j}", vec(io["conv_a_2"][0, j])))
        out.append((f"conv_b{j}", vec(io["conv_b_2"][0, j])))
    out.append(("onorm", vec(io["onorm_a_2"][0])))
    out.append(("final", vec(io["final_norm_2"])))
    return out


def stage_setup(K):
    nc, io = K.nc, K.io
    rows = vector_rows(K)
    n_rows = sum(a.shape[0] for _, a in rows)
    n_tiles = -(-n_rows // P)
    K.cols, pieces, at = {}, [], 0
    for name, a in rows:
        K.cols[name] = at
        done = 0
        while done < a.shape[0]:
            n = min(a.shape[0] - done, P - at % P)
            pieces.append((at // P, at % P, n, a[done:done + n]))
            done, at = done + n, at + n
    K.params = K.sb("params", [P, n_tiles * P])
    K.ident = K.sb("ident", [P, P])
    K.ones = K.sb("ones", [P, P])
    K.incl = K.sb("incl", [P, 2, P])
    K.after = K.sb("after", [P, P])
    K.xT = K.sb("xT", [P, KC, T])
    K.hT = K.sb("hT", [P, KC, T])
    K.rstd = K.sb("rstd", [P, T])
    K.epsb = K.sb("epsb", [P, 1])

    loads, made = K.counter("setup_loads", 16), K.counter("setup_made")
    turned, moved = K.counter("setup_turned"), K.counter("setup_moved")
    with K.stage() as st:
        table = K.sb("param_rows", [P, n_tiles, P], ctx=st)
        x_rows = K.sb("x_rows", [P, TT, D], ctx=st)
        ps = K.ps("setup_ps", [P, 2, 512], st)
        block = st.enter_context(nc.Block())
        n_loads = [0]

        @block.sync
        def _(sp):
            K.issue(sp, 2)

        @block.scalar
        def _(act):
            act.dma_start(x_rows[:, :, :], io["x"][0].rearrange("(a p) d -> p a d", p=P)).then_inc(loads.sem, loads.tick())
            act.wait_ge(made.sem, made.at(1))
            for t, r, n, a in pieces:
                act.dma_start(table[r:r + n, t, :], a).then_inc(loads.sem, loads.tick())
            n_loads[0] = 1 + len(pieces)
            K.issue(act, RING)

        @block.gpsimd
        def _(pool):
            pool.memset(table[:, n_tiles - 1, :], 0.0).then_inc(made.sem, made.tick())
            pool.memset(K.ident[:, :], 0.0).then_inc(made.sem, made.tick())
            pool.memset(K.ones[:, :], 1.0).then_inc(made.sem, made.tick())
            pool.memset(K.epsb[:, :], EPS).then_inc(made.sem, made.tick())
            pool.wait_ge(made.sem, made.at(4))
            pool.affine_select(out=K.ident[:, :], in_=K.ident[:, :], compare_op=ALU.not_equal, fill=1.0,
                                       base=0, pattern=[[-1, P]], channel_multiplier=1).then_inc(made.sem, made.tick())
            pool.affine_select(out=K.incl[:, 0, :], in_=K.ones[:, :], compare_op=ALU.is_ge, fill=0.0,
                                       base=0, pattern=[[1, P]], channel_multiplier=-1).then_inc(made.sem, made.tick())
            pool.affine_select(out=K.incl[:, 1, :], in_=K.ones[:, :], compare_op=ALU.is_ge, fill=0.0,
                                       base=0, pattern=[[-1, P]], channel_multiplier=1).then_inc(made.sem, made.tick())
            pool.affine_select(out=K.after[:, :], in_=K.ones[:, :], compare_op=ALU.is_gt, fill=0.0,
                                       base=0, pattern=[[-1, P]], channel_multiplier=1).then_inc(made.sem, made.tick())

        quads = TT * KC // 4

        @block.tensor
        def _(pe):
            pe.wait_ge(made.sem, made.at(5))
            pe.wait_ge(loads.sem, loads.at(n_loads[0]))
            for q in range(quads + -(-n_tiles // 4)):
                if q >= 2:
                    pe.wait_ge(moved.sem, moved.at(q - 1))
                n = 4 if q < quads else min(4, n_tiles - 4 * (q - quads))
                for j in range(n):
                    if q < quads:
                        a, c = divmod(4 * q + j, KC)
                        src = x_rows[:, a, c * P:(c + 1) * P]
                    else:
                        src = table[:, 4 * (q - quads) + j, :]
                    mm = pe.transpose(ps[:, q % 2, j * P:(j + 1) * P], src, K.ident[:, :])
                mm.then_inc(turned.sem, turned.tick())

        @block.vector
        def _(dve):
            for q in range(quads + -(-n_tiles // 4)):
                dve.wait_ge(turned.sem, turned.at(q + 1))
                n = 4 if q < quads else min(4, n_tiles - 4 * (q - quads))
                if q < quads:
                    a, c = divmod(4 * q, KC)
                    dst = K.xT[:, c:c + 4, a * P:(a + 1) * P]
                else:
                    dst = K.params[:, 4 * (q - quads) * P:(4 * (q - quads) + n) * P].rearrange("p (a n) -> p a n", n=P)
                dve.tensor_copy(dst, ps[:, q % 2, 0:n * P].rearrange("p (a n) -> p a n", n=P)).then_inc(moved.sem, moved.tick())


def turn_rows(K, dram, dst, name):
    nc = K.nc
    loads, turned, moved = K.counter("rows_landed", 16), K.counter("rows_turned"), K.counter("rows_moved")
    with K.stage() as st:
        rows = K.sb(f"rows_{name}", [P, TT, D], ctx=st)
        ps = K.ps("rows_ps", [P, 2, 512], st)
        block = st.enter_context(nc.Block())

        @block.scalar
        def _(act):
            act.dma_start(rows[:, :, :], dram.rearrange("(a p) d -> p a d", p=P)).then_inc(loads.sem, loads.tick())

        @block.tensor
        def _(pe):
            pe.wait_ge(loads.sem, loads.at(1))
            for q in range(TT * KC // 4):
                if q >= 2:
                    pe.wait_ge(moved.sem, moved.at(q - 1))
                for j in range(4):
                    a, c = divmod(4 * q + j, KC)
                    mm = pe.transpose(ps[:, q % 2, j * P:(j + 1) * P], rows[:, a, c * P:(c + 1) * P], K.ident[:, :])
                mm.then_inc(turned.sem, turned.tick())

        @block.vector
        def _(dve):
            for q in range(TT * KC // 4):
                dve.wait_ge(turned.sem, turned.at(q + 1))
                a, c = divmod(4 * q, KC)
                dve.tensor_copy(dst[:, c:c + 4, a * P:(a + 1) * P],
                                         ps[:, q % 2, :].rearrange("p (a n) -> p a n", n=P)).then_inc(moved.sem, moved.tick())


def stage_norm(K, src, dst, gain, shift=None, residual=None, post=None):
    nc = K.nc
    squared, summed, rooted, normed = (K.counter(n) for n in ("norm_squared", "norm_summed", "norm_rooted", "norm_scaled"))
    own = K.own["dve"]
    halves = 2
    with K.stage() as st:
        sq = dst if residual is None and src is not dst else K.sb("norm_sq", [P, KC, T], ctx=st)
        tmp = dst if residual is None else sq
        ss = K.ps("norm_ss", [P, 512], st)
        block = st.enter_context(nc.Block())
        n = KC // halves

        @block.scalar
        def _(act):
            for i in range(halves):
                act.activation(sq[:, i * n:(i + 1) * n, :], src[:, i * n:(i + 1) * n, :], ACT.Square,
                                          scale=D ** -0.5).then_inc(squared.sem, squared.tick())
            act.wait_ge(summed.sem, summed.at(1))
            act.activation(K.rstd[:, :], ss[:, 0:T], ACT.Sqrt, bias=K.epsb[:, :]).then_inc(rooted.sem, rooted.tick())

        @block.tensor
        def _(pe):
            for c in range(KC):
                if c % n == 0:
                    pe.wait_ge(squared.sem, squared.at(c // n + 1))
                mm = pe.matmul(ss[:, 0:T], K.ones[:, :], sq[:, c, :], start=c == 0, stop=c == KC - 1)
            mm.then_inc(summed.sem, summed.tick())

        @block.vector
        def _(dve):
            dve.wait_ge(rooted.sem, rooted.at(1))
            dve.reciprocal(K.rstd[:, :], K.rstd[:, :]).then_inc(own.sem, own.tick())
            dve.wait_ge(own.sem, own.count)
            for c in range(KC):
                dve.scalar_tensor_tensor(out=tmp[:, c, :], in0=src[:, c, :], scalar=gain(c), in1=K.rstd[:, :],
                                                   op0=ALU.mult, op1=ALU.mult).then_inc(normed.sem, normed.tick())

        if shift is not None or residual is not None:
            @block.gpsimd
            def _(pool):
                for c in range(KC):
                    pool.wait_ge(normed.sem, normed.at(c + 1))
                    if shift is not None:
                        pool.tensor_scalar(dst[:, c, :], tmp[:, c, :], shift(c), None, ALU.add)
                    else:
                        pool.tensor_tensor(dst[:, c, :], tmp[:, c, :], residual[:, c, :], ALU.add)


def linear_stage(K, src, n_chunks, evac, kc=KC, per_tile=4, n=T, extra=None, token_major=()):
    nc = K.nc
    full, free = K.products, K.counter("linear_free")
    g0 = K.used
    tiles = -(-n_chunks // per_tile)
    banks = 4
    with K.stage() as st:
        ps = K.ps("linear_ps", [P, banks, 512], st)
        block = st.enter_context(nc.Block())

        @block.tensor
        def _(pe):
            q = 0
            for t in range(tiles):
                w = K.tile(pe, g0 + t, kc)
                tok = t in token_major
                for j in range(TT if tok else min(per_tile, n_chunks - t * per_tile)):
                    if q >= banks:
                        pe.wait_ge(free.sem, free.at(q - banks + 1))
                    for k in range(kc):
                        if tok:
                            mm = pe.matmul(ps[:, q % banks, 0:512], src[:, k, j * P:(j + 1) * P], w[:, k, 0:512],
                                           start=k == 0, stop=k == kc - 1)
                        else:
                            mm = pe.matmul(ps[:, q % banks, 0:n], w[:, k, j * P:(j + 1) * P], src[:, k, 0:n],
                                           start=k == 0, stop=k == kc - 1)
                    mm.then_inc(full.sem, full.tick())
                    q += 1
                K.done_at[g0 + t] = full.count

        @block.scalar
        def _(act):
            q = 0
            for t in range(tiles):
                for j in range(TT if t in token_major else min(per_tile, n_chunks - t * per_tile)):
                    act.wait_ge(full.sem, full.at(q + 1))
                    evac(act, t, j, ps[:, q % banks, 0:512 if t in token_major else n]).then_inc(free.sem, free.tick())
                    q += 1
        @block.sync
        def _(sp):
            K.issue(sp, g0 + tiles + RING)

        if extra:
            extra(block)
    K.used = g0 + tiles


def stage_stick_breaking(K, qT, kT, v, oT):
    nc = K.nc
    W = T + P
    pairs = SB_HEADS // 2
    names = ("sb_scores", "sb_scaled", "sb_size", "sb_soft", "sb_masked", "sb_sums", "sb_arg", "sb_weights", "sb_causal", "sb_mixed", "sb_out")
    scores, scaled, size, soft, masked, sums, arg, weights, causal, mixed, stored = (K.counter(x) for x in names)
    with K.stage() as st:
        zs = K.sb("sb_zs", [P, 2, 2, W], ctx=st)
        ab = K.sb("sb_ab", [P, 2, 2, W], ctx=st)
        sp_ = K.sb("sb_sp", [P, 2, 2, W], ctx=st)
        t1 = K.sb("sb_t1", [P, 2, 2, W], ctx=st)
        w = K.sb("sb_w", [P, 2, 2, W], ctx=st)
        z_ps = K.ps("sb_z", [P, 2, 512], st)
        r_ps = K.ps("sb_r", [P, 2, 512], st)
        o_ps = K.ps("sb_o", [P, 2, 512], st)
        block = st.enter_context(nc.Block())

        def causal_parts(t, b):
            return t[:, b, :, 0:P], t[:, b, :, T:W]

        @block.tensor
        def _(pe):
            def make_scores(i):
                if i >= 1:
                    pe.wait_ge(scaled.sem, scaled.at(i))
                for h in range(2):
                    r = slice(SB_DIM * h, SB_DIM * h + SB_DIM)
                    pe.matmul(z_ps[:, h, 0:T], kT[r, i, 0:P], qT[r, i, 0:T], start=True, stop=True)
                    mm = pe.matmul(z_ps[:, h, T:W], kT[r, i, P:T], qT[r, i, P:T], start=True, stop=True)
                mm.then_inc(scores.sem, scores.tick())

            make_scores(0)
            for i in range(pairs):
                pe.wait_ge(masked.sem, masked.at(2 * (i + 1)))
                if i >= 1:
                    pe.wait_ge(arg.sem, arg.at(i))
                for h in range(2):
                    pe.matmul(r_ps[:, h, 0:W], K.after[:, :], sp_[:, i % 2, h, 0:W], start=True, stop=False)
                    mm = pe.matmul(r_ps[:, h, P:T], K.ones[:, :], sp_[:, i % 2, h, T:W], start=False, stop=True)
                mm.then_inc(sums.sem, sums.tick())
                if i + 1 < pairs:
                    make_scores(i + 1)
                pe.wait_ge(causal.sem, causal.at(2 * (i + 1)))
                if i >= 2:
                    pe.wait_ge(stored.sem, stored.at(i - 1))
                for h in range(2):
                    cols = slice(i * P + SB_DIM * h, i * P + SB_DIM * (h + 1))
                    o = o_ps[SB_DIM * h:SB_DIM * (h + 1), i % 2, :]
                    pe.matmul(o[:, 0:T], v[:, 0, cols], w[:, i % 2, h, 0:T], start=True, stop=False)
                    mm = pe.matmul(o[:, P:T], v[:, 1, cols], w[:, i % 2, h, T:W], start=False, stop=True)
                mm.then_inc(mixed.sem, mixed.tick())

        @block.scalar
        def _(act):
            own = K.own["act"]
            for i in range(pairs):
                b = i % 2
                act.wait_ge(scores.sem, scores.at(i + 1))
                if i >= 2:
                    act.wait_ge(arg.sem, arg.at(i - 1))
                act.activation(zs[:, b], z_ps[:, :, 0:W], ACT.Copy, scale=SB_DIM ** -0.5).then_inc(scaled.sem, scaled.tick())
                act.wait_ge(scaled.sem, scaled.at(i + 1))
                act.activation(ab[:, b], zs[:, b], ACT.Abs).then_inc(own.sem, own.tick())
                act.wait_ge(own.sem, own.count)
                act.activation(ab[:, b], ab[:, b], ACT.Exp, scale=-1.0).then_inc(own.sem, own.tick())
                act.wait_ge(own.sem, own.count)
                act.activation(ab[:, b], ab[:, b], ACT.Ln, bias=1.0).then_inc(size.sem, size.tick())
                act.wait_ge(arg.sem, arg.at(i + 1))
                if i >= 2:
                    act.wait_ge(mixed.sem, mixed.at(i - 1))
                act.activation(w[:, b], t1[:, b], ACT.Exp).then_inc(weights.sem, weights.tick())

        @block.gpsimd
        def _(pool):
            for i in range(pairs):
                pool.wait_ge(soft.sem, soft.at(i + 1))
                for part in causal_parts(sp_, i % 2):
                    pool.affine_select(out=part, in_=part, compare_op=ALU.is_gt, fill=0.0, base=0,
                                                 pattern=[[0, 2], [1, P]], channel_multiplier=-1).then_inc(masked.sem, masked.tick())
                pool.wait_ge(weights.sem, weights.at(i + 1))
                for part in causal_parts(w, i % 2):
                    pool.affine_select(out=part, in_=part, compare_op=ALU.is_gt, fill=0.0, base=0,
                                                 pattern=[[0, 2], [1, P]], channel_multiplier=-1).then_inc(causal.sem, causal.tick())

        @block.vector
        def _(dve):
            own = K.own["dve"]
            for i in range(pairs):
                b = i % 2
                dve.wait_ge(size.sem, size.at(i + 1))
                if i >= 2:
                    dve.wait_ge(sums.sem, sums.at(i - 1))
                dve.scalar_tensor_tensor(out=sp_[:, b], in0=zs[:, b], scalar=0.0, in1=ab[:, b],
                                                 op0=ALU.max, op1=ALU.add).then_inc(soft.sem, soft.tick())
                dve.wait_ge(masked.sem, masked.at(2 * (i + 1)))
                dve.tensor_tensor(t1[:, b], zs[:, b], sp_[:, b], ALU.subtract).then_inc(own.sem, own.tick())
                dve.wait_ge(own.sem, own.count)
                dve.wait_ge(sums.sem, sums.at(i + 1))
                dve.tensor_tensor(t1[:, b], t1[:, b], r_ps[:, :, 0:W], ALU.subtract).then_inc(arg.sem, arg.tick())
                dve.wait_ge(mixed.sem, mixed.at(i + 1))
                dve.tensor_copy(oT[:, i, :], o_ps[:, i % 2, 0:T]).then_inc(stored.sem, stored.tick())


def exact_exp(K, dve, out, x, k, r, two_k):
    own = K.own["dve"]
    dve.tensor_scalar(k, x, 1.4426950408889634, ROUND, ALU.mult, ALU.add).then_inc(own.sem, own.tick())
    dve.wait_ge(own.sem, own.count)
    dve.tensor_scalar(k, k, -ROUND, -126.0, ALU.add, ALU.max).then_inc(own.sem, own.tick())
    dve.wait_ge(own.sem, own.count)
    dve.tensor_scalar(k, k, 127.0, None, ALU.min).then_inc(own.sem, own.tick())
    dve.wait_ge(own.sem, own.count)
    dve.scalar_tensor_tensor(out=r, in0=k, scalar=-0.693359375, in1=x, op0=ALU.mult, op1=ALU.add).then_inc(own.sem, own.tick())
    dve.wait_ge(own.sem, own.count)
    dve.scalar_tensor_tensor(out=r, in0=k, scalar=2.12194440e-4, in1=r, op0=ALU.mult, op1=ALU.add).then_inc(own.sem, own.tick())
    dve.wait_ge(own.sem, own.count)
    dve.tensor_scalar(out, r, 1.0 / 5040, 1.0 / 720, ALU.mult, ALU.add).then_inc(own.sem, own.tick())
    dve.wait_ge(own.sem, own.count)
    for c in (1.0 / 120, 1.0 / 24, 1.0 / 6, 0.5, 1.0, 1.0):
        dve.tensor_tensor(out, out, r, ALU.mult).then_inc(own.sem, own.tick())
        dve.wait_ge(own.sem, own.count)
        dve.tensor_scalar(out, out, c, None, ALU.add).then_inc(own.sem, own.tick())
        dve.wait_ge(own.sem, own.count)
    dve.tensor_scalar(two_k, k, 127.0, 8388608.0, ALU.add, ALU.mult).then_inc(own.sem, own.tick())
    dve.wait_ge(own.sem, own.count)
    dve.tensor_tensor(out, out, two_k.bitcast(F32), ALU.mult).then_inc(own.sem, own.tick())
    dve.wait_ge(own.sem, own.count)


def stage_ssm_params(K, S, rot, scratch):
    nc, io = K.nc, K.io
    loads = K.counter("ssm_loads", 16)
    made, turned, moved, angle, waved = (K.counter(x) for x in ("ssm_made", "ssm_turned", "ssm_moved", "ssm_angle", "ssm_waved"))
    pool_made = K.counter("ssm_pool_made")
    with K.stage() as st:
        ld = K.sb("ssm_ld", [ST, 2], ctx=st)
        ldr = K.sb("ssm_ldr", [ST, P], ctx=st)
        at = [0]

        def part(*shape):
            n, names = 1, "abcd"[:len(shape)]
            for x in shape:
                n *= x
            at[0] += n
            form = f"p ({' '.join(names)}) -> p {' '.join(names)}"
            return scratch[:, at[0] - n:at[0]].rearrange(form, **dict(zip(names, shape)))

        br, bb, bx = part(2, ST, SSM_C), part(2, ST, SSM_C), part(2, ST, 2, SSM_C)
        cr, cx = part(2, 4, SSM_S), part(2, 4, 2, SSM_S)
        half = K.sb("ssm_half", [P, 4], ctx=st)
        s = K.sb("ssm_small", [P, 20, ST], ctx=st)
        ints = K.sb("ssm_ints", [P, ST], I32, ctx=st)
        tm = K.sb("ssm_time", [P, T], ctx=st)
        ps = K.ps("ssm_ps", [P, 3, 512], st)
        block = st.enter_context(nc.Block())
        are, aim = (K.params[:, K.cols[n]:K.cols[n] + ST] for n in ("ssm_a_re", "ssm_a_im"))
        DT, RE, IM, ER, CO, SI, LR, LI, DEN, KR, KI, PH, T0, T1, T2, PC = range(16)
        v = lambda i: s[:, i, :]

        @block.sync
        def _(sp):
            sp.dma_start(ld[:, :], io["ssm_log_dt"][0].rearrange("(i h) -> i h", h=2)).then_inc(loads.sem, loads.tick())
            for j, n in enumerate(("ssm_b_re", "ssm_b_im")):
                sp.dma_start(br[:, j], io[n][0].rearrange("g s c -> (g s) c").rearrange("(i q) c -> q i c", q=P)).then_inc(loads.sem, loads.tick())
            for j, n in enumerate(("ssm_c_re", "ssm_c_im")):
                sp.dma_start(cr[:, j], io[n][0].rearrange("g c s -> (g c) s").rearrange("(b r) s -> r b s", r=P)).then_inc(loads.sem, loads.tick())

        @block.gpsimd
        def _(pool):
            own = K.own["pool"]
            pool.iota(tm[:, :], pattern=[[1, T]], base=0, channel_multiplier=0,
                                   allow_small_or_imprecise_dtypes=True).then_inc(pool_made.sem, pool_made.tick())
            pool.memset(bx, 0.0).then_inc(pool_made.sem, pool_made.tick())
            pool.iota(half[:, 2:3], pattern=[[0, 1]], base=0, channel_multiplier=1,
                                allow_small_or_imprecise_dtypes=True).then_inc(own.sem, own.tick())
            pool.wait_ge(own.sem, own.count)
            pool.tensor_scalar(half[:, 3:4], half[:, 2:3], 1.0 / 16, -15.0 / 32, ALU.mult, ALU.add).then_inc(own.sem, own.tick())
            pool.wait_ge(own.sem, own.count)
            pool.tensor_scalar(half[:, 3:4], half[:, 3:4], ROUND, -ROUND, ALU.add, ALU.add).then_inc(own.sem, own.tick())
            pool.wait_ge(own.sem, own.count)
            pool.tensor_scalar(half[:, 2:3], half[:, 3:4], 0.5, -0.25, ALU.mult, ALU.add).then_inc(own.sem, own.tick())
            pool.wait_ge(own.sem, own.count)
            pool.tensor_scalar(half[:, 2:3], half[:, 2:3], ROUND, -ROUND, ALU.add, ALU.add).then_inc(own.sem, own.tick())
            pool.wait_ge(own.sem, own.count)
            pool.tensor_scalar(half[:, 2:3], half[:, 2:3], -2.0, None, ALU.mult).then_inc(own.sem, own.tick())
            pool.wait_ge(own.sem, own.count)
            pool.tensor_tensor(half[:, 1:2], half[:, 3:4], half[:, 2:3], ALU.add).then_inc(own.sem, own.tick())
            pool.wait_ge(own.sem, own.count)
            pool.tensor_scalar(half[:, 0:1], half[:, 1:2], -1.0, 1.0, ALU.mult, ALU.add).then_inc(own.sem, own.tick())
            pool.wait_ge(own.sem, own.count)
            pool.tensor_scalar(half[:, 2:4], half[:, 0:2], -1.0, None, ALU.mult).then_inc(own.sem, own.tick())
            pool.wait_ge(own.sem, own.count)
            pool.wait_ge(loads.sem, loads.at(5))
            for j in range(2):
                for h in range(2):
                    pool.tensor_scalar(cx[:, j, :, h, :], cr[:, j], half[:, 2 * j + h:2 * j + h + 1], None, ALU.mult).then_inc(pool_made.sem, pool_made.tick())

        @block.tensor
        def _(pe):
            pe.wait_ge(made.sem, made.at(1))
            pe.transpose(ps[:, 0, 0:ST], ldr[:, :], K.ident[0:ST, 0:ST]).then_inc(turned.sem, turned.tick())
            pe.wait_ge(pool_made.sem, pool_made.at(6))
            for j in range(2):
                for b in range(4):
                    mm = pe.transpose(ps[:, 1 + j, b * P:(b + 1) * P], cx[:, j, b].rearrange("p h s -> p (h s)"), K.ident[:, :])
            mm.then_inc(turned.sem, turned.tick())
            pe.wait_ge(made.sem, made.at(3))
            pe.wait_ge(moved.sem, moved.at(3))
            for j in range(2):
                for b in range(4):
                    mm = pe.transpose(ps[:, 1 + j, b * P:(b + 1) * P],
                                      bx[:, j, 4 * b:4 * b + 4].rearrange("p i h c -> p (i h c)"), K.ident[:, :])
            mm.then_inc(turned.sem, turned.tick())

        @block.vector
        def _(dve):
            own = K.own["dve"]
            tt, ts = dve.tensor_tensor, dve.tensor_scalar
            dve.wait_ge(loads.sem, loads.at(5))
            dve.tensor_copy(ldr[:, :].rearrange("p (h s) -> p h s", h=2), ld[:, :].unsqueeze(2).broadcast_to([ST, 2, SSM_S])).then_inc(made.sem, made.tick())
            dve.wait_ge(turned.sem, turned.at(1))
            dve.tensor_copy(v(T0), ps[:, 0, 0:ST]).then_inc(moved.sem, moved.tick())
            dve.wait_ge(moved.sem, moved.at(1))
            exact_exp(K, dve, v(DT), v(T0), v(T1), v(T2), ints[:, :])
            dve.wait_ge(turned.sem, turned.at(2))
            for j in range(2):
                dve.tensor_copy(S["cT"][:, j], ps[:, 1 + j, :].rearrange("p (b c) -> p b c", b=4)).then_inc(moved.sem, moved.tick())
            tt(v(RE), are, v(DT), ALU.mult).then_inc(own.sem, own.tick())
            dve.wait_ge(own.sem, own.count)
            tt(v(IM), aim, v(DT), ALU.mult).then_inc(own.sem, own.tick())
            dve.wait_ge(own.sem, own.count)
            ts(v(PH), v(IM), 1.0 / (2 * PI), None, ALU.mult).then_inc(own.sem, own.tick())
            dve.wait_ge(own.sem, own.count)
            ts(v(T0), v(PH), ROUND, -ROUND, ALU.add, ALU.add).then_inc(own.sem, own.tick())
            dve.wait_ge(own.sem, own.count)
            tt(v(PH), v(PH), v(T0), ALU.subtract).then_inc(own.sem, own.tick())
            dve.wait_ge(own.sem, own.count)
            ts(v(PC), v(PH), 0.25, None, ALU.add).then_inc(own.sem, own.tick())
            dve.wait_ge(own.sem, own.count)
            ts(v(T0), v(PC), ROUND, -ROUND, ALU.add, ALU.add).then_inc(own.sem, own.tick())
            dve.wait_ge(own.sem, own.count)
            tt(v(PC), v(PC), v(T0), ALU.subtract).then_inc(made.sem, made.tick())
            exact_exp(K, dve, v(ER), v(RE), v(T1), v(T2), ints[:, :])
            dve.tensor_copy(S["r"][:, :], v(ER)).then_inc(own.sem, own.tick())
            dve.wait_ge(own.sem, own.count)
            dve.wait_ge(angle.sem, angle.at(2))
            tt(v(LR), v(ER), v(CO), ALU.mult).then_inc(own.sem, own.tick())
            dve.wait_ge(own.sem, own.count)
            tt(v(LI), v(ER), v(SI), ALU.mult).then_inc(own.sem, own.tick())
            dve.wait_ge(own.sem, own.count)
            ts(v(LR), v(LR), -1.0, None, ALU.add).then_inc(own.sem, own.tick())
            dve.wait_ge(own.sem, own.count)
            tt(v(DEN), are, are, ALU.mult).then_inc(own.sem, own.tick())
            dve.wait_ge(own.sem, own.count)
            tt(v(T0), aim, aim, ALU.mult).then_inc(own.sem, own.tick())
            dve.wait_ge(own.sem, own.count)
            tt(v(DEN), v(DEN), v(T0), ALU.add).then_inc(own.sem, own.tick())
            dve.wait_ge(own.sem, own.count)
            dve.reciprocal(v(DEN), v(DEN)).then_inc(own.sem, own.tick())
            dve.wait_ge(own.sem, own.count)
            tt(v(T0), v(LR), are, ALU.mult).then_inc(own.sem, own.tick())
            dve.wait_ge(own.sem, own.count)
            tt(v(T1), v(LI), aim, ALU.mult).then_inc(own.sem, own.tick())
            dve.wait_ge(own.sem, own.count)
            tt(v(KR), v(T0), v(T1), ALU.add).then_inc(own.sem, own.tick())
            dve.wait_ge(own.sem, own.count)
            tt(v(T0), v(LI), are, ALU.mult).then_inc(own.sem, own.tick())
            dve.wait_ge(own.sem, own.count)
            tt(v(T1), v(LR), aim, ALU.mult).then_inc(own.sem, own.tick())
            dve.wait_ge(own.sem, own.count)
            tt(v(KI), v(T0), v(T1), ALU.subtract).then_inc(own.sem, own.tick())
            dve.wait_ge(own.sem, own.count)
            tt(v(KR), v(KR), v(DEN), ALU.mult).then_inc(own.sem, own.tick())
            dve.wait_ge(own.sem, own.count)
            tt(v(KI), v(KI), v(DEN), ALU.mult).then_inc(own.sem, own.tick())
            dve.wait_ge(own.sem, own.count)
            wide = lambda i: v(i).unsqueeze(2).broadcast_to([P, ST, SSM_C])
            tt(bb[:, 0], br[:, 0], wide(KR), ALU.mult).then_inc(own.sem, own.tick())
            dve.wait_ge(own.sem, own.count)
            tt(bb[:, 1], br[:, 0], wide(KI), ALU.mult).then_inc(own.sem, own.tick())
            dve.wait_ge(own.sem, own.count)
            tt(br[:, 0], br[:, 1], wide(KI), ALU.mult).then_inc(own.sem, own.tick())
            dve.wait_ge(own.sem, own.count)
            tt(br[:, 1], br[:, 1], wide(KR), ALU.mult).then_inc(own.sem, own.tick())
            dve.wait_ge(own.sem, own.count)
            dve.wait_ge(pool_made.sem, pool_made.at(2))
            for h in range(2):
                r = slice(64 * h, 64 * h + 64)
                tt(bx[r, 0, :, h, :], bb[r, 0], br[r, 0], ALU.subtract).then_inc(own.sem, own.tick())
                dve.wait_ge(own.sem, own.count)
                ins = tt(bx[r, 1, :, h, :], bb[r, 1], br[r, 1], ALU.add)
                if h == 0:
                    ins.then_inc(own.sem, own.tick())
                    dve.wait_ge(own.sem, own.count)
            ins.then_inc(made.sem, made.tick())
            dve.wait_ge(turned.sem, turned.at(3))
            for j in range(2):
                dve.tensor_copy(S["bT"][:, j], ps[:, 1 + j, :].rearrange("p (b c) -> p b c", b=4)).then_inc(moved.sem, moved.tick())
            for which, dst in enumerate((S["sin"], S["cos"])):
                for i in range(ST):
                    ins = ts(dst[:, i, :], tm[:, :], s[:, PH, i:i + 1], None, ALU.mult)
                ins.then_inc(own.sem, own.tick())
                dve.wait_ge(own.sem, own.count)
                if which:
                    dve.wait_ge(waved.sem, waved.at(1))
                ts(rot[:, :, :], dst[:, :, :], ROUND, -ROUND, ALU.add, ALU.add).then_inc(own.sem, own.tick())
                dve.wait_ge(own.sem, own.count)
                if which == 0:
                    tt(rot[:, :, :], dst[:, :, :], rot[:, :, :], ALU.subtract).then_inc(made.sem, made.tick())
                else:
                    tt(dst[:, :, :], dst[:, :, :], rot[:, :, :], ALU.subtract).then_inc(own.sem, own.tick())
                    dve.wait_ge(own.sem, own.count)
                    ts(dst[:, :, :], dst[:, :, :], 0.25, None, ALU.add).then_inc(own.sem, own.tick())
                    dve.wait_ge(own.sem, own.count)
                    ts(rot[:, :, :], dst[:, :, :], ROUND, -ROUND, ALU.add, ALU.add).then_inc(own.sem, own.tick())
                    dve.wait_ge(own.sem, own.count)
                    tt(rot[:, :, :], dst[:, :, :], rot[:, :, :], ALU.subtract).then_inc(made.sem, made.tick())

        TURN = 6.283185
        @block.scalar
        def _(act):
            act.wait_ge(made.sem, made.at(2))
            act.activation(v(CO), v(PC), ACT.Sin, scale=TURN).then_inc(angle.sem, angle.tick())
            act.activation(v(SI), v(PH), ACT.Sin, scale=TURN).then_inc(angle.sem, angle.tick())
            act.wait_ge(made.sem, made.at(4))
            act.activation(S["sin"][:, :, :], rot[:, :, :], ACT.Sin, scale=TURN).then_inc(waved.sem, waved.tick())
            act.wait_ge(made.sem, made.at(5))
            act.activation(S["cos"][:, :, :], rot[:, :, :], ACT.Sin, scale=TURN).then_inc(waved.sem, waved.tick())


def stage_ssm_scan(K, S, uT, yT):
    nc = K.nc
    drive, spun, scanned, back, y_full, y_skip, y_out = (K.counter(x) for x in
        ("ssm_drive", "ssm_spun", "ssm_scanned", "ssm_back", "ssm_y_full", "ssm_y_skip", "ssm_y_out"))
    with K.stage() as st:
        pr = K.sb("ssm_pr", [P, 2, 2, T], ctx=st)
        z = K.sb("ssm_z", [P, 2, T], ctx=st)
        pz = K.sb("ssm_pz", [P, 2, 2, T], ctx=st)
        zz = K.hT[:, 0:4, :].rearrange("p (b j) t -> p b j t", b=2)
        sx = K.hT[:, 4:8, :].rearrange("p (b j) t -> p b j t", b=2)
        rr = K.rstd
        bu = K.ps("ssm_bu", [P, 2, 512], st)
        yp = K.ps("ssm_yp", [P, 2, 512], st)
        block = st.enter_context(nc.Block())

        @block.tensor
        def _(pe):
            def make_drive(i):
                if i >= 2:
                    pe.wait_ge(spun.sem, spun.at(i - 1))
                r = slice(32 * (i % 4), 32 * (i % 4) + 32)
                for j in range(2):
                    mm = pe.matmul(bu[:, i % 2, j * T:(j + 1) * T], S["bT"][r, j, i // 4, :], uT[r, i // 4, :],
                                   start=True, stop=True, tile_position=(32 * (i % 4), 0))
                mm.then_inc(drive.sem, drive.tick())

            make_drive(0)
            for i in range(ST):
                if i + 1 < ST:
                    make_drive(i + 1)
                pe.wait_ge(back.sem, back.at(i + 1))
                if i % 4 == 0 and i >= 8:
                    pe.wait_ge(y_skip.sem, y_skip.at(i // 4 - 1))
                r = slice(32 * (i % 4), 32 * (i % 4) + 32)
                o = yp[r, (i // 4) % 2, 0:T]
                for j in range(2):
                    mm = pe.matmul(o, S["cT"][:, j, i // 4, r], sx[:, i % 2, j, :], start=j == 0, stop=j == 1,
                                   tile_position=(0, 32 * (i % 4)))
                mm.then_inc(y_full.sem, y_full.tick())

        @block.vector
        def _(dve):
            own = K.own["dve"]
            tt = dve.tensor_tensor
            for i in range(ST):
                b = i % 2
                pair = lambda t: t[:, i, :].unsqueeze(1).broadcast_to([P, 2, T])
                dve.wait_ge(drive.sem, drive.at(i + 1))
                tt(pr[:, 0], bu[:, b, :].rearrange("p (j t) -> p j t", j=2), pair(S["cos"]), ALU.mult).then_inc(own.sem, own.tick())
                dve.wait_ge(own.sem, own.count)
                tt(pr[:, 1], bu[:, b, :].rearrange("p (j t) -> p j t", j=2), pair(S["sin"]), ALU.mult).then_inc(spun.sem, spun.tick())
                dve.wait_ge(spun.sem, spun.at(i + 1))
                if i >= 1:
                    dve.wait_ge(scanned.sem, scanned.at(i))
                dve.tensor_scalar(rr[:, :], S["cos"][:, i, :], 0.0, S["r"][:, i:i + 1], ALU.mult, ALU.add)
                tt(z[:, 0, :], pr[:, 0, 0, :], pr[:, 1, 1, :], ALU.add)
                tt(z[:, 1, :], pr[:, 0, 1, :], pr[:, 1, 0, :], ALU.subtract).then_inc(own.sem, own.tick())
                dve.wait_ge(own.sem, own.count)
                if i >= 2:
                    dve.wait_ge(back.sem, back.at(i - 1))
                for j in range(2):
                    ins = dve.tensor_tensor_scan(out=zz[:, b, j, :], data0=rr[:, :], data1=z[:, j, :],
                                                 initial=0.0, op0=ALU.mult, op1=ALU.add)
                    if j == 0:
                        ins.then_inc(own.sem, own.tick())
                        dve.wait_ge(own.sem, own.count)
                ins.then_inc(scanned.sem, scanned.tick())
                if i % 4 == 3:
                    c = i // 4
                    dve.wait_ge(y_full.sem, y_full.at(i + 1))
                    dve.scalar_tensor_tensor(out=yT[:, c, :], in0=uT[:, c, :], scalar=K.col("ssm_d", c),
                                                       in1=yp[:, c % 2, 0:T], op0=ALU.mult, op1=ALU.add).then_inc(y_skip.sem, y_skip.tick())

        @block.gpsimd
        def _(pool):
            own = K.own["pool"]
            tt = pool.tensor_tensor
            for i in range(ST):
                b = i % 2
                pair = lambda t: t[:, i, :].unsqueeze(1).broadcast_to([P, 2, T])
                if i >= 1:
                    pool.wait_ge(back.sem, back.at(i))
                pool.wait_ge(scanned.sem, scanned.at(i + 1))
                tt(pz[:, 0], zz[:, b], pair(S["cos"]), ALU.mult).then_inc(own.sem, own.tick())
                pool.wait_ge(own.sem, own.count)
                tt(pz[:, 1], zz[:, b], pair(S["sin"]), ALU.mult).then_inc(own.sem, own.tick())
                pool.wait_ge(own.sem, own.count)
                if i >= 2:
                    pool.wait_ge(y_full.sem, y_full.at(i - 1))
                tt(sx[:, b, 0, :], pz[:, 0, 0, :], pz[:, 1, 1, :], ALU.subtract).then_inc(own.sem, own.tick())
                pool.wait_ge(own.sem, own.count)
                tt(sx[:, b, 1, :], pz[:, 0, 1, :], pz[:, 1, 0, :], ALU.add).then_inc(back.sem, back.tick())

        @block.scalar
        def _(act):
            for c in range(4):
                act.wait_ge(y_skip.sem, y_skip.at(c + 1))
                act.activation(yT[:, c, :], yT[:, c, :], ACT.Gelu_apprx_tanh).then_inc(y_out.sem, y_out.tick())


def stage_glu(K, yT, oT):
    gated = K.counter("glu_gated")
    sig = K.sb("glu_sig", [P, 4, T], ctx=K.part)
    free = K.counter("linear_free")

    def evac(act, t, j, ps):
        return act.activation(sig[:, j, :], ps, ACT.Sigmoid, bias=K.col("ssm_b_glu", j))

    def extra(block):
        @block.vector
        def _(dve):
            for j in range(4):
                dve.wait_ge(free.sem, free.at(j + 1))
                dve.tensor_tensor(oT[:, j, :], yT[:, j, :], sig[:, j, :], ALU.mult).then_inc(gated.sem, gated.tick())

    linear_stage(K, yT, 4, evac, kc=4, extra=extra)


def stage_merge(K, o_attn, o_ssm, gates, dst):
    nc = K.nc
    full, took = K.products, K.counter("merge_took")
    g0 = K.used
    with K.stage() as st:
        tmp = K.sb("merge_tmp", [P, 2, 2, T], ctx=st)
        ps = K.ps("merge_ps", [P, 4, 512], st)
        block = st.enter_context(nc.Block())

        @block.tensor
        def _(pe):
            wa = K.tile(pe, g0, 4)
            ws = K.tile(pe, g0 + 1, 4)
            for c in range(KC):
                if c >= 4:
                    pe.wait_ge(took.sem, took.at(c - 3))
                for j, (w, o) in enumerate(((wa, o_attn), (ws, o_ssm))):
                    for k in range(4):
                        mm = pe.matmul(ps[:, c % 4, j * T:(j + 1) * T], w[:, k, c * P:(c + 1) * P], o[:, k, :],
                                       start=k == 0, stop=k == 3)
                mm.then_inc(full.sem, full.tick())
            K.done_at[g0] = K.done_at[g0 + 1] = full.count

        @block.vector
        def _(dve):
            own = K.own["dve"]
            for c in range(KC):
                dve.wait_ge(full.sem, full.at(c + 1))
                dve.tensor_tensor(tmp[:, c % 2, :, :], ps[:, c % 4, :].rearrange("p (j t) -> p j t", j=2),
                                          gates[:, c:c + KC + 1:KC, :], ALU.mult).then_inc(took.sem, took.tick())
                dve.wait_ge(took.sem, took.at(c + 1))
                dve.tensor_tensor(dst[:, c, :], tmp[:, c % 2, 0, :], tmp[:, c % 2, 1, :], ALU.add)

        @block.sync
        def _(sp):
            K.issue(sp, g0 + 2 + RING)
    K.used = g0 + 2


def stage_cross(K, qT, kT, v, oT):
    nc = K.nc
    dim = D // XA_HEADS
    hc = dim // P
    steps = XA_HEADS * TT
    scores, peak, probs, normed, turned, moved, mixed, stored = (K.counter(x) for x in (
        "xa_scores", "xa_peak", "xa_probs", "xa_normed", "xa_turned", "xa_moved", "xa_mixed", "xa_stored"))
    with K.stage() as st:
        p = K.sb("xa_p", [P, 2, T], ctx=st)
        pT = K.sb("xa_pT", [P, 2, TT, T], ctx=st)
        nm = K.sb("xa_nm", [P, steps], ctx=st)
        sm = K.sb("xa_sm", [P, steps], ctx=st)
        s_ps = K.ps("xa_s", [P, 2, 512], st)
        t_ps = K.ps("xa_t", [P, 2, 512], st)
        o_ps = K.ps("xa_o", [P, 2, 512], st)
        block = st.enter_context(nc.Block())

        @block.tensor
        def _(pe):
            def make_scores(i):
                h, a = divmod(i, TT)
                if i >= 2:
                    pe.wait_ge(probs.sem, probs.at(i - 1))
                for k in range(hc):
                    mm = pe.matmul(s_ps[:, i % 2, 0:T], qT[:, h * hc + k, a * P:(a + 1) * P], kT[:, h * hc + k, :],
                                   start=k == 0, stop=k == hc - 1)
                mm.then_inc(scores.sem, scores.tick())

            make_scores(0)
            for i in range(steps):
                h, a = divmod(i, TT)
                if i + 1 < steps:
                    make_scores(i + 1)
                pe.wait_ge(normed.sem, normed.at(i + 1))
                if i >= 2:
                    pe.wait_ge(moved.sem, moved.at(i - 1))
                for m in range(TT):
                    mm = pe.transpose(t_ps[:, i % 2, m * P:(m + 1) * P], p[:, i % 2, m * P:(m + 1) * P], K.ident[:, :])
                mm.then_inc(turned.sem, turned.tick())
                if a == TT - 1:
                    pe.wait_ge(moved.sem, moved.at(i + 1))
                    if h >= 2:
                        pe.wait_ge(stored.sem, stored.at(h - 1))
                    for c in range(hc):
                        for m in range(TT):
                            cc = (h * hc + c) * P
                            mm = pe.matmul(o_ps[:, h % 2, c * T:(c + 1) * T], v[:, m, cc:cc + P], pT[:, h % 2, m, :],
                                           start=m == 0, stop=m == TT - 1)
                    mm.then_inc(mixed.sem, mixed.tick())

        @block.vector
        def _(dve):
            own = K.own["dve"]
            for i in range(steps):
                h, a = divmod(i, TT)
                dve.wait_ge(scores.sem, scores.at(i + 1))
                dve.tensor_reduce(nm[:, i:i + 1], s_ps[:, i % 2, 0:T], AX.X, ALU.max).then_inc(own.sem, own.tick())
                dve.wait_ge(own.sem, own.count)
                dve.tensor_scalar(nm[:, i:i + 1], nm[:, i:i + 1], -dim ** -0.5, None, ALU.mult).then_inc(peak.sem, peak.tick())
                dve.wait_ge(probs.sem, probs.at(i + 1))
                dve.reciprocal(sm[:, i:i + 1], sm[:, i:i + 1]).then_inc(own.sem, own.tick())
                dve.wait_ge(own.sem, own.count)
                dve.tensor_scalar(p[:, i % 2, :], p[:, i % 2, :], sm[:, i:i + 1], None, ALU.mult).then_inc(normed.sem, normed.tick())
                if a == TT - 1:
                    dve.wait_ge(mixed.sem, mixed.at(h + 1))
                    dve.tensor_copy(oT[:, h * hc:(h + 1) * hc, :],
                                              o_ps[:, h % 2, :].rearrange("p (c t) -> p c t", c=hc)).then_inc(stored.sem, stored.tick())

        @block.scalar
        def _(act):
            for i in range(steps):
                h, a = divmod(i, TT)
                act.wait_ge(peak.sem, peak.at(i + 1))
                if i >= 2:
                    act.wait_ge(turned.sem, turned.at(i - 1))
                act.activation(p[:, i % 2, :], s_ps[:, i % 2, 0:T], ACT.Exp, bias=nm[:, i:i + 1],
                                        scale=dim ** -0.5, accum_out=sm[:, i:i + 1]).then_inc(probs.sem, probs.tick())
                act.wait_ge(turned.sem, turned.at(i + 1))
                if h >= 2 and a == 0:
                    act.wait_ge(mixed.sem, mixed.at(h - 1))
                act.activation(pT[:, h % 2, :, a * P:(a + 1) * P],
                                        t_ps[:, i % 2, 0:T].rearrange("p (m q) -> p m q", m=TT), ACT.Copy).then_inc(moved.sem, moved.tick())


def stage_ffn_up(K, src, hid):
    nc = K.nc
    full, base, conved, gelued, made = K.products, K.counter("ffn_base"), K.counter("ffn_conved"), K.counter("ffn_gelued"), K.counter("ffn_made")
    g0, per = K.used, 2
    with K.stage() as st:
        cv = K.sb("ffn_cv", [P, 2, 2, T], ctx=st)
        ps = K.ps("ffn_ps", [P, 4, 512], st)
        block = st.enter_context(nc.Block())

        @block.tensor
        def _(pe):
            for c in range(FC):
                g = g0 + c // per
                if c % per == 0:
                    w = K.tile(pe, g, 2 * KC)
                if c >= 4:
                    pe.wait_ge(conved.sem, conved.at(2 * (c - 3)))
                for j in range(2):
                    for k in range(KC):
                        mm = pe.matmul(ps[:, c % 4, j * T:(j + 1) * T], w[:, j * KC + k, (c % per) * P:(c % per + 1) * P],
                                       src[:, k, :], start=k == 0, stop=k == KC - 1)
                mm.then_inc(full.sem, full.tick())
                K.done_at[g] = full.count

        @block.scalar
        def _(act):
            for c in range(FC):
                act.wait_ge(full.sem, full.at(c + 1))
                if c >= 2:
                    act.wait_ge(made.sem, made.at(c - 1))
                for j in range(2):
                    act.activation(cv[:, c % 2, j, :], ps[:, c % 4, j * T:(j + 1) * T], ACT.Identity,
                                           scale=K.col("ffn_conv_w2", j * FC + c), bias=K.col("ffn_conv_b", j * FC + c)).then_inc(base.sem, base.tick())
                act.wait_ge(conved.sem, conved.at(2 * c + 2))
                act.activation(cv[:, c % 2, 0, :], cv[:, c % 2, 0, :], ACT.Gelu_apprx_tanh).then_inc(gelued.sem, gelued.tick())

        @block.vector
        def _(dve):
            own = K.own["dve"]
            for c in range(FC):
                dve.wait_ge(base.sem, base.at(2 * c + 2))
                for lag in (1, 2):
                    for j in range(2):
                        out = cv[:, c % 2, j, lag:T]
                        ins = dve.scalar_tensor_tensor(out=out, in0=ps[:, c % 4, j * T:(j + 1) * T - lag],
                                                       scalar=K.col(f"ffn_conv_w{2 - lag}", j * FC + c), in1=out,
                                                       op0=ALU.mult, op1=ALU.add)
                        if lag == 1:
                            ins.then_inc(own.sem, own.tick())
                            dve.wait_ge(own.sem, own.count)
                        else:
                            ins.then_inc(conved.sem, conved.tick())

        @block.gpsimd
        def _(pool):
            for c in range(FC):
                pool.wait_ge(gelued.sem, gelued.at(c + 1))
                pool.tensor_tensor(hid[:, c, :], cv[:, c % 2, 0, :], cv[:, c % 2, 1, :], ALU.mult).then_inc(made.sem, made.tick())

        @block.sync
        def _(sp):
            K.issue(sp, g0 + FC // per + RING)
    K.used = g0 + FC // per


def stage_ffn_down(K, hid, dst):
    nc = K.nc
    full, taken = K.products, K.counter("down_taken")
    g0, per = K.used, 4
    tiles = -(-FC // per)
    with K.stage() as st:
        ps = K.ps("down_ps", [P, KC, 512], st)
        block = st.enter_context(nc.Block())

        @block.tensor
        def _(pe):
            for f in range(FC):
                if f % per == 0:
                    w = K.tile(pe, g0 + f // per, min(per, FC - f))
                for c in range(KC):
                    mm = pe.matmul(ps[:, c, 0:T], w[:, f % per, c * P:(c + 1) * P], hid[:, f, :],
                                   start=f == 0, stop=f == FC - 1)
                mm.then_inc(full.sem, full.tick())
                K.done_at[g0 + f // per] = full.count

        @block.scalar
        def _(act):
            act.wait_ge(full.sem, full.at(FC))
            for c in range(KC):
                act.activation(dst[:, c, :], ps[:, c, 0:T], ACT.Copy).then_inc(taken.sem, taken.tick())

        @block.sync
        def _(sp):
            K.issue(sp, g0 + tiles + RING)
    K.used = g0 + tiles


def copy_to(dst):
    return lambda act, t, j, ps: act.activation(dst[:, 4 * t + j, :], ps, ACT.Copy)


def queue_first_block(K):
    io = K.io
    queue_columns(K, io["w_in"][0], 4096)
    queue_columns(K, io["ssm_w_glu"][0], 512)
    for n in ("w_branch_attn", "w_branch_ssm"):
        K.queue((0, (4, D), rows_of(io[n][0], 0, D)))
    queue_columns(K, io["w_out"][0], D)
    for n in ("xa_wk", "xa_wv", "xa_wq", "xa_wo"):
        queue_columns(K, io[n][0], D)
    for c in range(0, FC, 2):
        K.queue((0, (KC, 2 * P), rows_of(io["ffn_w_up"][0], c * P, 2 * P)),
                (2 * P * KC, (KC, 2 * P), rows_of(io["ffn_w_up"][0], D_FF + c * P, 2 * P)))
    for f in range(0, FC, 4):
        n = min(4, FC - f)
        K.queue((0, (n, D), io["ffn_w_down"][0][f * P:(f + n) * P].rearrange("(k p) n -> p k n", p=P)))


def first_block(K):
    gain = lambda name: (lambda c: K.col(name, c))
    with ExitStack() as K.part:
        proj = K.sb("proj", [P, 32, T], ctx=K.part)
        yT = K.sb("ssm_y", [P, 4, T], ctx=K.part)
        v = proj[:, 8:12, :].rearrange("p (a b) t -> p a (b t)", a=TT)
        with ExitStack() as ssm:
            S = {"sin": K.sb("ssm_sin", [P, ST, T], ctx=ssm), "cos": K.sb("ssm_cos", [P, ST, T], ctx=ssm),
                 "bT": K.sb("ssm_bT", [P, 2, 4, P], ctx=ssm), "cT": K.sb("ssm_cT", [P, 2, 4, P], ctx=ssm),
                 "r": K.sb("ssm_r", [P, ST], ctx=ssm)}
            stage_ssm_params(K, S, proj[:, 0:ST, :], proj[:, ST:, :].rearrange("p c t -> p (c t)"))
            stage_norm(K, K.xT, K.hT, gain("norm_mix_pre"))

            def evac(act, t, j, ps):
                if t == 2:
                    return act.activation(v[:, j, :], ps, ACT.Copy)
                c = 4 * t + j
                if c < 16:
                    return act.activation(proj[:, c, :], ps, ACT.Copy)
                return act.activation(proj[:, c, :], ps, ACT.Sigmoid, bias=K.col("b_gate", c - 16))

            linear_stage(K, K.hT, 32, evac, token_major=(2,))
            stage_ssm_scan(K, S, proj[:, 12:16, :], yT)
        o_ssm = K.sb("o_ssm", [P, 4, T], ctx=K.part)
        o_attn = K.sb("o_attn", [P, 4, T], ctx=K.part)
        stage_glu(K, yT, o_ssm)
        stage_stick_breaking(K, proj[:, 0:4, :], proj[:, 4:8, :], v, o_attn)
        stage_merge(K, o_attn, o_ssm, proj[:, 16:32, :], K.hT)
        linear_stage(K, K.hT, KC, copy_to(proj))
        stage_norm(K, proj[:, 0:KC, :], K.xT, gain("norm_mix_post"), residual=K.xT)
    with ExitStack() as K.part:
        memT = K.sb("memT", [P, KC, T], ctx=K.part)
        kT = K.sb("xa_kT", [P, KC, T], ctx=K.part)
        v = K.sb("xa_v", [P, TT, D], ctx=K.part)
        qT = K.sb("xa_qT", [P, KC, T], ctx=K.part)
        turn_rows(K, K.io["mem"][0], memT, "mem")
        stage_norm(K, memT, memT, gain("norm_mem"))
        linear_stage(K, memT, KC, copy_to(kT))
        linear_stage(K, memT, KC, lambda act, t, j, ps: act.activation(v[:, j, t * 512:(t + 1) * 512], ps, ACT.Copy),
                     token_major=(0, 1))
        stage_norm(K, K.xT, K.hT, gain("norm_xa_pre"))
        linear_stage(K, K.hT, KC, copy_to(qT))
        stage_cross(K, qT, kT, v, K.hT)
        linear_stage(K, K.hT, KC, copy_to(qT))
        stage_norm(K, qT, K.xT, gain("norm_xa_post"), residual=K.xT)
    with ExitStack() as K.part:
        hid = K.sb("ffn_hid", [P, FC, T], ctx=K.part)
        stage_norm(K, K.xT, K.hT, gain("norm_ffn_pre"))
        stage_ffn_up(K, K.hT, hid)
        stage_ffn_down(K, hid, K.hT)
        stage_norm(K, K.hT, K.xT, gain("norm_ffn_post"), residual=K.xT)


def stage_ada(K, l, mods, gains):
    nc = K.nc
    full, free, silued = K.products, K.counter("ada_free"), K.counter("ada_silued")
    turned, added, gained = K.counter("ada_turned"), K.counter("ada_added"), K.counter("ada_gained")
    g0, tiles = K.used, 12
    with K.stage() as st:
        row = K.sb("ada_row", [2, 6 * D], ctx=st)
        c = K.sb("ada_c", [P, KC, 2], ctx=st)
        ps = K.ps("ada_ps", [P, 2, 512], st)
        t_ps = K.ps("ada_t", [P, 512], st)
        block = st.enter_context(nc.Block())

        @block.tensor
        def _(pe):
            pe.wait_ge(silued.sem, silued.at(2))
            for t in range(tiles):
                w = K.tile(pe, g0 + t, KC)
                if t >= 2:
                    pe.wait_ge(free.sem, free.at(t - 1))
                for k in range(KC):
                    mm = pe.matmul(ps[0:2, t % 2, :], c[:, k, :], w[:, k, :], start=k == 0, stop=k == KC - 1)
                mm.then_inc(full.sem, full.tick())
                K.done_at[g0 + t] = full.count
            pe.wait_ge(free.sem, free.at(tiles))
            for i in range(6 * KC):
                mm = pe.matmul(t_ps[:, 2 * i:2 * i + 2], row[:, i * P:(i + 1) * P], K.ident[0:2, 0:2], start=True, stop=True)
            mm.then_inc(turned.sem, turned.tick())

        @block.scalar
        def _(act):
            for v, name in enumerate(("c", "c_ctx")):
                act.activation(c[:, :, v], K.params[:, K.cols[name]:K.cols[name] + KC], ACT.Silu).then_inc(silued.sem, silued.tick())
            for t in range(tiles):
                act.wait_ge(full.sem, full.at(t + 1))
                act.activation(row[:, t * 512:(t + 1) * 512], ps[0:2, t % 2, :], ACT.Copy).then_inc(free.sem, free.tick())

        @block.vector
        def _(dve):
            dve.wait_ge(turned.sem, turned.at(1))
            b0 = K.cols[f"ada_b{l}"]
            for v in range(2):
                dve.tensor_tensor(mods[:, v, :], t_ps[:, v:12 * KC:2], K.params[:, b0:b0 + 6 * KC], ALU.add).then_inc(added.sem, added.tick())
            dve.wait_ge(added.sem, added.at(2))
            for v in range(2):
                for i, (name, scale) in enumerate(((f"norm_mix{l}", 1), (f"norm_ffn{l}", 4))):
                    g = K.cols[name]
                    dve.scalar_tensor_tensor(out=gains[:, v, i, :], in0=mods[:, v, scale * KC:(scale + 1) * KC],
                                                       scalar=1.0, in1=K.params[:, g:g + KC], op0=ALU.add, op1=ALU.mult).then_inc(gained.sem, gained.tick())

        @block.sync
        def _(sp):
            K.issue(sp, g0 + tiles + RING)
    K.used = g0 + tiles


def stage_add_gated(K, y, gate):
    with K.stage() as st:
        block = st.enter_context(K.nc.Block())

        @block.vector
        def _(dve):
            for c in range(KC):
                dve.scalar_tensor_tensor(out=K.xT[:, c, :], in0=y[:, c, 0:T], scalar=gate(c), in1=K.xT[:, c, :],
                                         op0=ALU.mult, op1=ALU.add)


def stage_delta_project(K, src, kT, v, qT, z):
    nc = K.nc
    full, base, conved, out = K.products, K.counter("dp_base"), K.counter("dp_conved"), K.counter("dp_out")
    g0 = K.used
    jobs = [(kT, KC, 2), (v, 2 * KC, 2), (qT, 0, 1), (z, None, 1)]
    with K.stage() as st:
        cv = K.sb("dp_cv", [P, 2, 2, T], ctx=st)
        ps = K.ps("dp_ps", [P, 4, 512], st)
        block = st.enter_context(nc.Block())

        @block.tensor
        def _(pe):
            q = 0
            for n, (dst, taps, segs) in enumerate(jobs):
                for t in range(2):
                    w = K.tile(pe, g0 + 2 * n + t, KC)
                    for j in range(4):
                        if q >= 4:
                            pe.wait_ge(conved.sem, conved.at(q - 3))
                        for k in range(KC):
                            mm = pe.matmul(ps[:, q % 4, 0:segs * T], w[:, k, j * P:(j + 1) * P], src[:, k, 0:segs * T],
                                           start=k == 0, stop=k == KC - 1)
                        mm.then_inc(full.sem, full.tick())
                        q += 1
                    K.done_at[g0 + 2 * n + t] = full.count

        @block.scalar
        def _(act):
            q = 0
            for dst, taps, segs in jobs:
                for c in range(KC):
                    act.wait_ge(full.sem, full.at(q + 1))
                    seg = ps[:, q % 4, 0:segs * T].rearrange("p (s t) -> p s t", s=segs)
                    if q >= 2:
                        act.wait_ge(out.sem, out.at(q - 1))
                    scale = 1.0 if taps is None else K.col("conv_a1", taps + c)
                    act.activation(cv[:, q % 2, 0:segs, :], seg, ACT.Copy, scale=scale).then_inc(base.sem, base.tick())
                    act.wait_ge(conved.sem, conved.at(q + 1))
                    act.activation(dst[:, c, 0:segs * T].rearrange("p (s t) -> p s t", s=segs),
                                          cv[:, q % 2, 0:segs, :], ACT.Silu).then_inc(out.sem, out.tick())
                    q += 1

        @block.vector
        def _(dve):
            own = K.own["dve"]
            q = 0
            for dst, taps, segs in jobs:
                for c in range(KC):
                    dve.wait_ge(base.sem, base.at(q + 1))
                    seg = ps[:, q % 4, 0:segs * T].rearrange("p (s t) -> p s t", s=segs)
                    b = cv[:, q % 2, 0:segs, :]
                    if taps is None:
                        dve.tensor_copy(b[:, :, 0:1], b[:, :, 0:1]).then_inc(conved.sem, conved.tick())
                    else:
                        dve.scalar_tensor_tensor(out=b[:, :, 1:T], in0=seg[:, :, 0:T - 1], scalar=K.col("conv_a0", taps + c),
                                                          in1=b[:, :, 1:T], op0=ALU.mult, op1=ALU.add).then_inc(own.sem, own.tick())
                        dve.wait_ge(own.sem, own.count)
                        dve.scalar_tensor_tensor(out=b[:, :, 0:T - 1], in0=seg[:, :, 1:T], scalar=K.col("conv_a2", taps + c),
                                                           in1=b[:, :, 0:T - 1], op0=ALU.mult, op1=ALU.add).then_inc(conved.sem, conved.tick())
                    q += 1

        @block.sync
        def _(sp):
            K.issue(sp, g0 + 8 + RING)
    K.used = g0 + 8


def stage_head_norm(K, S, t, n, scale, eps_scale=1.0, gain=None, times=None):
    nc = K.nc
    squared, summed, rooted, spread, scaled, done = (K.counter(x) for x in (
        "hn_squared", "hn_summed", "hn_rooted", "hn_spread", "hn_scaled", "hn_done"))
    inverted = K.counter("hn_inverted")
    with K.stage() as st:
        sq = K.sb("hn_sq", [P, 2, n], ctx=st)
        r = K.sb("hn_r", [NH, n], ctx=st)
        ps = K.ps("hn_ps", [P, 3, 512], st)
        block = st.enter_context(nc.Block())

        @block.scalar
        def _(act):
            for h in range(NH):
                if h >= 2:
                    act.wait_ge(summed.sem, summed.at(h - 1))
                act.activation(sq[:, h % 2, :], t[:, h, 0:n], ACT.Square, scale=eps_scale ** 0.5).then_inc(squared.sem, squared.tick())
            act.wait_ge(summed.sem, summed.at(NH))
            act.activation(r[:, :], ps[0:NH, 0, 0:n], ACT.Sqrt, bias=K.epsb[0:NH, :]).then_inc(rooted.sem, rooted.tick())

        @block.tensor
        def _(pe):
            for h in range(NH):
                pe.wait_ge(squared.sem, squared.at(h + 1))
                pe.matmul(ps[0:NH, 0, 0:n], S["head_sum"][:, h, :], sq[:, h % 2, :], start=h == 0, stop=h == NH - 1).then_inc(summed.sem, summed.tick())
            pe.wait_ge(inverted.sem, inverted.at(1))
            for h in range(NH):
                if h >= 2:
                    pe.wait_ge(scaled.sem, scaled.at(h - 1))
                pe.matmul(ps[:, 1 + h % 2, 0:n], S["head_row"][:, h, :], r[:, :], start=True, stop=True).then_inc(spread.sem, spread.tick())

        @block.vector
        def _(dve):
            dve.wait_ge(rooted.sem, rooted.at(1))
            dve.reciprocal(r[:, :], r[:, :]).then_inc(inverted.sem, inverted.tick())
            for h in range(NH):
                dve.wait_ge(spread.sem, spread.at(h + 1))
                dve.scalar_tensor_tensor(out=t[:, h, 0:n], in0=t[:, h, 0:n],
                                                   scalar=scale if gain is None else gain, in1=ps[:, 1 + h % 2, 0:n],
                                                   op0=ALU.mult, op1=ALU.mult).then_inc(scaled.sem, scaled.tick())

        if times is not None:
            @block.gpsimd
            def _(pool):
                for h in range(NH):
                    pool.wait_ge(scaled.sem, scaled.at(h + 1))
                    pool.tensor_tensor(t[:, h, 0:n], t[:, h, 0:n], times[:, h, 0:n], ALU.mult).then_inc(done.sem, done.tick())


def stage_delta_setup(K, S):
    nc, io = K.nc, K.io
    loads, made = K.counter("delta_loads", 16), K.counter("delta_made")
    with K.stage() as st:
        block = st.enter_context(nc.Block())

        @block.scalar
        def _(act):
            w = io["w_in_a_2"][0].rearrange("(k p) n -> p k n", p=P)[:, :, 4 * D:4 * D + 4 * NH]
            act.dma_start(S["wg"][:, :, :], w).then_inc(loads.sem, loads.tick())
            for i, n in enumerate(("dt_bias_a_2", "a_log_a_2")):
                act.dma_start(S["rows"][:, i, :], io[n].rearrange("a d h -> a (d h)").broadcast_to([P, 2 * NH])).then_inc(loads.sem, loads.tick())
            act.wait_ge(loads.sem, loads.at(3))

        @block.gpsimd
        def _(pool):
            own = K.own["pool"]
            pool.memset(S["head_sum"][:, :, :], 0.0).then_inc(own.sem, own.tick())
            pool.wait_ge(own.sem, own.count)
            pool.memset(S["head_row"][:, :, :], 1.0).then_inc(own.sem, own.tick())
            pool.wait_ge(own.sem, own.count)
            pool.memset(S["level"][:, :, :, :], 0.0).then_inc(own.sem, own.tick())
            pool.wait_ge(own.sem, own.count)
            for h in range(NH):
                pool.memset(S["head_sum"][:, h, h:h + 1], 1.0).then_inc(made.sem, made.tick())
            pool.affine_select(out=S["head_row"][:, :, :], in_=S["head_row"][:, :, :], compare_op=ALU.is_equal, fill=0.0,
                                       base=0, pattern=[[1, NH], [0, P]], channel_multiplier=-1).then_inc(made.sem, made.tick())
            for k in range(7):
                s = 1 << k
                nb = P // (2 * s)
                for d in range(2):
                    m = S["level"][:, d, k, :].rearrange("p (b o i) -> p b o i", o=2, i=s)[:, :, d, :]
                    lo = s if d == 0 else 0
                    pool.memset(m, 1.0).then_inc(own.sem, own.tick())
                    pool.wait_ge(own.sem, own.count)
                    pool.affine_select(out=m, in_=m, compare_op=ALU.is_ge, fill=0.0, base=-lo,
                                                 pattern=[[-2 * s, nb], [0, s]], channel_multiplier=1).then_inc(own.sem, own.tick())
                    pool.wait_ge(own.sem, own.count)
                    pool.affine_select(out=m, in_=m, compare_op=ALU.is_ge, fill=0.0, base=lo + s - 1,
                                               pattern=[[2 * s, nb], [0, s]], channel_multiplier=-1).then_inc(made.sem, made.tick())


def stage_delta_gates(K, S, src):
    nc = K.nc
    full, took, added, size, gated, sums, out = (K.counter(x) for x in (
        "dg_full", "dg_took", "dg_added", "dg_size", "dg_gated", "dg_sums", "dg_out"))
    with K.stage() as st:
        a = K.sb("dg_a", [P, 2, 4, NH], ctx=st)
        b = K.sb("dg_b", [P, 2, 4, NH], ctx=st)
        ps = K.ps("dg_ps", [P, 2, 512], st)
        block = st.enter_context(nc.Block())
        prod = ps[:, 0, 0:P].rearrange("p (t f d h) -> p f d t h", t=4, f=2, d=2)
        flat = lambda x: x[:, :, :, :].rearrange("p d t h -> p (d t h)")

        @block.tensor
        def _(pe):
            for t in range(4):
                for k in range(KC):
                    mm = pe.matmul(ps[:, 0, 32 * t:32 * t + 32], src[:, k, t * P:(t + 1) * P], S["wg"][:, k, :],
                                   start=k == 0, stop=k == KC - 1)
            mm.then_inc(full.sem, full.tick())
            pe.wait_ge(gated.sem, gated.at(1))
            for d in range(2):
                pe.matmul(ps[:, 1, 32 * d:32 * d + 32], K.incl[:, d, :], a[:, d].rearrange("p t h -> p (t h)"), start=True, stop=True)
            pe.matmul(ps[:, 1, 64:128], K.ones[:, :], flat(a), start=True, stop=True).then_inc(sums.sem, sums.tick())

        @block.scalar
        def _(act):
            act.wait_ge(full.sem, full.at(1))
            for d in range(2):
                act.activation(S["beta"][:, d], prod[:, 0, d], ACT.Sigmoid).then_inc(took.sem, took.tick())
            act.wait_ge(added.sem, added.at(1))
            act.activation(b[:, :], a[:, :], ACT.Abs).then_inc(took.sem, took.tick())
            act.wait_ge(took.sem, took.at(3))
            act.activation(b[:, :], b[:, :], ACT.Exp, scale=-1.0).then_inc(took.sem, took.tick())
            act.wait_ge(took.sem, took.at(4))
            act.activation(b[:, :], b[:, :], ACT.Ln, bias=1.0).then_inc(size.sem, size.tick())
            act.activation(S["rows"][:, 1, :], S["rows"][:, 1, :], ACT.Exp).then_inc(size.sem, size.tick())
            act.wait_ge(out.sem, out.at(3))
            act.activation(S["egl"][:, :], S["gl"][:, :], ACT.Exp)
            act.activation(S["negegc"][:, :], S["gc"][:, :], ACT.Exp)
            act.activation(S["ekd"][:, :], S["ekd"][:, :], ACT.Exp)

        @block.vector
        def _(dve):
            own = K.own["dve"]
            row = lambda i: S["rows"][:, i, :].rearrange("p (d h) -> p d h", d=2)
            dve.wait_ge(took.sem, took.at(2))
            for d in range(2):
                ins = dve.tensor_tensor(a[:, d], prod[:, 1, d], row(0)[:, d, :].unsqueeze(1).broadcast_to([P, 4, NH]), ALU.add)
                if d == 0:
                    ins.then_inc(own.sem, own.tick())
                    dve.wait_ge(own.sem, own.count)
            ins.then_inc(added.sem, added.tick())
            dve.wait_ge(size.sem, size.at(2))
            dve.scalar_tensor_tensor(out=b[:, :], in0=a[:, :], scalar=0.0, in1=b[:, :], op0=ALU.max, op1=ALU.add).then_inc(own.sem, own.tick())
            dve.wait_ge(own.sem, own.count)
            for d in range(2):
                ins = dve.scalar_tensor_tensor(out=a[:, d], in0=b[:, d], scalar=-1.0,
                                               in1=row(1)[:, d, :].unsqueeze(1).broadcast_to([P, 4, NH]), op0=ALU.mult, op1=ALU.mult)
                if d == 0:
                    ins.then_inc(own.sem, own.tick())
                    dve.wait_ge(own.sem, own.count)
            ins.then_inc(gated.sem, gated.tick())
            dve.wait_ge(sums.sem, sums.at(1))
            dve.tensor_copy(flat(S["gc"]), ps[:, 1, 0:64]).then_inc(out.sem, out.tick())
            dve.tensor_copy(flat(S["gl"]), ps[:, 1, 64:128]).then_inc(out.sem, out.tick())
            dve.wait_ge(out.sem, out.at(2))
            dve.tensor_tensor(flat(S["ekd"]), flat(S["gl"]), flat(S["gc"]), ALU.subtract).then_inc(out.sem, out.tick())


def stage_delta_finish_gates(K, S):
    with K.stage() as st:
        block = st.enter_context(K.nc.Block())

        @block.vector
        def _(dve):
            dve.tensor_scalar(S["negegc"][:, :], S["negegc"][:, :], -1.0, None, ALU.mult)


def stage_turn_values(K, v):
    nc = K.nc
    turned, moved = K.counter("tv_turned"), K.counter("tv_moved")
    with K.stage() as st:
        ps = K.ps("tv_ps", [P, 2, 512], st)
        block = st.enter_context(nc.Block())

        @block.tensor
        def _(pe):
            for h in range(NH):
                if h >= 2:
                    pe.wait_ge(moved.sem, moved.at(h - 1))
                for t in range(4):
                    mm = pe.transpose(ps[:, h % 2, t * P:(t + 1) * P], v[:, h, t * P:(t + 1) * P], K.ident[:, :])
                mm.then_inc(turned.sem, turned.tick())

        @block.scalar
        def _(act):
            for h in range(NH):
                act.wait_ge(turned.sem, turned.at(h + 1))
                act.activation(v[:, h, :], ps[:, h % 2, :], ACT.Copy).then_inc(moved.sem, moved.tick())


CHAIN = ([("new", 0), ("state", 0)] +
         [(what, s) for s in (1, 2, 3) for what in ("read", "new", "state")])
ORDER = ((2, 3, 0, 1), (3, 2, 1, 0))
LEVELS = 7


def stage_delta(K, S, qT, kT, v):
    nc = K.nc
    names = ("gram", "gram_used", "turned", "kd", "diag", "sums", "diff", "masked", "decay", "decay_beta", "sums_used",
             "lt", "qd", "z", "t1", "uv", "x", "first", "chain_read", "rest", "new", "new_done", "state", "state_done", "o_taken")
    dl = {n: K.counter("dl_" + n) for n in names}
    with K.stage() as st:
        kd = K.sb("dl_kd", [P, 2, 2, 4, P], ctx=st)
        E = K.sb("dl_E", [P, 2, 4, P], ctx=st)
        Eb = K.sb("dl_Eb", [P, 2, 4, P], ctx=st)
        LT = K.sb("dl_LT", [P, 2, 4, P], ctx=st)
        X = K.sb("dl_X", [P, 2, 4, P], ctx=st)
        XT = K.sb("dl_XT", [P, 2, 2, 4, P], ctx=st)
        T1 = K.sb("dl_T1", [P, 2, 4, P], ctx=st)
        pt = K.sb("dl_pt", [P, 2, 2, 2, P], ctx=st)
        qd = K.sb("dl_qd", [P, 2, 2, T], ctx=st)
        er = K.sb("dl_er", [P, 2, T], ctx=st)
        Ss = K.sb("dl_S", [P, 2, P], ctx=st)
        res = K.sb("dl_res", [P, 2, P], ctx=st)
        vn = K.sb("dl_vn", [P, 2, P], ctx=st)
        g_ps = K.ps("dl_gram", [P, 4, P], st)
        a_ps = K.ps("dl_a", [P, 2, 4, P], st)
        b_ps = K.ps("dl_b", [P, 2, 4, P], st)
        c_ps = K.ps("dl_c", [P, 2, 4, P], st)
        o_ps = K.ps("dl_o", [P, 4, P], st)
        block = st.enter_context(nc.Block())
        wide = lambda ap, n: ap.unsqueeze(2).broadcast_to([P, n, P])
        col = lambda t, d, tile, h: t[:, d, tile, h:h + 1]
        ident4 = K.ident[:, :].unsqueeze(1).broadcast_to([P, 4, P])

        def schedule():
            for h in range(NH + 1):
                chain = iter(CHAIN if h else ())
                if h < NH:
                    yield "prep", h, None
                for k in range(LEVELS):
                    for what in ("cross", "join"):
                        if h < NH:
                            yield what, h, k
                        step = next(chain, None)
                        if step:
                            yield step[0], h - 1, step[1]

        @block.tensor
        def _(pe):
            for what, h, k in schedule():
                if what == "prep":
                    if h:
                        pe.wait_ge(dl["gram_used"].sem, dl["gram_used"].at(2 * h))
                        pe.wait_ge(dl["x"].sem, dl["x"].at(2 * LEVELS * h))
                    for t in range(4):
                        mm = pe.transpose(g_ps[:, t, :], kT[:, h, t * P:(t + 1) * P], K.ident[:, :])
                    mm.then_inc(dl["turned"].sem, dl["turned"].tick())
                    pe.wait_ge(dl["kd"].sem, dl["kd"].at(8 * (h + 1)))
                    for t in range(4):
                        pe.matmul(g_ps[:, t, :], kT[:, h, t * P:(t + 1) * P], kT[:, h, t * P:(t + 1) * P], start=True, stop=True)
                    for t in range(2):
                        mm = pe.matmul(b_ps[:, 0, t, :], kT[:, h, t * P:(t + 1) * P], qT[:, h, t * P:(t + 1) * P], start=True, stop=True)
                    mm.then_inc(dl["gram"].sem, dl["gram"].tick())
                    for d in range(2):
                        pe.wait_ge(dl["diag"].sem, dl["diag"].at(2 * h + d + 1))
                        for t in range(4):
                            mm = pe.matmul(a_ps[:, d, t, :], K.ones[:, :], Eb[:, d, t, :], start=True, stop=True)
                        mm.then_inc(dl["sums"].sem, dl["sums"].tick())
                elif what == "cross":
                    for d in range(2):
                        if k == 0:
                            pe.wait_ge(dl["lt"].sem, dl["lt"].at(2 * h + d + 1))
                            pe.wait_ge(dl["sums_used"].sem, dl["sums_used"].at(2 * h + d + 1))
                        else:
                            pe.wait_ge(dl["x"].sem, dl["x"].at(2 * (LEVELS * h + k - 1) + d + 1))
                        for t in range(4):
                            mm = pe.matmul(a_ps[:, d, t, :], LT[:, d, t, :], K.ident[:, :] if k == 0 else X[:, d, t, :],
                                           start=True, stop=True)
                        mm.then_inc(dl["z"].sem, dl["z"].tick())
                elif what == "join":
                    if k == 0:
                        continue
                    for d in range(2):
                        pe.wait_ge(dl["t1"].sem, dl["t1"].at(2 * (LEVELS * h + k) + d + 1))
                        if k == 1:
                            pe.wait_ge(dl["gram_used"].sem, dl["gram_used"].at(2 * h + 2))
                        for t in range(4):
                            if k < LEVELS - 1:
                                pe.matmul(a_ps[:, d, t, :], XT[:, h % 2, d, t, :], T1[:, d, t, :], start=True, stop=True)
                            mm = pe.matmul(b_ps[:, d, t, :], T1[:, d, t, :], XT[:, h % 2, d, t, :], start=True, stop=True)
                        mm.then_inc(dl["uv"].sem, dl["uv"].tick())
                elif what == "read":
                    for d in range(2):
                        t = ORDER[d][k]
                        pe.wait_ge(dl["state_done"].sem, dl["state_done"].at(2 * (3 * h + k - 1) + d + 1))
                        pe.matmul(c_ps[:, d, 0, :], kT[:, h, t * P:(t + 1) * P], Ss[:, d, :], start=True, stop=True).then_inc(dl["chain_read"].sem, dl["chain_read"].tick())
                elif what == "new":
                    for d in range(2):
                        t = ORDER[d][k]
                        if k == 0:
                            pe.wait_ge(dl["x"].sem, dl["x"].at(2 * (LEVELS * (h + 1) - 1) + d + 1))
                            if h:
                                pe.wait_ge(dl["state_done"].sem, dl["state_done"].at(2 * 3 * h))
                                pe.wait_ge(dl["new_done"].sem, dl["new_done"].at(2 * 4 * h))
                        else:
                            pe.wait_ge(dl["rest"].sem, dl["rest"].at(2 * (3 * h + k - 1) + d + 1))
                        rhs = v[:, h, t * P:(t + 1) * P] if k == 0 else res[:, d, :]
                        pe.matmul(c_ps[:, d, 1, :], XT[:, h % 2, d, t, :], rhs, start=True, stop=True).then_inc(dl["new"].sem, dl["new"].tick())
                elif what == "state":
                    for d in range(2):
                        t = ORDER[d][k]
                        pe.wait_ge(dl["new_done"].sem, dl["new_done"].at(2 * (4 * h + k) + d + 1))
                        if k >= 2:
                            if k == 2 and d == 0:
                                pe.wait_ge(dl["qd"].sem, dl["qd"].at(2 * h + 2))
                                if h:
                                    pe.wait_ge(dl["o_taken"].sem, dl["o_taken"].at(h))
                            pe.matmul(o_ps[:, t, :], Ss[:, d, :], qd[:, h % 2, d, t * P:(t + 1) * P],
                                      start=k == 2 and d == 0, stop=False, skip_group_check=True)
                            mm = pe.matmul(o_ps[:, t, :], vn[:, d, :], pt[:, h % 2, d, t, :],
                                           start=False, stop=k == 3 and d == 1, skip_group_check=True)
                        if k < 3:
                            mm = pe.matmul(c_ps[:, d, 2, :], kd[:, h % 2, d, t, :], vn[:, d, :], start=True, stop=True)
                        mm.then_inc(dl["state"].sem, dl["state"].tick())

        @block.gpsimd
        def _(pool):
            for what, h, k in schedule():
                if what == "prep":
                    for d in range(2):
                        if h:
                            pool.wait_ge(dl["lt"].sem, dl["lt"].at(2 * (h - 1) + d + 1))
                        pool.tensor_tensor(Eb[:, d], ident4, wide(S["gc"][:, d, :, h], 4), ALU.mult).then_inc(dl["diag"].sem, dl["diag"].tick())
                    for d in range(2):
                        pool.wait_ge(dl["diff"].sem, dl["diff"].at(2 * h + d + 1))
                        sign = 1 if d == 0 else -1
                        pool.affine_select(out=E[:, d], in_=E[:, d], compare_op=ALU.is_ge, fill=-BIG, base=0,
                                                           pattern=[[0, 4], [sign, P]], channel_multiplier=-sign).then_inc(dl["masked"].sem, dl["masked"].tick())
                        pool.wait_ge(dl["decay"].sem, dl["decay"].at(2 * h + d + 1))
                        pool.wait_ge(dl["sums_used"].sem, dl["sums_used"].at(2 * h + d + 1))
                        pool.tensor_tensor(Eb[:, d], E[:, d], wide(S["beta"][:, d, :, h], 4), ALU.mult).then_inc(dl["decay_beta"].sem, dl["decay_beta"].tick())
                        pool.tensor_tensor(qd[:, h % 2, d, :], qT[:, h, :], er[:, d, :], ALU.mult).then_inc(dl["qd"].sem, dl["qd"].tick())
                elif what == "join" and k == 0:
                    for d in range(2):
                        pool.wait_ge(dl["z"].sem, dl["z"].at(2 * LEVELS * h + d + 1))
                        mask = S["level"][:, 1 - d, 0, :].unsqueeze(1).broadcast_to([P, 4, P])
                        own = K.own["pool"]
                        pool.tensor_tensor(XT[:, h % 2, d], LT[:, d], mask, ALU.mult).then_inc(own.sem, own.tick())
                        pool.wait_ge(own.sem, own.count)
                        pool.tensor_tensor(XT[:, h % 2, d], ident4, XT[:, h % 2, d], ALU.subtract).then_inc(dl["first"].sem, dl["first"].tick())

        @block.scalar
        def _(act):
            for what, h, k in schedule():
                if what == "prep":
                    act.wait_ge(dl["turned"].sem, dl["turned"].at(h + 1))
                    for d in range(2):
                        for t in range(4):
                            act.activation(kd[:, h % 2, d, t, :], g_ps[:, t, :], ACT.Copy, scale=col(S["ekd"], d, t, h)).then_inc(dl["kd"].sem, dl["kd"].tick())
                    for d in range(2):
                        act.wait_ge(dl["diff"].sem, dl["diff"].at(2 * h + d + 1))
                        if h:
                            act.wait_ge(dl["qd"].sem, dl["qd"].at(2 * (h - 1) + d + 1))
                        act.activation(er[:, d, :], a_ps[:, d, 0:2, :].rearrange("p t i -> p (t i)"), ACT.Exp).then_inc(dl["sums_used"].sem, dl["sums_used"].tick())
                        act.wait_ge(dl["masked"].sem, dl["masked"].at(2 * h + d + 1))
                        act.activation(E[:, d], E[:, d], ACT.Exp).then_inc(dl["decay"].sem, dl["decay"].tick())
                elif what == "new":
                    for d in range(2):
                        t = ORDER[d][k]
                        act.wait_ge(dl["new"].sem, dl["new"].at(2 * (4 * h + k) + d + 1))
                        act.activation(vn[:, d, :], c_ps[:, d, 1, :], ACT.Copy, scale=col(S["beta"], d, t, h)).then_inc(dl["new_done"].sem, dl["new_done"].tick())
                elif what == "state" and k == 3:
                    act.wait_ge(dl["state"].sem, dl["state"].at(2 * (4 * h + 3) + 2))
                    act.activation(qT[:, h, :], o_ps[:, 0:2, :].rearrange("p t i -> p (t i)"), ACT.Copy).then_inc(dl["o_taken"].sem, dl["o_taken"].tick())

        @block.vector
        def _(dve):
            own = K.own["dve"]
            for what, h, k in schedule():
                if what == "prep":
                    for d in range(2):
                        dve.wait_ge(dl["sums"].sem, dl["sums"].at(2 * h + d + 1))
                        dve.tensor_tensor(E[:, d], a_ps[:, d], wide(S["gc"][:, d, :, h], 4), ALU.subtract).then_inc(dl["diff"].sem, dl["diff"].tick())
                    dve.wait_ge(dl["gram"].sem, dl["gram"].at(h + 1))
                    for d in range(2):
                        dve.wait_ge(dl["decay_beta"].sem, dl["decay_beta"].at(2 * h + d + 1))
                        dve.tensor_tensor(LT[:, d], g_ps[:, :, :], Eb[:, d], ALU.mult).then_inc(dl["lt"].sem, dl["lt"].tick())
                        dve.tensor_tensor(pt[:, h % 2, d], b_ps[:, 0, 0:2, :], E[:, d, 0:2], ALU.mult).then_inc(dl["gram_used"].sem, dl["gram_used"].tick())
                elif what == "cross":
                    for d in range(2):
                        dve.wait_ge(dl["z"].sem, dl["z"].at(2 * (LEVELS * h + k) + d + 1))
                        mask = S["level"][:, d, k, :].unsqueeze(1).broadcast_to([P, 4, P])
                        dve.tensor_tensor(T1[:, d], a_ps[:, d], mask, ALU.mult).then_inc(dl["t1"].sem, dl["t1"].tick())
                elif what == "join":
                    for d in range(2):
                        if k == 0:
                            dve.wait_ge(dl["t1"].sem, dl["t1"].at(2 * LEVELS * h + d + 1))
                            dve.wait_ge(dl["first"].sem, dl["first"].at(2 * h + d + 1))
                            dve.tensor_tensor(X[:, d], ident4, T1[:, d], ALU.subtract).then_inc(dl["x"].sem, dl["x"].tick())
                        else:
                            dve.wait_ge(dl["uv"].sem, dl["uv"].at(2 * ((LEVELS - 1) * h + k - 1) + d + 1))
                            if k < LEVELS - 1:
                                dve.tensor_tensor(X[:, d], X[:, d], a_ps[:, d], ALU.subtract).then_inc(own.sem, own.tick())
                                dve.wait_ge(own.sem, own.count)
                            dve.tensor_tensor(XT[:, h % 2, d], XT[:, h % 2, d], b_ps[:, d], ALU.subtract).then_inc(dl["x"].sem, dl["x"].tick())
                elif what == "read":
                    for d in range(2):
                        t = ORDER[d][k]
                        dve.wait_ge(dl["chain_read"].sem, dl["chain_read"].at(2 * (3 * h + k - 1) + d + 1))
                        dve.scalar_tensor_tensor(out=res[:, d, :], in0=c_ps[:, d, 0, :], scalar=col(S["negegc"], d, t, h),
                                                               in1=v[:, h, t * P:(t + 1) * P], op0=ALU.mult, op1=ALU.add).then_inc(dl["rest"].sem, dl["rest"].tick())
                elif what == "state" and k < 3:
                    for d in range(2):
                        t = ORDER[d][k]
                        dve.wait_ge(dl["state"].sem, dl["state"].at(2 * (4 * h + k) + d + 1))
                        if k == 0:
                            dve.tensor_copy(Ss[:, d, :], c_ps[:, d, 2, :]).then_inc(dl["state_done"].sem, dl["state_done"].tick())
                        else:
                            dve.scalar_tensor_tensor(out=Ss[:, d, :], in0=Ss[:, d, :], scalar=col(S["egl"], d, t, h),
                                                                         in1=c_ps[:, d, 2, :], op0=ALU.mult, op1=ALU.add).then_inc(dl["state_done"].sem, dl["state_done"].tick())


def stage_grid_conv(K, proj, dst):
    made, conved = K.counter("gc_made"), K.counter("gc_conved")
    with K.stage() as st:
        cv = K.sb("gc_cv", [P, KC, T], ctx=st)
        block = st.enter_context(K.nc.Block())

        @block.gpsimd
        def _(pool):
            for c in range(KC):
                pool.tensor_tensor(proj[:, 2 * KC + c, :], proj[:, KC + c, :], proj[:, 2 * KC + c, :], ALU.mult).then_inc(made.sem, made.tick())

        @block.vector
        def _(dve):
            own = K.own["dve"]
            for c in range(KC):
                dve.wait_ge(made.sem, made.at(c + 1))
                u, o = proj[:, 2 * KC + c, :], cv[:, c, :]
                dve.tensor_scalar(o, u, K.col("conv_b1", c), None, ALU.mult).then_inc(own.sem, own.tick())
                dve.wait_ge(own.sem, own.count)
                if c < KC // 2:
                    u, o = (x.rearrange("p (r w) -> p r w", w=GRID_W) for x in (u, o))
                    parts = ((0, o[:, :, 1:], u[:, :, :-1]), (2, o[:, :, :-1], u[:, :, 1:]))
                else:
                    parts = ((0, o[:, GRID_W:], u[:, :-GRID_W]), (2, o[:, :-GRID_W], u[:, GRID_W:]))
                for tap, to, of in parts:
                    dve.scalar_tensor_tensor(out=to, in0=of, scalar=K.col(f"conv_b{tap}", c), in1=to,
                                                      op0=ALU.mult, op1=ALU.add).then_inc(own.sem, own.tick())
                    dve.wait_ge(own.sem, own.count)
                dve.tensor_tensor(dst[:, c, :], cv[:, c, :], proj[:, c, :], ALU.mult)


def stage_router(K, l, hT, wb):
    nc = K.nc
    loads, full, tops, size, exps, ready, diag, spread, moved, made = (K.counter(x, 16 if x == "rt_loads" else 1) for x in (
        "rt_loads", "rt_full", "rt_tops", "rt_size", "rt_exps", "rt_ready", "rt_diag", "rt_spread", "rt_moved", "rt_made"))
    NG = N_GRP + N_EXP
    with K.stage() as st:
        rw = K.sb("rt_w", [P, KC, NG], ctx=st)
        lg = K.sb("rt_lg", [P, TT, 8], ctx=st)
        le = K.sb("rt_le", [P, TT, N_EXP], ctx=st)
        top = K.sb("rt_top", [P, TT, 2, 8], ctx=st)
        idx = K.sb("rt_idx", [P, TT, 2, 8], U32, ctx=st)
        idf = K.sb("rt_idf", [P, TT, 2, 8], ctx=st)
        sel = K.sb("rt_sel", [P, TT, 8], ctx=st)
        ex = K.sb("rt_ex", [P, TT, 8], ctx=st)
        wt = K.sb("rt_wt", [P, TT, 2, N_EXP], ctx=st)
        iota = K.sb("rt_iota", [P, N_EXP], ctx=st)
        dg = K.sb("rt_dg", [P, 2, 4, P], ctx=st)
        l_ps = K.ps("rt_ps", [P, 512], st)
        w_ps = K.ps("rt_wps", [P, 2, 512], st)
        block = st.enter_context(nc.Block())

        @block.sync
        def _(sp):
            sp.dma_start(rw[:, :, 0:N_GRP], K.io["router_g_2"][l].rearrange("(k p) n -> p k n", p=P)).then_inc(loads.sem, loads.tick())
            sp.dma_start(rw[:, :, N_GRP:NG], K.io["router_e_2"][l].rearrange("(k p) n -> p k n", p=P)).then_inc(loads.sem, loads.tick())

        @block.gpsimd
        def _(pool):
            pool.memset(lg[:, :, :], -BIG).then_inc(made.sem, made.tick())
            pool.iota(iota[:, :], pattern=[[1, N_EXP]], base=0, channel_multiplier=0,
                              allow_small_or_imprecise_dtypes=True).then_inc(made.sem, made.tick())

        @block.tensor
        def _(pe):
            pe.wait_ge(loads.sem, loads.at(2))
            for t in range(TT):
                for k in range(KC):
                    mm = pe.matmul(l_ps[:, t * NG:(t + 1) * NG], hT[:, k, t * P:(t + 1) * P], rw[:, k, :],
                                   start=k == 0, stop=k == KC - 1)
            mm.then_inc(full.sem, full.tick())
            for e in range(0, N_EXP, 2):
                pe.wait_ge(diag.sem, diag.at(e // 2 + 1))
                if e >= 4:
                    pe.wait_ge(moved.sem, moved.at(e // 2 - 1))
                for j in range(4):
                    mm = pe.matmul(w_ps[:, (e // 2) % 2, j * P:(j + 1) * P], K.ones[:, :], dg[:, (e // 2) % 2, j, :],
                                   start=True, stop=True)
                mm.then_inc(spread.sem, spread.tick())

        @block.scalar
        def _(act):
            act.wait_ge(tops.sem, tops.at(1))
            for t in range(TT):
                act.activation(ex[:, t, 0:N_GRP], lg[:, t, 0:N_GRP], ACT.Exp, bias=sel[:, t, 4:5], accum_out=ex[:, t, 4:5]).then_inc(size.sem, size.tick())
            act.wait_ge(tops.sem, tops.at(2))
            for t in range(TT):
                act.activation(ex[:, t, 5:6], top[:, t, 1, 1:2], ACT.Exp, bias=sel[:, t, 5:6]).then_inc(exps.sem, exps.tick())
            for e in range(0, N_EXP, 2):
                act.wait_ge(spread.sem, spread.at(e // 2 + 1))
                act.activation(wb[:, e:e + 2, :].rearrange("p e t -> p (e t)"), w_ps[:, (e // 2) % 2, :], ACT.Copy).then_inc(moved.sem, moved.tick())

        @block.vector
        def _(dve):
            own = K.own["dve"]
            dve.wait_ge(made.sem, made.at(2))
            dve.wait_ge(full.sem, full.at(1))
            logits = l_ps[:, 0:TT * NG].rearrange("p (t n) -> p t n", t=TT)
            dve.tensor_copy(lg[:, :, 0:N_GRP], logits[:, :, 0:N_GRP]).then_inc(own.sem, own.tick())
            dve.wait_ge(own.sem, own.count)
            for t in range(TT):
                dve.max(top[:, t, 0, :], lg[:, t, :]).then_inc(own.sem, own.tick())
                dve.wait_ge(own.sem, own.count)
                dve.max_index(idx[:, t, 0, :], top[:, t, 0, :], lg[:, t, :]).then_inc(own.sem, own.tick())
                dve.wait_ge(own.sem, own.count)
            dve.tensor_copy(idf[:, :, 0, :], idx[:, :, 0, :]).then_inc(own.sem, own.tick())
            dve.wait_ge(own.sem, own.count)
            dve.tensor_scalar(sel[:, :, 4:5], top[:, :, 0, 0:1], -1.0, None, ALU.mult).then_inc(tops.sem, tops.tick())
            for t in range(TT):
                dve.tensor_scalar(sel[:, t, 0:N_GRP], iota[:, 0:N_GRP], idf[:, t, 0, 0:1], None, ALU.is_equal).then_inc(own.sem, own.tick())
                dve.wait_ge(own.sem, own.count)
            dve.tensor_scalar(sel[:, :, 0:N_GRP], sel[:, :, 0:N_GRP], -1.0, BIG, ALU.add, ALU.mult).then_inc(own.sem, own.tick())
            dve.wait_ge(own.sem, own.count)
            for t in range(TT):
                dve.tensor_tensor(le[:, t, :].rearrange("p (g e) -> p g e", g=N_GRP),
                                           logits[:, t, N_GRP:NG].rearrange("p (g e) -> p g e", g=N_GRP),
                                           sel[:, t, 0:N_GRP].unsqueeze(2).broadcast_to([P, N_GRP, E_GRP]), ALU.add).then_inc(own.sem, own.tick())
                dve.wait_ge(own.sem, own.count)
                dve.max(top[:, t, 1, :], le[:, t, :]).then_inc(own.sem, own.tick())
                dve.wait_ge(own.sem, own.count)
                dve.max_index(idx[:, t, 1, :], top[:, t, 1, :], le[:, t, :]).then_inc(own.sem, own.tick())
                dve.wait_ge(own.sem, own.count)
            dve.tensor_copy(idf[:, :, 1, :], idx[:, :, 1, :]).then_inc(own.sem, own.tick())
            dve.wait_ge(own.sem, own.count)
            dve.tensor_scalar(sel[:, :, 5:6], top[:, :, 1, 0:1], -1.0, None, ALU.mult).then_inc(tops.sem, tops.tick())
            dve.wait_ge(exps.sem, exps.at(2))
            dve.tensor_scalar(ex[:, :, 6:7], ex[:, :, 5:6], 1.0, None, ALU.add).then_inc(own.sem, own.tick())
            dve.wait_ge(own.sem, own.count)
            dve.tensor_tensor(ex[:, :, 6:7], ex[:, :, 6:7], ex[:, :, 4:5], ALU.mult).then_inc(own.sem, own.tick())
            dve.wait_ge(own.sem, own.count)
            dve.reciprocal(ex[:, :, 6:7], ex[:, :, 6:7]).then_inc(own.sem, own.tick())
            dve.wait_ge(own.sem, own.count)
            dve.tensor_tensor(ex[:, :, 7:8], ex[:, :, 6:7], ex[:, :, 5:6], ALU.mult).then_inc(own.sem, own.tick())
            dve.wait_ge(own.sem, own.count)
            for t in range(TT):
                for j in range(2):
                    dve.tensor_scalar(wt[:, t, j, :], iota[:, :], idf[:, t, 1, j:j + 1], ex[:, t, 6 + j:7 + j],
                                               ALU.is_equal, ALU.mult).then_inc(own.sem, own.tick())
                    dve.wait_ge(own.sem, own.count)
            dve.tensor_tensor(wt[:, :, 0, :], wt[:, :, 0, :], wt[:, :, 1, :], ALU.add).then_inc(own.sem, own.tick())
            dve.wait_ge(own.sem, own.count)
            for e in range(0, N_EXP, 2):
                if e >= 4:
                    dve.wait_ge(spread.sem, spread.at(e // 2 - 1))
                for j in range(4):
                    ins = dve.tensor_scalar(dg[:, (e // 2) % 2, j, :], K.ident[:, :], wt[:, j % TT, 0, e + j // TT:e + j // TT + 1], None, ALU.mult)
                ins.then_inc(diag.sem, diag.tick())


def queue_experts(K, l):
    io = K.io
    for e in range(N_EXP):
        for n in ("w1_2", "w3_2"):
            K.queue((0, (KC, D_EXP), rows_of(io[n][l, e], 0, D_EXP)))
        K.queue((0, (4, D), rows_of(io["w2_2"][l, e], 0, D)))


def stage_experts(K, l, hT, wb, gate):
    nc, io = K.nc, K.io
    per, fc = 4, D_EXP // P
    rounds = N_EXP // per
    full, hid_done, silued, gated, cleared = K.products, K.counter("ex_hidden"), K.counter("ex_silued"), K.counter("ex_gated"), K.counter("ex_cleared")
    g0 = K.used
    events = fc + 1
    tiles = 3 * per
    with K.stage() as st:
        sil = K.sb("ex_sil", [P, fc, T], ctx=st)
        hid = K.sb("ex_hid", [P, fc, T], ctx=st)
        zero = K.sb("ex_zero", [P, 512], ctx=st)
        gu = K.ps("ex_gu", [P, fc, 512], st)
        y = K.ps("ex_y", [P, 4, 512], st)
        block = st.enter_context(nc.Block())
        p0, h0, s0, t0 = full.base, hid_done.base, silued.base, gated.base
        for e in range(N_EXP):
            for i, n in enumerate((fc, fc, fc + 1)):
                K.done_at[g0 + 3 * e + i] = p0 + events * e + n

        def landed(pe, it, n):
            g = g0 + n
            pe.wait_ge(K.landed[g % RING], it * (16 * tiles // RING) + K.need[g])

        @block.gpsimd
        def _(pool):
            pool.memset(zero[:, :], 0.0).then_inc(cleared.sem, cleared.tick())

        @block.tensor
        def _(pe):
            pe.wait_ge(cleared.sem, cleared.at(1))
            for b in range(4):
                pe.matmul(y[:, b, :], zero[:, 0:P], zero[:, :], start=True, stop=False, skip_group_check=True)
            with pe.Fori(0, rounds) as it:
                for j in range(per):
                    w = [K.ring[(g0 + 3 * j + i) % RING][:, :].rearrange("p (k n) -> p k n", k=KC if i < 2 else 4) for i in range(3)]
                    landed(pe, it, 3 * j)
                    landed(pe, it, 3 * j + 1)
                    for f in range(fc):
                        for i in range(2):
                            for k in range(KC):
                                mm = pe.matmul(gu[:, f, i * T:(i + 1) * T], w[i][:, k, f * P:(f + 1) * P], hT[:, k, :],
                                               start=k == 0, stop=k == KC - 1)
                        mm.then_inc(full.sem, 1)
                    landed(pe, it, 3 * j + 2)
                    for f in range(fc):
                        pe.wait_ge(hid_done.sem, it * (per * fc) + (h0 + j * fc + f + 1))
                        for c in range(KC):
                            mm = pe.matmul(y[:, c // 2, (c % 2) * T:(c % 2 + 1) * T], w[2][:, f, c * P:(c + 1) * P], hid[:, f, :],
                                           start=False, stop=False, skip_group_check=True)
                    mm.then_inc(full.sem, 1)
            full.count = p0 + N_EXP * events

        @block.scalar
        def _(act):
            with act.Fori(0, rounds) as it:
                for j in range(per):
                    for f in range(fc):
                        act.wait_ge(full.sem, it * (per * events) + (p0 + j * events + f + 1))
                        act.activation(sil[:, f, :], gu[:, f, 0:T], ACT.Silu).then_inc(silued.sem, 1)
            silued.count = s0 + N_EXP * fc
            gated.count, hid_done.count = t0 + N_EXP * fc, h0 + N_EXP * fc

        @block.vector
        def _(dve):
            with dve.Fori(0, rounds) as it:
                for j in range(per):
                    for f in range(fc):
                        dve.wait_ge(silued.sem, it * (per * fc) + (s0 + j * fc + f + 1))
                        dve.tensor_tensor(hid[:, f, :], sil[:, f, :], gu[:, f, T:2 * T], ALU.mult).then_inc(gated.sem, 1)
                        dve.wait_ge(gated.sem, it * (per * fc) + (t0 + j * fc + f + 1))
                        dve.tensor_tensor(hid[:, f, :].unsqueeze(1), hid[:, f, :].unsqueeze(1), wb[:, bass.ds(it * per + j, 1), :],
                                          ALU.mult).then_inc(hid_done.sem, 1)
            dve.wait_ge(full.sem, p0 + N_EXP * events)
            for c in range(KC):
                dve.scalar_tensor_tensor(out=K.xT[:, c, :], in0=y[:, c // 2, (c % 2) * T:(c % 2 + 1) * T], scalar=gate(c),
                                         in1=K.xT[:, c, :], op0=ALU.mult, op1=ALU.add)

        @block.sync
        def _(sp):
            K.issue(sp, g0 + RING)
            with sp.Fori(0, rounds - 1) as it:
                for m in range(tiles):
                    n = m + RING
                    e, kind = n // 3, n % 3
                    sp.wait_ge(full.sem, it * (per * events) + (K.done_at[g0 + m]))
                    w = io[("w1_2", "w3_2", "w2_2")[kind]][l][bass.ds(it * per + e, 1)]
                    src = w.rearrange("a (k p) n -> p (a k) n", p=P)
                    dst = K.ring[(g0 + n) % RING][:, :].rearrange("p (k n) -> p k n", k=4 if kind == 2 else KC)
                    sp.dma_start(dst, src).then_inc(K.landed[(g0 + n) % RING], 16)
            for m in range(tiles * (rounds - 1)):
                K.landed_count[(g0 + RING + m) % RING] += 16
            K.issued = g0 + RING + tiles * (rounds - 1)
            K.issue(sp, g0 + 3 * N_EXP + RING)
    K.used = g0 + 3 * N_EXP


def stage_output(K, src, out):
    nc = K.nc
    turned, moved, written = K.counter("out_turned"), K.counter("out_moved"), K.counter("out_written", 16)
    with K.stage() as st:
        rows = K.sb("out_rows", [P, TT, D], ctx=st)
        ps = K.ps("out_ps", [P, 2, 512], st)
        block = st.enter_context(nc.Block())
        quads = TT * KC // 4

        @block.tensor
        def _(pe):
            for q in range(quads):
                if q >= 2:
                    pe.wait_ge(moved.sem, moved.at(q - 1))
                a, c = divmod(4 * q, KC)
                for j in range(4):
                    mm = pe.transpose(ps[:, q % 2, j * P:(j + 1) * P], src[:, c + j, a * P:(a + 1) * P], K.ident[:, :])
                mm.then_inc(turned.sem, turned.tick())

        @block.vector
        def _(dve):
            for q in range(quads):
                dve.wait_ge(turned.sem, turned.at(q + 1))
                a, c = divmod(4 * q, KC)
                dve.tensor_copy(rows[:, a, c * P:(c + 4) * P], ps[:, q % 2, :]).then_inc(moved.sem, moved.tick())

        @block.sync
        def _(sp):
            for a in range(TT):
                sp.wait_ge(moved.sem, moved.at(2 * (a + 1)))
                sp.dma_start(out[0, a * P:(a + 1) * P, :], rows[:, a, :]).then_inc(written.sem, written.tick())
            sp.wait_ge(written.sem, written.at(TT))


def queue_second_block(K):
    io = K.io
    queue_columns(K, io["ada_w_2"][0], 6 * D)
    for c in (D, 2 * D, 0, 3 * D):
        for h in range(2):
            K.queue((0, (KC, 512), rows_of(io["w_in_a_2"][0], c + 512 * h, 512)))
    queue_columns(K, io["w_out_a_2"][0], D)
    queue_experts(K, 0)
    queue_columns(K, io["ada_w_2"][1], 6 * D)
    queue_columns(K, io["w_in_b_2"][0], 3 * D)
    queue_columns(K, io["w_out_b_2"][0], D)
    queue_experts(K, 1)


def second_block(K):
    mods = K.sb("mods", [P, 2, 6 * KC])
    gains = K.sb("gains", [P, 2, 2, KC])
    mod = lambda v, i: (lambda c: mods[:, v, i * KC + c:i * KC + c + 1])
    gain = lambda v, i: (lambda c: gains[:, v, i, c:c + 1])
    stage_ada(K, 0, mods, gains)
    with ExitStack() as part:
        kT = K.sb("dn_kT", [P, NH, 2 * T], ctx=part)
        v = K.sb("dn_v", [P, NH, 2 * T], ctx=part)
        qT = K.sb("dn_qT", [P, NH, T], ctx=part)
        S = {n: K.sb("dn_" + n, [P, 2, 4, NH], ctx=part) for n in ("beta", "gc", "gl", "egl", "negegc", "ekd")}
        S["wg"] = K.sb("dn_wg", [P, KC, 4 * NH], ctx=part)
        S["rows"] = K.sb("dn_rows", [P, 2, 2 * NH], ctx=part)
        S["head_sum"] = K.sb("dn_head_sum", [P, NH, NH], ctx=part)
        S["head_row"] = K.sb("dn_head_row", [NH, NH, P], ctx=part)
        S["level"] = K.sb("dn_level", [P, 2, LEVELS, P], ctx=part)
        stage_delta_setup(K, S)
        with ExitStack() as K.part:
            src = K.sb("dn_src", [P, KC, 2 * T], ctx=K.part)
            turn_rows(K, K.io["ctx_2"][0], kT[:, :, 0:T], "ctx")
            stage_norm(K, kT[:, :, 0:T], src[:, :, T:2 * T], gain(1, 0), shift=mod(1, 0))
            stage_norm(K, K.xT, src[:, :, 0:T], gain(0, 0), shift=mod(0, 0))
            stage_delta_project(K, src, kT, v, qT, K.hT)
            stage_delta_gates(K, S, src)
        stage_delta_finish_gates(K, S)
        stage_head_norm(K, S, kT, 2 * T, 1.0)
        stage_head_norm(K, S, qT, T, P ** -0.5)
        stage_turn_values(K, v)
        stage_delta(K, S, qT, kT, v)
        stage_head_norm(K, S, qT, T, 1.0, eps_scale=1.0 / P, gain=K.col("onorm"), times=K.hT)
        linear_stage(K, qT, KC, copy_to(kT[:, :, 0:T]))
        stage_add_gated(K, kT, mod(0, 2))
    with ExitStack() as part:
        wb = K.sb("expert_weights", [P, N_EXP, T], ctx=part)
        stage_norm(K, K.xT, K.hT, gain(0, 1), shift=mod(0, 3))
        stage_router(K, 0, K.hT, wb)
        stage_experts(K, 0, K.hT, wb, mod(0, 5))
    stage_ada(K, 1, mods, gains)
    with ExitStack() as part:
        proj = K.sb("sc_proj", [P, 3 * KC, T], ctx=part)
        stage_norm(K, K.xT, K.hT, gain(0, 0), shift=mod(0, 0))
        linear_stage(K, K.hT, 3 * KC, copy_to(proj))
        stage_grid_conv(K, proj, K.hT)
        linear_stage(K, K.hT, KC, copy_to(proj))
        stage_add_gated(K, proj, mod(0, 2))
    with ExitStack() as part:
        wb = K.sb("expert_weights", [P, N_EXP, T], ctx=part)
        stage_norm(K, K.xT, K.hT, gain(0, 1), shift=mod(0, 3))
        stage_router(K, 1, K.hT, wb)
        stage_experts(K, 1, K.hT, wb, mod(0, 5))
    stage_norm(K, K.xT, K.hT, lambda c: K.col("final", c))


def two_blocks(nc, io, out):
    with ExitStack() as ctx:
        K = Kit(nc, ctx, io)
        queue_first_block(K)
        queue_second_block(K)
        stage_setup(K)
        first_block(K)
        second_block(K)
        stage_output(K, K.hT, out)


INPUTS = (
    "x", "mem", "norm_mix_pre", "norm_mix_post", "w_in", "b_gate", "ssm_a_re", "ssm_a_im", "ssm_log_dt",
    "ssm_b_re", "ssm_b_im", "ssm_c_re", "ssm_c_im", "ssm_d", "ssm_w_glu", "ssm_b_glu", "w_branch_attn",
    "w_branch_ssm", "w_out", "norm_xa_pre", "norm_xa_post", "norm_mem", "xa_wq", "xa_wk", "xa_wv", "xa_wo",
    "norm_ffn_pre", "norm_ffn_post", "ffn_w_up", "ffn_conv_w", "ffn_conv_b", "ffn_w_down", "c_2", "ctx_2",
    "c_ctx_2", "ada_w_2", "ada_b_2", "norm_mix_2", "norm_ffn_2", "w_in_a_2", "conv_a_2", "a_log_a_2",
    "dt_bias_a_2", "onorm_a_2", "w_out_a_2", "w_in_b_2", "conv_b_2", "w_out_b_2", "router_g_2", "router_e_2",
    "w1_2", "w3_2", "w2_2", "final_norm_2",
)


def kernel(**inputs):
    import numpy as np
    import concourse.bacc as bacc
    from concourse.bass_utils import run_bass_kernel_spmd

    nc = bacc.Bacc("TRN2", target_bir_lowering=False, num_devices=1)
    arrays, io = {}, {}
    for name in INPUTS:
        a = np.ascontiguousarray(inputs[name])
        arrays[f"in_{name}"] = a
        io[name] = nc.dram_tensor(f"in_{name}", a.shape, mybir.dt.from_np(a.dtype), kind="ExternalInput").ap()
    out = nc.dram_tensor("out_0", (1, T, D), F32, kind="ExternalOutput").ap()
    two_blocks(nc, io, out)
    result = run_bass_kernel_spmd(nc, [arrays], core_ids=[0])
    return result.results[0]["out_0"]
```

```python
from contextlib import ExitStack

import concourse.bass as bass
from concourse import mybir
from concourse.alu_op_type import AluOpType as ALU

F32 = mybir.dt.float32
U32 = mybir.dt.uint32
I32 = mybir.dt.int32
ACT = mybir.ActivationFunctionType
AX = mybir.AxisListType

P = 128
T = 256
TT = T // P
D = 1024
KC = D // P
RING = 4
SLOT = 4096
EPS = 1e-6
PI = 3.141592653589793
ROUND = 12582912.0
BIG = 1.0e30

SB_HEADS, SB_DIM = 8, 64
SB_W = SB_HEADS * SB_DIM
SSM_W, SSM_G, SSM_C, SSM_S = 512, 32, 16, 64
ST = SSM_G * SSM_S // P
XA_HEADS = 4
D_FF = 2816
FC = D_FF // P
NH = 8
N_EXP, N_GRP, E_GRP = 32, 4, 8
D_EXP = 512
GRID_W = 64
SLOTS = 64


class Counter:

    def __init__(self, sem, step=1):
        self.sem, self.step, self.count, self.base = sem, step, 0, 0

    def tick(self):
        self.count += self.step
        return self.step

    def at(self, k):
        return self.base + self.step * k


class Kit:

    def __init__(self, nc, ctx, io):
        self.nc, self.ctx, self.io = nc, ctx, io
        self.counters, self.names = {}, {}
        self.tiles, self.issued, self.used = [], 0, 0
        self.landed = [ctx.enter_context(nc.semaphore(f"slot{i}_landed")) for i in range(RING)]
        self.landed_count, self.queued = [0] * RING, [0] * RING
        self.need = []
        self.products = self.counter("products")
        self.done_at = {}
        self.own = {n: Counter(ctx.enter_context(nc.semaphore(f"{n}_own_step"))) for n in ("dve", "act", "pool")}
        self.ring = [self.sb(f"ring{i}", [P, SLOT]) for i in range(RING)]

    def unique(self, name):
        n = self.names[name] = self.names.get(name, 0) + 1
        return name if n == 1 else f"{name}_{n}"

    def sb(self, name, shape, dt=F32, ctx=None):
        return (ctx or self.ctx).enter_context(self.nc.sbuf_tensor(self.unique(name), shape, dt))

    def ps(self, name, shape, ctx, dt=F32):
        return ctx.enter_context(self.nc.psum_tensor(self.unique(name), shape, dt))

    def counter(self, name, step=1):
        if name not in self.counters:
            self.counters[name] = Counter(self.ctx.enter_context(self.nc.semaphore(name)), step)
        return self.counters[name]

    def stage(self):
        for s in self.counters.values():
            s.base = s.count
        return ExitStack()

    def queue(self, *parts):
        slot = len(self.tiles) % RING
        self.queued[slot] += 16 * len(parts)
        self.tiles.append(parts)
        self.need.append(self.queued[slot])

    def issue(self, sp, upto):
        for g in range(self.issued, min(upto, len(self.tiles))):
            if g >= RING:
                sp.wait_ge(self.products.sem, self.done_at[g - RING])
            for off, shape, src in self.tiles[g]:
                n = shape[0] * shape[1]
                dst = self.ring[g % RING][:, off:off + n].rearrange("p (a n) -> p a n", a=shape[0])
                sp.dma_start(dst, src).then_inc(self.landed[g % RING], 16)
                self.landed_count[g % RING] += 16
        self.issued = max(self.issued, min(upto, len(self.tiles)))

    def tile(self, eng, g, a):
        eng.wait_ge(self.landed[g % RING], self.need[g])
        words = sum(s[0] * s[1] for _, s, _ in self.tiles[g])
        return self.ring[g % RING][:, 0:words].rearrange("p (a n) -> p a n", a=a)

    def col(self, name, i=0):
        return self.params[:, self.cols[name] + i:self.cols[name] + i + 1]


def rows_of(w, c0, n):
    return w.rearrange("(k p) n -> p k n", p=P)[:, :, c0:c0 + n]


def queue_columns(K, w, n_total, n=512):
    for c in range(0, n_total, n):
        K.queue((0, (w.shape[0] // P, n), rows_of(w, c, n)))


def vector_rows(K):
    io = K.io
    vec = lambda a: a.rearrange("(c p) -> c p", p=P)
    out = []
    for n in ("norm_mix_pre", "norm_mix_post", "norm_xa_pre", "norm_xa_post", "norm_mem",
              "norm_ffn_pre", "norm_ffn_post", "b_gate", "ssm_b_glu", "ssm_d", "ffn_conv_b"):
        out.append((n, vec(io[n][0])))
    for j in range(3):
        out.append((f"ffn_conv_w{j}", vec(io["ffn_conv_w"][0, j])))
    out.append(("ssm_a_re", io["ssm_a_re"][0].rearrange("(i h) s -> i (h s)", h=2)))
    out.append(("ssm_a_im", io["ssm_a_im"][0].rearrange("(i h) s -> i (h s)", h=2)))
    out.append(("c", vec(io["c_2"][0])))
    out.append(("c_ctx", vec(io["c_ctx_2"])))
    for l in range(2):
        out.append((f"ada_b{l}", vec(io["ada_b_2"][l])))
        out.append((f"norm_mix{l}", vec(io["norm_mix_2"][l])))
        out.append((f"norm_ffn{l}", vec(io["norm_ffn_2"][l])))
    for j in range(3):
        out.append((f"conv_a{j}", vec(io["conv_a_2"][0, j])))
        out.append((f"conv_b{j}", vec(io["conv_b_2"][0, j])))
    out.append(("onorm", vec(io["onorm_a_2"][0])))
    out.append(("final", vec(io["final_norm_2"])))
    return out


def stage_setup(K):
    nc, io = K.nc, K.io
    rows = vector_rows(K)
    n_rows = sum(a.shape[0] for _, a in rows)
    n_tiles = -(-n_rows // P)
    K.cols, pieces, at = {}, [], 0
    for name, a in rows:
        K.cols[name] = at
        done = 0
        while done < a.shape[0]:
            n = min(a.shape[0] - done, P - at % P)
            pieces.append((at // P, at % P, n, a[done:done + n]))
            done, at = done + n, at + n
    K.params = K.sb("params", [P, n_tiles * P])
    K.ident = K.sb("ident", [P, P])
    K.ones = K.sb("ones", [P, P])
    K.incl = K.sb("incl", [P, 2, P])
    K.after = K.sb("after", [P, P])
    K.xT = K.sb("xT", [P, KC, T])
    K.hT = K.sb("hT", [P, KC, T])
    K.rstd = K.sb("rstd", [P, T])
    K.epsb = K.sb("epsb", [P, 1])

    loads, x_loads, made = K.counter("setup_loads", 16), K.counter("setup_x", 16), K.counter("setup_made")
    turned, moved = K.counter("setup_turned"), K.counter("setup_moved")
    with K.stage() as st:
        table = K.sb("param_rows", [P, n_tiles, P], ctx=st)
        x_rows = K.sb("x_rows", [P, TT, D], ctx=st)
        ps = K.ps("setup_ps", [P, 2, 512], st)
        block = st.enter_context(nc.Block())
        n_sync = len(pieces) // 2

        @block.sync
        def _(sp):
            sp.dma_start(x_rows[:, :, :], io["x"][0].rearrange("(a p) d -> p a d", p=P)).then_inc(x_loads.sem, x_loads.tick())
            for t, r, n, a in pieces[:n_sync]:
                if t == n_tiles - 1:
                    sp.wait_ge(made.sem, made.at(1))
                sp.dma_start(table[r:r + n, t, :], a).then_inc(loads.sem, loads.tick())
            K.issue(sp, RING)

        @block.scalar
        def _(act):
            act.wait_ge(made.sem, made.at(1))
            for t, r, n, a in pieces[n_sync:]:
                act.dma_start(table[r:r + n, t, :], a).then_inc(loads.sem, loads.tick())

        @block.gpsimd
        def _(pool):
            pool.memset(table[:, n_tiles - 1, :], 0.0).then_inc(made.sem, made.tick())
            pool.memset(K.ident[:, :], 0.0).then_inc(made.sem, made.tick())
            pool.memset(K.ones[:, :], 1.0).then_inc(made.sem, made.tick())
            pool.memset(K.epsb[:, :], EPS).then_inc(made.sem, made.tick())
            pool.wait_ge(made.sem, made.at(4))
            pool.affine_select(out=K.ident[:, :], in_=K.ident[:, :], compare_op=ALU.not_equal, fill=1.0,
                                       base=0, pattern=[[-1, P]], channel_multiplier=1).then_inc(made.sem, made.tick())
            pool.affine_select(out=K.incl[:, 0, :], in_=K.ones[:, :], compare_op=ALU.is_ge, fill=0.0,
                                       base=0, pattern=[[1, P]], channel_multiplier=-1).then_inc(made.sem, made.tick())
            pool.affine_select(out=K.incl[:, 1, :], in_=K.ones[:, :], compare_op=ALU.is_ge, fill=0.0,
                                       base=0, pattern=[[-1, P]], channel_multiplier=1).then_inc(made.sem, made.tick())
            pool.affine_select(out=K.after[:, :], in_=K.ones[:, :], compare_op=ALU.is_gt, fill=0.0,
                                       base=0, pattern=[[-1, P]], channel_multiplier=1).then_inc(made.sem, made.tick())

        quads = TT * KC // 4

        @block.tensor
        def _(pe):
            pe.wait_ge(made.sem, made.at(5))
            pe.wait_ge(x_loads.sem, x_loads.at(1))
            for q in range(quads + -(-n_tiles // 4)):
                if q >= 2:
                    pe.wait_ge(moved.sem, moved.at(q - 1))
                if q == quads:
                    pe.wait_ge(loads.sem, loads.at(len(pieces)))
                n = 4 if q < quads else min(4, n_tiles - 4 * (q - quads))
                for j in range(n):
                    if q < quads:
                        a, c = divmod(4 * q + j, KC)
                        src = x_rows[:, a, c * P:(c + 1) * P]
                    else:
                        src = table[:, 4 * (q - quads) + j, :]
                    mm = pe.transpose(ps[:, q % 2, j * P:(j + 1) * P], src, K.ident[:, :])
                mm.then_inc(turned.sem, turned.tick())

        @block.vector
        def _(dve):
            for q in range(quads + -(-n_tiles // 4)):
                dve.wait_ge(turned.sem, turned.at(q + 1))
                n = 4 if q < quads else min(4, n_tiles - 4 * (q - quads))
                if q < quads:
                    a, c = divmod(4 * q, KC)
                    dst = K.xT[:, c:c + 4, a * P:(a + 1) * P]
                else:
                    dst = K.params[:, 4 * (q - quads) * P:(4 * (q - quads) + n) * P].rearrange("p (a n) -> p a n", n=P)
                dve.tensor_copy(dst, ps[:, q % 2, 0:n * P].rearrange("p (a n) -> p a n", n=P)).then_inc(moved.sem, moved.tick())


def turn_rows(K, dram, dst, name, rows=None):
    nc = K.nc
    loads, turned, moved = K.counter("rows_landed", 16), K.counter("rows_turned"), K.counter("rows_moved")
    with K.stage() as st:
        load = rows is None
        if load:
            rows = K.sb(f"rows_{name}", [P, TT, D], ctx=st)
        ps = K.ps("rows_ps", [P, 2, 512], st)
        block = st.enter_context(nc.Block())

        if load:
            @block.scalar
            def _(act):
                act.dma_start(rows[:, :, :], dram.rearrange("(a p) d -> p a d", p=P)).then_inc(loads.sem, loads.tick())

        @block.tensor
        def _(pe):
            if load:
                pe.wait_ge(loads.sem, loads.at(1))
            for q in range(TT * KC // 4):
                if q >= 2:
                    pe.wait_ge(moved.sem, moved.at(q - 1))
                for j in range(4):
                    a, c = divmod(4 * q + j, KC)
                    mm = pe.transpose(ps[:, q % 2, j * P:(j + 1) * P], rows[:, a, c * P:(c + 1) * P], K.ident[:, :])
                mm.then_inc(turned.sem, turned.tick())

        @block.vector
        def _(dve):
            for q in range(TT * KC // 4):
                dve.wait_ge(turned.sem, turned.at(q + 1))
                a, c = divmod(4 * q, KC)
                dve.tensor_copy(dst[:, c:c + 4, a * P:(a + 1) * P],
                                         ps[:, q % 2, :].rearrange("p (a n) -> p a n", n=P)).then_inc(moved.sem, moved.tick())


def stage_norm(K, src, dst, gain, shift=None, residual=None, post=None):
    nc = K.nc
    squared, summed, rooted, normed = (K.counter(n) for n in ("norm_squared", "norm_summed", "norm_rooted", "norm_scaled"))
    own = K.own["dve"]
    halves = 2
    with K.stage() as st:
        sq = dst if residual is None and src is not dst else K.sb("norm_sq", [P, KC, T], ctx=st)
        tmp = dst if residual is None else sq
        ss = K.ps("norm_ss", [P, 512], st)
        block = st.enter_context(nc.Block())
        n = KC // halves

        @block.scalar
        def _(act):
            for i in range(halves):
                act.activation(sq[:, i * n:(i + 1) * n, :], src[:, i * n:(i + 1) * n, :], ACT.Square,
                                          scale=D ** -0.5).then_inc(squared.sem, squared.tick())
            act.wait_ge(summed.sem, summed.at(1))
            act.activation(K.rstd[:, :], ss[:, 0:T], ACT.Sqrt, bias=K.epsb[:, :]).then_inc(rooted.sem, rooted.tick())
            if shift is not None:
                for c in range(KC):
                    act.wait_ge(normed.sem, normed.at(c + 1))
                    act.activation(dst[:, c, :], tmp[:, c, :], ACT.Identity, bias=shift(c))

        @block.tensor
        def _(pe):
            for c in range(KC):
                if c % n == 0:
                    pe.wait_ge(squared.sem, squared.at(c // n + 1))
                mm = pe.matmul(ss[:, 0:T], K.ones[:, :], sq[:, c, :], start=c == 0, stop=c == KC - 1)
            mm.then_inc(summed.sem, summed.tick())

        @block.vector
        def _(dve):
            dve.wait_ge(rooted.sem, rooted.at(1))
            dve.reciprocal(K.rstd[:, :], K.rstd[:, :]).then_inc(own.sem, own.tick())
            dve.wait_ge(own.sem, own.count)
            for c in range(KC):
                dve.scalar_tensor_tensor(out=tmp[:, c, :], in0=src[:, c, :], scalar=gain(c), in1=K.rstd[:, :],
                                                   op0=ALU.mult, op1=ALU.mult).then_inc(normed.sem, normed.tick())

        if residual is not None:
            @block.gpsimd
            def _(pool):
                for c in range(KC):
                    pool.wait_ge(normed.sem, normed.at(c + 1))
                    pool.tensor_tensor(dst[:, c, :], tmp[:, c, :], residual[:, c, :], ALU.add)


def linear_stage(K, src, n_chunks, evac, kc=KC, per_tile=4, n=T, beside=None, token_major=()):
    nc = K.nc
    full, free = K.products, K.counter("linear_free")
    g0 = K.used
    tiles = -(-n_chunks // per_tile)
    banks = 4
    with K.stage() as st:
        ps = K.ps("linear_ps", [P, banks, 512], st)
        pe_steps, act_steps, programs = beside(st) if beside else ({}, {}, None)
        block = st.enter_context(nc.Block())
        if programs:
            programs(block)

        @block.tensor
        def _(pe):
            q = 0
            for t in range(tiles):
                if t in pe_steps:
                    pe_steps[t](pe)
                w = K.tile(pe, g0 + t, kc)
                tok = t in token_major
                for j in range(TT if tok else min(per_tile, n_chunks - t * per_tile)):
                    if q >= banks:
                        pe.wait_ge(free.sem, free.at(q - banks + 1))
                    for k in range(kc):
                        if tok:
                            mm = pe.matmul(ps[:, q % banks, 0:512], src[:, k, j * P:(j + 1) * P], w[:, k, 0:512],
                                           start=k == 0, stop=k == kc - 1)
                        else:
                            mm = pe.matmul(ps[:, q % banks, 0:n], w[:, k, j * P:(j + 1) * P], src[:, k, 0:n],
                                           start=k == 0, stop=k == kc - 1)
                    mm.then_inc(full.sem, full.tick())
                    q += 1
                K.done_at[g0 + t] = full.count

        @block.scalar
        def _(act):
            q = 0
            for t in range(tiles):
                if t in act_steps:
                    act_steps[t](act)
                for j in range(TT if t in token_major else min(per_tile, n_chunks - t * per_tile)):
                    act.wait_ge(full.sem, full.at(q + 1))
                    evac(act, t, j, ps[:, q % banks, 0:512 if t in token_major else n]).then_inc(free.sem, free.tick())
                    q += 1
        @block.sync
        def _(sp):
            K.issue(sp, g0 + tiles + RING)
    K.used = g0 + tiles


def stage_stick_breaking(K, qT, kT, v, oT):
    nc = K.nc
    W = T + P
    pairs = SB_HEADS // 2
    names = ("sb_scores", "sb_scaled", "sb_size", "sb_soft", "sb_masked", "sb_sums", "sb_arg", "sb_weights", "sb_causal", "sb_mixed", "sb_out")
    scores, scaled, size, soft, masked, sums, arg, weights, causal, mixed, stored = (K.counter(x) for x in names)
    with K.stage() as st:
        zs = K.sb("sb_zs", [P, 2, 2, W], ctx=st)
        ab = K.sb("sb_ab", [P, 2, 2, W], ctx=st)
        sp_ = K.sb("sb_sp", [P, 2, 2, W], ctx=st)
        t1 = K.sb("sb_t1", [P, 2, 2, W], ctx=st)
        w = K.sb("sb_w", [P, 2, 2, W], ctx=st)
        z_ps = K.ps("sb_z", [P, 2, 512], st)
        r_ps = K.ps("sb_r", [P, 2, 512], st)
        o_ps = K.ps("sb_o", [P, 2, 512], st)
        block = st.enter_context(nc.Block())

        def causal_parts(t, b):
            return t[:, b, :, 0:P], t[:, b, :, T:W]

        @block.tensor
        def _(pe):
            def make_scores(i):
                if i >= 1:
                    pe.wait_ge(scaled.sem, scaled.at(i))
                for h in range(2):
                    r = slice(SB_DIM * h, SB_DIM * h + SB_DIM)
                    pe.matmul(z_ps[:, h, 0:T], kT[r, i, 0:P], qT[r, i, 0:T], start=True, stop=True)
                    mm = pe.matmul(z_ps[:, h, T:W], kT[r, i, P:T], qT[r, i, P:T], start=True, stop=True)
                mm.then_inc(scores.sem, scores.tick())

            make_scores(0)
            for i in range(pairs):
                pe.wait_ge(masked.sem, masked.at(2 * (i + 1)))
                if i >= 1:
                    pe.wait_ge(arg.sem, arg.at(i))
                for h in range(2):
                    pe.matmul(r_ps[:, h, 0:W], K.after[:, :], sp_[:, i % 2, h, 0:W], start=True, stop=False)
                    mm = pe.matmul(r_ps[:, h, P:T], K.ones[:, :], sp_[:, i % 2, h, T:W], start=False, stop=True)
                mm.then_inc(sums.sem, sums.tick())
                if i + 1 < pairs:
                    make_scores(i + 1)
                pe.wait_ge(causal.sem, causal.at(2 * (i + 1)))
                if i >= 2:
                    pe.wait_ge(stored.sem, stored.at(i - 1))
                for h in range(2):
                    cols = slice(i * P + SB_DIM * h, i * P + SB_DIM * (h + 1))
                    o = o_ps[SB_DIM * h:SB_DIM * (h + 1), i % 2, :]
                    pe.matmul(o[:, 0:T], v[:, 0, cols], w[:, i % 2, h, 0:T], start=True, stop=False)
                    mm = pe.matmul(o[:, P:T], v[:, 1, cols], w[:, i % 2, h, T:W], start=False, stop=True)
                mm.then_inc(mixed.sem, mixed.tick())

        @block.scalar
        def _(act):
            own = K.own["act"]

            def softplus_part(i):
                b = i % 2
                act.wait_ge(scores.sem, scores.at(i + 1))
                if i >= 2:
                    act.wait_ge(arg.sem, arg.at(i - 1))
                act.activation(zs[:, b], z_ps[:, :, 0:W], ACT.Copy, scale=SB_DIM ** -0.5).then_inc(scaled.sem, scaled.tick())
                act.wait_ge(scaled.sem, scaled.at(i + 1))
                act.activation(ab[:, b], zs[:, b], ACT.Abs).then_inc(own.sem, own.tick())
                act.wait_ge(own.sem, own.count)
                act.activation(ab[:, b], ab[:, b], ACT.Exp, scale=-1.0).then_inc(own.sem, own.tick())
                act.wait_ge(own.sem, own.count)
                act.activation(ab[:, b], ab[:, b], ACT.Ln, bias=1.0).then_inc(size.sem, size.tick())

            softplus_part(0)
            for i in range(pairs):
                b = i % 2
                if i + 1 < pairs:
                    softplus_part(i + 1)
                act.wait_ge(arg.sem, arg.at(i + 1))
                if i >= 2:
                    act.wait_ge(mixed.sem, mixed.at(i - 1))
                act.activation(w[:, b], t1[:, b], ACT.Exp).then_inc(weights.sem, weights.tick())

        @block.gpsimd
        def _(pool):
            def mask_softplus(i):
                pool.wait_ge(soft.sem, soft.at(i + 1))
                for part in causal_parts(sp_, i % 2):
                    pool.affine_select(out=part, in_=part, compare_op=ALU.is_gt, fill=0.0, base=0,
                                       pattern=[[0, 2], [1, P]], channel_multiplier=-1).then_inc(masked.sem, masked.tick())

            mask_softplus(0)
            for i in range(pairs):
                pool.wait_ge(weights.sem, weights.at(i + 1))
                for part in causal_parts(w, i % 2):
                    pool.affine_select(out=part, in_=part, compare_op=ALU.is_gt, fill=0.0, base=0,
                                       pattern=[[0, 2], [1, P]], channel_multiplier=-1).then_inc(causal.sem, causal.tick())
                if i + 1 < pairs:
                    mask_softplus(i + 1)

        @block.vector
        def _(dve):
            own = K.own["dve"]

            def softplus(i):
                b = i % 2
                dve.wait_ge(size.sem, size.at(i + 1))
                if i >= 2:
                    dve.wait_ge(sums.sem, sums.at(i - 1))
                dve.scalar_tensor_tensor(out=sp_[:, b], in0=zs[:, b], scalar=0.0, in1=ab[:, b],
                                                 op0=ALU.max, op1=ALU.add).then_inc(soft.sem, soft.tick())

            softplus(0)
            for i in range(pairs):
                b = i % 2
                dve.wait_ge(masked.sem, masked.at(2 * (i + 1)))
                dve.tensor_tensor(t1[:, b], zs[:, b], sp_[:, b], ALU.subtract).then_inc(own.sem, own.tick())
                dve.wait_ge(own.sem, own.count)
                dve.wait_ge(sums.sem, sums.at(i + 1))
                dve.tensor_tensor(t1[:, b], t1[:, b], r_ps[:, :, 0:W], ALU.subtract).then_inc(arg.sem, arg.tick())
                if i + 1 < pairs:
                    softplus(i + 1)
                dve.wait_ge(mixed.sem, mixed.at(i + 1))
                dve.tensor_copy(oT[:, i, :], o_ps[:, i % 2, 0:T]).then_inc(stored.sem, stored.tick())


def exact_exp(K, dve, out, x, k, r, two_k):
    own = K.own["dve"]
    dve.tensor_scalar(k, x, 1.4426950408889634, ROUND, ALU.mult, ALU.add).then_inc(own.sem, own.tick())
    dve.wait_ge(own.sem, own.count)
    dve.tensor_scalar(k, k, -ROUND, -126.0, ALU.add, ALU.max).then_inc(own.sem, own.tick())
    dve.wait_ge(own.sem, own.count)
    dve.tensor_scalar(k, k, 127.0, None, ALU.min).then_inc(own.sem, own.tick())
    dve.wait_ge(own.sem, own.count)
    dve.scalar_tensor_tensor(out=r, in0=k, scalar=-0.693359375, in1=x, op0=ALU.mult, op1=ALU.add).then_inc(own.sem, own.tick())
    dve.wait_ge(own.sem, own.count)
    dve.scalar_tensor_tensor(out=r, in0=k, scalar=2.12194440e-4, in1=r, op0=ALU.mult, op1=ALU.add).then_inc(own.sem, own.tick())
    dve.wait_ge(own.sem, own.count)
    dve.tensor_scalar(out, r, 1.0 / 5040, 1.0 / 720, ALU.mult, ALU.add).then_inc(own.sem, own.tick())
    dve.wait_ge(own.sem, own.count)
    for c in (1.0 / 120, 1.0 / 24, 1.0 / 6, 0.5, 1.0, 1.0):
        dve.tensor_tensor(out, out, r, ALU.mult).then_inc(own.sem, own.tick())
        dve.wait_ge(own.sem, own.count)
        dve.tensor_scalar(out, out, c, None, ALU.add).then_inc(own.sem, own.tick())
        dve.wait_ge(own.sem, own.count)
    dve.tensor_scalar(two_k, k, 127.0, 8388608.0, ALU.add, ALU.mult).then_inc(own.sem, own.tick())
    dve.wait_ge(own.sem, own.count)
    dve.tensor_tensor(out, out, two_k.bitcast(F32), ALU.mult).then_inc(own.sem, own.tick())
    dve.wait_ge(own.sem, own.count)


def ssm_params(K, S, st):
    io = K.io
    loads = K.counter("ssm_loads", 16)
    made, turned, moved, angle, waved = (K.counter(x) for x in ("ssm_made", "ssm_turned", "ssm_moved", "ssm_angle", "ssm_waved"))
    pool_made = K.counter("ssm_pool_made")
    ld = K.sb("ssm_ld", [ST, 2], ctx=st)
    ldr = K.sb("ssm_ldr", [ST, P], ctx=st)
    rot = K.sb("ssm_rot", [P, ST, T], ctx=st)
    br, bb, bx = (K.sb("ssm_" + n, [P, 2, ST] + m, ctx=st) for n, m in (("br", [SSM_C]), ("bb", [SSM_C]), ("bx", [2, SSM_C])))
    cr, cx = K.sb("ssm_cr", [P, 2, 4, SSM_S], ctx=st), K.sb("ssm_cx", [P, 2, 4, 2, SSM_S], ctx=st)
    half = K.sb("ssm_half", [P, 4], ctx=st)
    s = K.sb("ssm_small", [P, 20, ST], ctx=st)
    ints = K.sb("ssm_ints", [P, ST], I32, ctx=st)
    tm = K.sb("ssm_time", [P, T], ctx=st)
    ps = K.ps("ssm_ps", [P, 3, 512], st)
    are, aim = (K.params[:, K.cols[n]:K.cols[n] + ST] for n in ("ssm_a_re", "ssm_a_im"))
    DT, RE, IM, ER, CO, SI, LR, LI, DEN, KR, KI, PH, T0, T1, T2, PC = range(16)
    v = lambda i: s[:, i, :]

    def first_turns(pe):
        pe.wait_ge(made.sem, made.at(1))
        pe.transpose(ps[:, 0, 0:ST], ldr[:, :], K.ident[0:ST, 0:ST]).then_inc(turned.sem, turned.tick())
        pe.wait_ge(pool_made.sem, pool_made.at(6))
        for j in range(2):
            for b in range(4):
                mm = pe.transpose(ps[:, 1 + j, b * P:(b + 1) * P], cx[:, j, b].rearrange("p h s -> p (h s)"), K.ident[:, :])
        mm.then_inc(turned.sem, turned.tick())

    def turn_b(pe):
        pe.wait_ge(made.sem, made.at(3))
        pe.wait_ge(moved.sem, moved.at(3))
        for j in range(2):
            for b in range(4):
                mm = pe.transpose(ps[:, 1 + j, b * P:(b + 1) * P],
                                  bx[:, j, 4 * b:4 * b + 4].rearrange("p i h c -> p (i h c)"), K.ident[:, :])
        mm.then_inc(turned.sem, turned.tick())

    turn = 6.283185

    def angles(act):
        act.wait_ge(made.sem, made.at(2))
        act.activation(v(CO), v(PC), ACT.Sin, scale=turn).then_inc(angle.sem, angle.tick())
        act.activation(v(SI), v(PH), ACT.Sin, scale=turn).then_inc(angle.sem, angle.tick())

    def sines(act):
        act.wait_ge(made.sem, made.at(4))
        act.activation(S["sin"][:, :, :], rot[:, :, :], ACT.Sin, scale=turn).then_inc(waved.sem, waved.tick())

    def cosines(act):
        act.wait_ge(made.sem, made.at(5))
        act.activation(S["cos"][:, :, :], rot[:, :, :], ACT.Sin, scale=turn).then_inc(waved.sem, waved.tick())

    def programs(block):
        @block.gpsimd
        def _(pool):
            own = K.own["pool"]
            pool.dma_start(ld[:, :], io["ssm_log_dt"][0].rearrange("(i h) -> i h", h=2)).then_inc(loads.sem, loads.tick())
            for j, n in enumerate(("ssm_b_re", "ssm_b_im")):
                pool.dma_start(br[:, j], io[n][0].rearrange("g s c -> (g s) c").rearrange("(i q) c -> q i c", q=P)).then_inc(loads.sem, loads.tick())
            for j, n in enumerate(("ssm_c_re", "ssm_c_im")):
                pool.dma_start(cr[:, j], io[n][0].rearrange("g c s -> (g c) s").rearrange("(b r) s -> r b s", r=P)).then_inc(loads.sem, loads.tick())
            pool.iota(tm[:, :], pattern=[[1, T]], base=0, channel_multiplier=0,
                                   allow_small_or_imprecise_dtypes=True).then_inc(pool_made.sem, pool_made.tick())
            pool.memset(bx[:, :, :, :, :], 0.0).then_inc(pool_made.sem, pool_made.tick())
            pool.iota(half[:, 2:3], pattern=[[0, 1]], base=0, channel_multiplier=1,
                                allow_small_or_imprecise_dtypes=True).then_inc(own.sem, own.tick())
            pool.wait_ge(own.sem, own.count)
            pool.tensor_scalar(half[:, 3:4], half[:, 2:3], 1.0 / 16, -15.0 / 32, ALU.mult, ALU.add).then_inc(own.sem, own.tick())
            pool.wait_ge(own.sem, own.count)
            pool.tensor_scalar(half[:, 3:4], half[:, 3:4], ROUND, -ROUND, ALU.add, ALU.add).then_inc(own.sem, own.tick())
            pool.wait_ge(own.sem, own.count)
            pool.tensor_scalar(half[:, 2:3], half[:, 3:4], 0.5, -0.25, ALU.mult, ALU.add).then_inc(own.sem, own.tick())
            pool.wait_ge(own.sem, own.count)
            pool.tensor_scalar(half[:, 2:3], half[:, 2:3], ROUND, -ROUND, ALU.add, ALU.add).then_inc(own.sem, own.tick())
            pool.wait_ge(own.sem, own.count)
            pool.tensor_scalar(half[:, 2:3], half[:, 2:3], -2.0, None, ALU.mult).then_inc(own.sem, own.tick())
            pool.wait_ge(own.sem, own.count)
            pool.tensor_tensor(half[:, 1:2], half[:, 3:4], half[:, 2:3], ALU.add).then_inc(own.sem, own.tick())
            pool.wait_ge(own.sem, own.count)
            pool.tensor_scalar(half[:, 0:1], half[:, 1:2], -1.0, 1.0, ALU.mult, ALU.add).then_inc(own.sem, own.tick())
            pool.wait_ge(own.sem, own.count)
            pool.tensor_scalar(half[:, 2:4], half[:, 0:2], -1.0, None, ALU.mult).then_inc(own.sem, own.tick())
            pool.wait_ge(own.sem, own.count)
            pool.wait_ge(loads.sem, loads.at(5))
            for j in range(2):
                for h in range(2):
                    pool.tensor_scalar(cx[:, j, :, h, :], cr[:, j, :, :], half[:, 2 * j + h:2 * j + h + 1], None, ALU.mult).then_inc(pool_made.sem, pool_made.tick())


        @block.vector
        def _(dve):
            own = K.own["dve"]
            tt, ts = dve.tensor_tensor, dve.tensor_scalar
            dve.wait_ge(loads.sem, loads.at(5))
            dve.tensor_copy(ldr[:, :].rearrange("p (h s) -> p h s", h=2), ld[:, :].unsqueeze(2).broadcast_to([ST, 2, SSM_S])).then_inc(made.sem, made.tick())
            dve.wait_ge(turned.sem, turned.at(1))
            dve.tensor_copy(v(T0), ps[:, 0, 0:ST]).then_inc(moved.sem, moved.tick())
            dve.wait_ge(moved.sem, moved.at(1))
            exact_exp(K, dve, v(DT), v(T0), v(T1), v(T2), ints[:, :])
            dve.wait_ge(turned.sem, turned.at(2))
            for j in range(2):
                dve.tensor_copy(S["cT"][:, j], ps[:, 1 + j, :].rearrange("p (b c) -> p b c", b=4)).then_inc(moved.sem, moved.tick())
            dve.tensor_scalar(S["cT"][:, 2], ps[:, 1, :].rearrange("p (b c) -> p b c", b=4), -1.0, None, ALU.mult)
            tt(v(RE), are, v(DT), ALU.mult).then_inc(own.sem, own.tick())
            dve.wait_ge(own.sem, own.count)
            tt(v(IM), aim, v(DT), ALU.mult).then_inc(own.sem, own.tick())
            dve.wait_ge(own.sem, own.count)
            ts(v(PH), v(IM), 1.0 / (2 * PI), None, ALU.mult).then_inc(own.sem, own.tick())
            dve.wait_ge(own.sem, own.count)
            ts(v(T0), v(PH), ROUND, -ROUND, ALU.add, ALU.add).then_inc(own.sem, own.tick())
            dve.wait_ge(own.sem, own.count)
            tt(v(PH), v(PH), v(T0), ALU.subtract).then_inc(own.sem, own.tick())
            dve.wait_ge(own.sem, own.count)
            ts(v(PC), v(PH), 0.25, None, ALU.add).then_inc(own.sem, own.tick())
            dve.wait_ge(own.sem, own.count)
            ts(v(T0), v(PC), ROUND, -ROUND, ALU.add, ALU.add).then_inc(own.sem, own.tick())
            dve.wait_ge(own.sem, own.count)
            tt(v(PC), v(PC), v(T0), ALU.subtract).then_inc(made.sem, made.tick())
            exact_exp(K, dve, v(ER), v(RE), v(T1), v(T2), ints[:, :])
            dve.tensor_copy(S["r"][:, :], v(ER)).then_inc(own.sem, own.tick())
            dve.wait_ge(own.sem, own.count)
            dve.wait_ge(angle.sem, angle.at(2))
            tt(v(LR), v(ER), v(CO), ALU.mult).then_inc(own.sem, own.tick())
            dve.wait_ge(own.sem, own.count)
            tt(v(LI), v(ER), v(SI), ALU.mult).then_inc(own.sem, own.tick())
            dve.wait_ge(own.sem, own.count)
            ts(v(LR), v(LR), -1.0, None, ALU.add).then_inc(own.sem, own.tick())
            dve.wait_ge(own.sem, own.count)
            tt(v(DEN), are, are, ALU.mult).then_inc(own.sem, own.tick())
            dve.wait_ge(own.sem, own.count)
            tt(v(T0), aim, aim, ALU.mult).then_inc(own.sem, own.tick())
            dve.wait_ge(own.sem, own.count)
            tt(v(DEN), v(DEN), v(T0), ALU.add).then_inc(own.sem, own.tick())
            dve.wait_ge(own.sem, own.count)
            dve.reciprocal(v(DEN), v(DEN)).then_inc(own.sem, own.tick())
            dve.wait_ge(own.sem, own.count)
            tt(v(T0), v(LR), are, ALU.mult).then_inc(own.sem, own.tick())
            dve.wait_ge(own.sem, own.count)
            tt(v(T1), v(LI), aim, ALU.mult).then_inc(own.sem, own.tick())
            dve.wait_ge(own.sem, own.count)
            tt(v(KR), v(T0), v(T1), ALU.add).then_inc(own.sem, own.tick())
            dve.wait_ge(own.sem, own.count)
            tt(v(T0), v(LI), are, ALU.mult).then_inc(own.sem, own.tick())
            dve.wait_ge(own.sem, own.count)
            tt(v(T1), v(LR), aim, ALU.mult).then_inc(own.sem, own.tick())
            dve.wait_ge(own.sem, own.count)
            tt(v(KI), v(T0), v(T1), ALU.subtract).then_inc(own.sem, own.tick())
            dve.wait_ge(own.sem, own.count)
            tt(v(KR), v(KR), v(DEN), ALU.mult).then_inc(own.sem, own.tick())
            dve.wait_ge(own.sem, own.count)
            tt(v(KI), v(KI), v(DEN), ALU.mult).then_inc(own.sem, own.tick())
            dve.wait_ge(own.sem, own.count)
            wide = lambda i: v(i).unsqueeze(2).broadcast_to([P, ST, SSM_C])
            tt(bb[:, 0], br[:, 0], wide(KR), ALU.mult).then_inc(own.sem, own.tick())
            dve.wait_ge(own.sem, own.count)
            tt(bb[:, 1], br[:, 0], wide(KI), ALU.mult).then_inc(own.sem, own.tick())
            dve.wait_ge(own.sem, own.count)
            tt(br[:, 0], br[:, 1], wide(KI), ALU.mult).then_inc(own.sem, own.tick())
            dve.wait_ge(own.sem, own.count)
            tt(br[:, 1], br[:, 1], wide(KR), ALU.mult).then_inc(own.sem, own.tick())
            dve.wait_ge(own.sem, own.count)
            dve.wait_ge(pool_made.sem, pool_made.at(2))
            for h in range(2):
                r = slice(64 * h, 64 * h + 64)
                tt(bx[r, 0, :, h, :], bb[r, 0], br[r, 0], ALU.subtract).then_inc(own.sem, own.tick())
                dve.wait_ge(own.sem, own.count)
                ins = tt(bx[r, 1, :, h, :], bb[r, 1], br[r, 1], ALU.add)
                if h == 0:
                    ins.then_inc(own.sem, own.tick())
                    dve.wait_ge(own.sem, own.count)
            ins.then_inc(made.sem, made.tick())
            dve.wait_ge(turned.sem, turned.at(3))
            for j in range(2):
                dve.tensor_copy(S["bT"][:, j], ps[:, 1 + j, :].rearrange("p (b c) -> p b c", b=4)).then_inc(moved.sem, moved.tick())
            for which, dst in enumerate((S["sin"], S["cos"])):
                for i in range(ST):
                    ins = ts(dst[:, i, :], tm[:, :], s[:, PH, i:i + 1], None, ALU.mult)
                ins.then_inc(own.sem, own.tick())
                dve.wait_ge(own.sem, own.count)
                if which:
                    dve.wait_ge(waved.sem, waved.at(1))
                ts(rot[:, :, :], dst[:, :, :], ROUND, -ROUND, ALU.add, ALU.add).then_inc(own.sem, own.tick())
                dve.wait_ge(own.sem, own.count)
                if which == 0:
                    tt(rot[:, :, :], dst[:, :, :], rot[:, :, :], ALU.subtract).then_inc(made.sem, made.tick())
                else:
                    tt(dst[:, :, :], dst[:, :, :], rot[:, :, :], ALU.subtract).then_inc(own.sem, own.tick())
                    dve.wait_ge(own.sem, own.count)
                    ts(dst[:, :, :], dst[:, :, :], 0.25, None, ALU.add).then_inc(own.sem, own.tick())
                    dve.wait_ge(own.sem, own.count)
                    ts(rot[:, :, :], dst[:, :, :], ROUND, -ROUND, ALU.add, ALU.add).then_inc(own.sem, own.tick())
                    dve.wait_ge(own.sem, own.count)
                    tt(rot[:, :, :], dst[:, :, :], rot[:, :, :], ALU.subtract).then_inc(made.sem, made.tick())

    return {1: first_turns, 4: turn_b}, {2: angles, 5: sines, 7: cosines}, programs


def stage_ssm_scan(K, S, uT, yT):
    nc = K.nc
    drive, spun, scanned, back, y_full, y_skip, y_out, spread = (K.counter(x) for x in
        ("ssm_drive", "ssm_spun", "ssm_scanned", "ssm_back", "ssm_y_full", "ssm_y_skip", "ssm_y_out", "ssm_spread"))
    with K.stage() as st:
        pr = K.sb("ssm_pr", [P, 2, 2, 2, T], ctx=st)
        z = K.sb("ssm_z", [P, 2, 2, T], ctx=st)
        pz = K.sb("ssm_pz", [P, 2, 2, 2, T], ctx=st)
        zz = K.hT[:, 0:4, :].rearrange("p (b j) t -> p b j t", b=2)
        rr = K.hT[:, 4:6, :]
        bu = K.ps("ssm_bu", [P, 4, 512], st)
        yp = K.ps("ssm_yp", [P, 2, 512], st)
        block = st.enter_context(nc.Block())

        @block.tensor
        def _(pe):
            def make_drive(i):
                if i >= 4:
                    pe.wait_ge(spun.sem, spun.at(i - 3))
                r = slice(32 * (i % 4), 32 * (i % 4) + 32)
                for j in range(2):
                    mm = pe.matmul(bu[:, i % 4, j * T:(j + 1) * T], S["bT"][r, j, i // 4, :], uT[r, i // 4, :],
                                   start=True, stop=True, tile_position=(32 * (i % 4), 0))
                mm.then_inc(drive.sem, drive.tick())

            make_drive(0)
            make_drive(1)
            for i in range(ST):
                if i + 2 < ST:
                    make_drive(i + 2)
                pe.wait_ge(back.sem, back.at(i + 1))
                if i % 4 == 0 and i >= 8:
                    pe.wait_ge(y_skip.sem, y_skip.at(i // 4 - 1))
                r = slice(32 * (i % 4), 32 * (i % 4) + 32)
                o = yp[r, (i // 4) % 2, 0:T]
                for n, (c, a, j) in enumerate(((0, 0, 0), (2, 1, 1), (1, 1, 0), (1, 0, 1))):
                    mm = pe.matmul(o, S["cT"][:, c, i // 4, r], pz[:, i % 2, a, j, :], start=n == 0, stop=n == 3,
                                   tile_position=(0, 32 * (i % 4)))
                mm.then_inc(y_full.sem, y_full.tick())

        @block.vector
        def _(dve):
            own = K.own["dve"]
            tt = dve.tensor_tensor
            pair = lambda t, i: t[:, i, :].unsqueeze(1).broadcast_to([P, 2, T])

            def turn_drive(i):
                dve.wait_ge(drive.sem, drive.at(i + 1))
                part = bu[:, i % 4, :].rearrange("p (j t) -> p j t", j=2)
                tt(pr[:, i % 2, 0], part, pair(S["cos"], i), ALU.mult)
                tt(pr[:, i % 2, 1], part, pair(S["sin"], i), ALU.mult).then_inc(spun.sem, spun.tick())

            def skip(c):
                dve.wait_ge(y_full.sem, y_full.at(4 * c + 4))
                dve.scalar_tensor_tensor(out=yT[:, c, :], in0=uT[:, c, :], scalar=K.col("ssm_d", c),
                                         in1=yp[:, c % 2, 0:T], op0=ALU.mult, op1=ALU.add).then_inc(y_skip.sem, y_skip.tick())

            turn_drive(0)
            for i in range(ST):
                b = i % 2
                dve.wait_ge(spun.sem, spun.at(i + 1))
                if i >= 2:
                    dve.wait_ge(scanned.sem, scanned.at(i - 1))
                tt(z[:, b, 0, :], pr[:, b, 0, 0, :], pr[:, b, 1, 1, :], ALU.add)
                tt(z[:, b, 1, :], pr[:, b, 0, 1, :], pr[:, b, 1, 0, :], ALU.subtract).then_inc(own.sem, own.tick())
                if i + 1 < ST:
                    turn_drive(i + 1)
                dve.wait_ge(own.sem, own.count)
                if i >= 2:
                    dve.wait_ge(back.sem, back.at(i - 1))
                dve.wait_ge(spread.sem, spread.at(i + 1))
                for j in range(2):
                    ins = dve.tensor_tensor_scan(out=zz[:, b, j, :], data0=rr[:, b, :], data1=z[:, b, j, :],
                                                 initial=0.0, op0=ALU.mult, op1=ALU.add)
                ins.then_inc(scanned.sem, scanned.tick())
                if i % 4 == 1 and i > 4:
                    skip(i // 4 - 1)
            skip(ST // 4 - 1)

        @block.gpsimd
        def _(pool):
            tt = pool.tensor_tensor
            for i in range(ST):
                b = i % 2
                pair = lambda t: t[:, i, :].unsqueeze(1).broadcast_to([P, 2, T])
                if i >= 2:
                    pool.wait_ge(y_full.sem, y_full.at(i - 1))
                pool.wait_ge(scanned.sem, scanned.at(i + 1))
                tt(pz[:, b, 0], zz[:, b], pair(S["cos"]), ALU.mult)
                tt(pz[:, b, 1], zz[:, b], pair(S["sin"]), ALU.mult).then_inc(back.sem, back.tick())

        @block.scalar
        def _(act):
            for i in range(ST):
                if i >= 2:
                    act.wait_ge(scanned.sem, scanned.at(i - 1))
                act.activation(rr[:, i % 2, :], S["cos"][:, i, :], ACT.Identity, scale=0.0, bias=S["r"][:, i:i + 1]).then_inc(spread.sem, spread.tick())
            for c in range(4):
                act.wait_ge(y_skip.sem, y_skip.at(c + 1))
                act.activation(yT[:, c, :], yT[:, c, :], ACT.Gelu_apprx_tanh).then_inc(y_out.sem, y_out.tick())


def stage_glu(K, yT, oT):
    gated = K.counter("glu_gated")
    sig = K.sb("glu_sig", [P, 4, T], ctx=K.part)
    free = K.counter("linear_free")

    def evac(act, t, j, ps):
        return act.activation(sig[:, j, :], ps, ACT.Sigmoid, bias=K.col("ssm_b_glu", j))

    def programs(block):
        @block.vector
        def _(dve):
            for j in range(4):
                dve.wait_ge(free.sem, free.at(j + 1))
                dve.tensor_tensor(oT[:, j, :], yT[:, j, :], sig[:, j, :], ALU.mult).then_inc(gated.sem, gated.tick())

    linear_stage(K, yT, 4, evac, kc=4, beside=lambda st: ({}, {}, programs))


def stage_merge(K, o_attn, o_ssm, gates, dst):
    nc = K.nc
    full, took = K.products, K.counter("merge_took")
    g0 = K.used
    with K.stage() as st:
        tmp = K.sb("merge_tmp", [P, 2, 2, T], ctx=st)
        ps = K.ps("merge_ps", [P, 4, 512], st)
        block = st.enter_context(nc.Block())

        @block.tensor
        def _(pe):
            wa = K.tile(pe, g0, 4)
            ws = K.tile(pe, g0 + 1, 4)
            for c in range(KC):
                if c >= 4:
                    pe.wait_ge(took.sem, took.at(c - 3))
                for j, (w, o) in enumerate(((wa, o_attn), (ws, o_ssm))):
                    for k in range(4):
                        mm = pe.matmul(ps[:, c % 4, j * T:(j + 1) * T], w[:, k, c * P:(c + 1) * P], o[:, k, :],
                                       start=k == 0, stop=k == 3)
                mm.then_inc(full.sem, full.tick())
            K.done_at[g0] = K.done_at[g0 + 1] = full.count

        @block.vector
        def _(dve):
            own = K.own["dve"]
            for c in range(KC):
                dve.wait_ge(full.sem, full.at(c + 1))
                dve.tensor_tensor(tmp[:, c % 2, :, :], ps[:, c % 4, :].rearrange("p (j t) -> p j t", j=2),
                                          gates[:, c:c + KC + 1:KC, :], ALU.mult).then_inc(took.sem, took.tick())
                dve.wait_ge(took.sem, took.at(c + 1))
                dve.tensor_tensor(dst[:, c, :], tmp[:, c % 2, 0, :], tmp[:, c % 2, 1, :], ALU.add)

        @block.sync
        def _(sp):
            K.issue(sp, g0 + 2 + RING)
    K.used = g0 + 2


def stage_cross(K, qT, kT, v, oT):
    nc = K.nc
    dim = D // XA_HEADS
    hc = dim // P
    steps = XA_HEADS * TT
    scores, peak, probs, normed, turned, moved, mixed, stored = (K.counter(x) for x in (
        "xa_scores", "xa_peak", "xa_probs", "xa_normed", "xa_turned", "xa_moved", "xa_mixed", "xa_stored"))
    with K.stage() as st:
        p = K.sb("xa_p", [P, 2, T], ctx=st)
        pT = K.sb("xa_pT", [P, 2, TT, T], ctx=st)
        nm = K.sb("xa_nm", [P, steps], ctx=st)
        sm = K.sb("xa_sm", [P, steps], ctx=st)
        s_ps = K.ps("xa_s", [P, 2, 512], st)
        t_ps = K.ps("xa_t", [P, 2, 512], st)
        o_ps = K.ps("xa_o", [P, 2, 512], st)
        block = st.enter_context(nc.Block())

        @block.tensor
        def _(pe):
            def make_scores(i):
                h, a = divmod(i, TT)
                if i >= 2:
                    pe.wait_ge(probs.sem, probs.at(i - 1))
                for k in range(hc):
                    mm = pe.matmul(s_ps[:, i % 2, 0:T], qT[:, h * hc + k, a * P:(a + 1) * P], kT[:, h * hc + k, :],
                                   start=k == 0, stop=k == hc - 1)
                mm.then_inc(scores.sem, scores.tick())

            make_scores(0)
            for i in range(steps):
                h, a = divmod(i, TT)
                if i + 1 < steps:
                    make_scores(i + 1)
                pe.wait_ge(normed.sem, normed.at(i + 1))
                if i >= 2:
                    pe.wait_ge(moved.sem, moved.at(i - 1))
                for m in range(TT):
                    mm = pe.transpose(t_ps[:, i % 2, m * P:(m + 1) * P], p[:, i % 2, m * P:(m + 1) * P], K.ident[:, :])
                mm.then_inc(turned.sem, turned.tick())
                if a == TT - 1:
                    pe.wait_ge(moved.sem, moved.at(i + 1))
                    if h >= 2:
                        pe.wait_ge(stored.sem, stored.at(h - 1))
                    for c in range(hc):
                        for m in range(TT):
                            cc = (h * hc + c) * P
                            mm = pe.matmul(o_ps[:, h % 2, c * T:(c + 1) * T], v[:, m, cc:cc + P], pT[:, h % 2, m, :],
                                           start=m == 0, stop=m == TT - 1)
                    mm.then_inc(mixed.sem, mixed.tick())

        @block.vector
        def _(dve):
            own = K.own["dve"]
            for i in range(steps):
                h, a = divmod(i, TT)
                dve.wait_ge(scores.sem, scores.at(i + 1))
                dve.tensor_reduce(nm[:, i:i + 1], s_ps[:, i % 2, 0:T], AX.X, ALU.max).then_inc(own.sem, own.tick())
                dve.wait_ge(own.sem, own.count)
                dve.tensor_scalar(nm[:, i:i + 1], nm[:, i:i + 1], -dim ** -0.5, None, ALU.mult).then_inc(peak.sem, peak.tick())
                dve.wait_ge(probs.sem, probs.at(i + 1))
                dve.reciprocal(sm[:, i:i + 1], sm[:, i:i + 1]).then_inc(own.sem, own.tick())
                dve.wait_ge(own.sem, own.count)
                dve.tensor_scalar(p[:, i % 2, :], p[:, i % 2, :], sm[:, i:i + 1], None, ALU.mult).then_inc(normed.sem, normed.tick())
                if a == TT - 1:
                    dve.wait_ge(mixed.sem, mixed.at(h + 1))
                    dve.tensor_copy(oT[:, h * hc:(h + 1) * hc, :],
                                              o_ps[:, h % 2, :].rearrange("p (c t) -> p c t", c=hc)).then_inc(stored.sem, stored.tick())

        @block.scalar
        def _(act):
            for i in range(steps):
                h, a = divmod(i, TT)
                act.wait_ge(peak.sem, peak.at(i + 1))
                if i >= 2:
                    act.wait_ge(turned.sem, turned.at(i - 1))
                act.activation(p[:, i % 2, :], s_ps[:, i % 2, 0:T], ACT.Exp, bias=nm[:, i:i + 1],
                                        scale=dim ** -0.5, accum_out=sm[:, i:i + 1]).then_inc(probs.sem, probs.tick())
                act.wait_ge(turned.sem, turned.at(i + 1))
                if h >= 2 and a == 0:
                    act.wait_ge(mixed.sem, mixed.at(h - 1))
                act.activation(pT[:, h % 2, :, a * P:(a + 1) * P],
                                        t_ps[:, i % 2, 0:T].rearrange("p (m q) -> p m q", m=TT), ACT.Copy).then_inc(moved.sem, moved.tick())


def stage_ffn_up(K, src, hid):
    nc = K.nc
    full, base, conved, gelued, made = K.products, K.counter("ffn_base"), K.counter("ffn_conved"), K.counter("ffn_gelued"), K.counter("ffn_made")
    g0, per = K.used, 2
    with K.stage() as st:
        cv = K.sb("ffn_cv", [P, 2, 2, T], ctx=st)
        ps = K.ps("ffn_ps", [P, 4, 512], st)
        block = st.enter_context(nc.Block())

        @block.tensor
        def _(pe):
            for c in range(FC):
                g = g0 + c // per
                if c % per == 0:
                    w = K.tile(pe, g, 2 * KC)
                if c >= 4:
                    pe.wait_ge(conved.sem, conved.at(2 * (c - 3)))
                for j in range(2):
                    for k in range(KC):
                        mm = pe.matmul(ps[:, c % 4, j * T:(j + 1) * T], w[:, j * KC + k, (c % per) * P:(c % per + 1) * P],
                                       src[:, k, :], start=k == 0, stop=k == KC - 1)
                mm.then_inc(full.sem, full.tick())
                K.done_at[g] = full.count

        @block.scalar
        def _(act):
            for c in range(FC):
                act.wait_ge(full.sem, full.at(c + 1))
                if c >= 2:
                    act.wait_ge(made.sem, made.at(c - 1))
                for j in range(2):
                    act.activation(cv[:, c % 2, j, :], ps[:, c % 4, j * T:(j + 1) * T], ACT.Identity,
                                           scale=K.col("ffn_conv_w2", j * FC + c), bias=K.col("ffn_conv_b", j * FC + c)).then_inc(base.sem, base.tick())
                act.wait_ge(conved.sem, conved.at(2 * c + 2))
                act.activation(cv[:, c % 2, 0, :], cv[:, c % 2, 0, :], ACT.Gelu_apprx_tanh).then_inc(gelued.sem, gelued.tick())

        @block.vector
        def _(dve):
            own = K.own["dve"]
            for c in range(FC):
                dve.wait_ge(base.sem, base.at(2 * c + 2))
                for lag in (1, 2):
                    for j in range(2):
                        out = cv[:, c % 2, j, lag:T]
                        ins = dve.scalar_tensor_tensor(out=out, in0=ps[:, c % 4, j * T:(j + 1) * T - lag],
                                                       scalar=K.col(f"ffn_conv_w{2 - lag}", j * FC + c), in1=out,
                                                       op0=ALU.mult, op1=ALU.add)
                        if lag == 1:
                            ins.then_inc(own.sem, own.tick())
                            dve.wait_ge(own.sem, own.count)
                        else:
                            ins.then_inc(conved.sem, conved.tick())

        @block.gpsimd
        def _(pool):
            for c in range(FC):
                pool.wait_ge(gelued.sem, gelued.at(c + 1))
                pool.tensor_tensor(hid[:, c, :], cv[:, c % 2, 0, :], cv[:, c % 2, 1, :], ALU.mult).then_inc(made.sem, made.tick())

        @block.sync
        def _(sp):
            K.issue(sp, g0 + FC // per + RING)
    K.used = g0 + FC // per


def stage_ffn_down(K, hid, dst):
    nc = K.nc
    full, taken = K.products, K.counter("down_taken")
    g0, per = K.used, 4
    tiles = -(-FC // per)
    with K.stage() as st:
        ps = K.ps("down_ps", [P, KC, 512], st)
        block = st.enter_context(nc.Block())

        @block.tensor
        def _(pe):
            for f in range(FC):
                if f % per == 0:
                    w = K.tile(pe, g0 + f // per, min(per, FC - f))
                for c in range(KC):
                    mm = pe.matmul(ps[:, c, 0:T], w[:, f % per, c * P:(c + 1) * P], hid[:, f, :],
                                   start=f == 0, stop=f == FC - 1)
                mm.then_inc(full.sem, full.tick())
                K.done_at[g0 + f // per] = full.count

        @block.scalar
        def _(act):
            act.wait_ge(full.sem, full.at(FC))
            for c in range(KC):
                act.activation(dst[:, c, :], ps[:, c, 0:T], ACT.Copy).then_inc(taken.sem, taken.tick())

        @block.sync
        def _(sp):
            K.issue(sp, g0 + tiles + RING)
    K.used = g0 + tiles


def copy_to(dst):
    return lambda act, t, j, ps: act.activation(dst[:, 4 * t + j, :], ps, ACT.Copy)


def queue_first_block(K):
    io = K.io
    queue_columns(K, io["w_in"][0], 4096)
    queue_columns(K, io["ssm_w_glu"][0], 512)
    for n in ("w_branch_attn", "w_branch_ssm"):
        K.queue((0, (4, D), rows_of(io[n][0], 0, D)))
    queue_columns(K, io["w_out"][0], D)
    for n in ("xa_wk", "xa_wv", "xa_wq", "xa_wo"):
        queue_columns(K, io[n][0], D)
    for c in range(0, FC, 2):
        K.queue((0, (KC, 2 * P), rows_of(io["ffn_w_up"][0], c * P, 2 * P)),
                (2 * P * KC, (KC, 2 * P), rows_of(io["ffn_w_up"][0], D_FF + c * P, 2 * P)))
    for f in range(0, FC, 4):
        n = min(4, FC - f)
        K.queue((0, (n, D), io["ffn_w_down"][0][f * P:(f + n) * P].rearrange("(k p) n -> p k n", p=P)))


def first_block(K):
    gain = lambda name: (lambda c: K.col(name, c))
    with ExitStack() as K.part:
        proj = K.sb("proj", [P, 32, T], ctx=K.part)
        yT = K.sb("ssm_y", [P, 4, T], ctx=K.part)
        v = proj[:, 8:12, :].rearrange("p (a b) t -> p a (b t)", a=TT)
        with ExitStack() as ssm:
            S = {"sin": K.sb("ssm_sin", [P, ST, T], ctx=ssm), "cos": K.sb("ssm_cos", [P, ST, T], ctx=ssm),
                 "bT": K.sb("ssm_bT", [P, 2, 4, P], ctx=ssm), "cT": K.sb("ssm_cT", [P, 3, 4, P], ctx=ssm),
                 "r": K.sb("ssm_r", [P, ST], ctx=ssm)}
            stage_norm(K, K.xT, K.hT, gain("norm_mix_pre"))

            def evac(act, t, j, ps):
                if t == 2:
                    return act.activation(v[:, j, :], ps, ACT.Copy)
                c = 4 * t + j
                if c < 16:
                    return act.activation(proj[:, c, :], ps, ACT.Copy)
                return act.activation(proj[:, c, :], ps, ACT.Sigmoid, bias=K.col("b_gate", c - 16))

            linear_stage(K, K.hT, 32, evac, token_major=(2,), beside=lambda st: ssm_params(K, S, st))
            stage_ssm_scan(K, S, proj[:, 12:16, :], yT)
        o_ssm = K.sb("o_ssm", [P, 4, T], ctx=K.part)
        o_attn = K.sb("o_attn", [P, 4, T], ctx=K.part)
        stage_glu(K, yT, o_ssm)
        stage_stick_breaking(K, proj[:, 0:4, :], proj[:, 4:8, :], v, o_attn)
        stage_merge(K, o_attn, o_ssm, proj[:, 16:32, :], K.hT)
        linear_stage(K, K.hT, KC, copy_to(proj))
        stage_norm(K, proj[:, 0:KC, :], K.xT, gain("norm_mix_post"), residual=K.xT)
    with ExitStack() as K.part:
        memT = K.sb("memT", [P, KC, T], ctx=K.part)
        kT = K.sb("xa_kT", [P, KC, T], ctx=K.part)
        v = K.sb("xa_v", [P, TT, D], ctx=K.part)
        qT = K.sb("xa_qT", [P, KC, T], ctx=K.part)
        turn_rows(K, K.io["mem"][0], memT, "mem")
        stage_norm(K, memT, memT, gain("norm_mem"))
        linear_stage(K, memT, KC, copy_to(kT))
        linear_stage(K, memT, KC, lambda act, t, j, ps: act.activation(v[:, j, t * 512:(t + 1) * 512], ps, ACT.Copy),
                     token_major=(0, 1))
        stage_norm(K, K.xT, K.hT, gain("norm_xa_pre"))
        linear_stage(K, K.hT, KC, copy_to(qT))
        stage_cross(K, qT, kT, v, K.hT)
        linear_stage(K, K.hT, KC, copy_to(qT))
        stage_norm(K, qT, K.xT, gain("norm_xa_post"), residual=K.xT)
    with ExitStack() as K.part:
        hid = K.sb("ffn_hid", [P, FC, T], ctx=K.part)
        stage_norm(K, K.xT, K.hT, gain("norm_ffn_pre"))
        stage_ffn_up(K, K.hT, hid)
        stage_ffn_down(K, hid, K.hT)
        stage_norm(K, K.hT, K.xT, gain("norm_ffn_post"), residual=K.xT)


def stage_ada(K, l, mods, gains, extra=None):
    nc = K.nc
    full, free, silued, cleared = K.products, K.counter("ada_free"), K.counter("ada_silued"), K.counter("ada_cleared")
    turned, added, gained = K.counter("ada_turned"), K.counter("ada_added"), K.counter("ada_gained")
    g0, tiles = K.used, 12
    with K.stage() as st:
        row = K.sb("ada_row", [P, 2, 512], ctx=st)
        c = K.sb("ada_c", [P, KC, 32], ctx=st)
        parts = K.sb("ada_parts", [P, 2], ctx=st)
        ps = K.ps("ada_ps", [P, 2, 512], st)
        t_ps = K.ps("ada_t", [P, 512], st)
        block = st.enter_context(nc.Block())

        @block.tensor
        def _(pe):
            def turn(t):
                pe.wait_ge(free.sem, free.at(t + 1))
                for i in range(4):
                    mm = pe.matmul(t_ps[:, 2 * (4 * t + i):2 * (4 * t + i) + 2], row[:, t % 2, i * P:(i + 1) * P], parts[:, :],
                                   start=True, stop=True)
                mm.then_inc(turned.sem, turned.tick())

            pe.wait_ge(silued.sem, silued.at(2))
            pe.wait_ge(cleared.sem, cleared.at(2))
            for t in range(tiles):
                w = K.tile(pe, g0 + t, KC)
                if t >= 2:
                    pe.wait_ge(free.sem, free.at(t - 1))
                for k in range(2):
                    for part in range(4):
                        mm = pe.matmul(ps[32 * part:32 * part + 32, t % 2, :], c[:, 2 * part + k, :], w[:, 2 * part + k, :],
                                       start=k == 0, stop=k == 1, tile_position=(0, 32 * part), skip_group_check=True)
                mm.then_inc(full.sem, full.tick())
                K.done_at[g0 + t] = full.count
                if t:
                    turn(t - 1)
            turn(tiles - 1)

        @block.scalar
        def _(act):
            act.wait_ge(cleared.sem, cleared.at(1))
            for v, name in enumerate(("c", "c_ctx")):
                act.activation(c[:, :, v], K.params[:, K.cols[name]:K.cols[name] + KC], ACT.Silu).then_inc(silued.sem, silued.tick())
            for t in range(tiles):
                act.wait_ge(full.sem, full.at(t + 1))
                if t >= 2:
                    act.wait_ge(turned.sem, turned.at(t - 1))
                act.activation(row[:, t % 2, :], ps[:, t % 2, :], ACT.Copy).then_inc(free.sem, free.tick())

        @block.vector
        def _(dve):
            dve.memset(c[:, :, :], 0.0).then_inc(cleared.sem, cleared.tick())
            dve.tensor_reduce(parts[:, :], K.ident[:, :].rearrange("p (j r) -> p r j", j=4)[:, 0:2, :], AX.X,
                              ALU.add).then_inc(cleared.sem, cleared.tick())
            dve.wait_ge(turned.sem, turned.at(tiles))
            b0 = K.cols[f"ada_b{l}"]
            for v in range(2):
                dve.tensor_tensor(mods[:, v, :], t_ps[:, v:12 * KC:2], K.params[:, b0:b0 + 6 * KC], ALU.add).then_inc(added.sem, added.tick())
            dve.wait_ge(added.sem, added.at(2))
            for v in range(2):
                for i, (name, scale) in enumerate(((f"norm_mix{l}", 1), (f"norm_ffn{l}", 4))):
                    g = K.cols[name]
                    dve.scalar_tensor_tensor(out=gains[:, v, i, :], in0=mods[:, v, scale * KC:(scale + 1) * KC],
                                                       scalar=1.0, in1=K.params[:, g:g + KC], op0=ALU.add, op1=ALU.mult).then_inc(gained.sem, gained.tick())

        @block.sync
        def _(sp):
            K.issue(sp, g0 + tiles + RING)

        if extra:
            extra(block)
    K.used = g0 + tiles


def stage_add_gated(K, y, gate):
    with K.stage() as st:
        block = st.enter_context(K.nc.Block())

        @block.vector
        def _(dve):
            for c in range(KC):
                dve.scalar_tensor_tensor(out=K.xT[:, c, :], in0=y[:, c, 0:T], scalar=gate(c), in1=K.xT[:, c, :],
                                         op0=ALU.mult, op1=ALU.add)


def stage_delta_project(K, src, kT, v, qT, z):
    nc = K.nc
    full, base, conved, out = K.products, K.counter("dp_base"), K.counter("dp_conved"), K.counter("dp_out")
    g0 = K.used
    jobs = [(kT, KC, 2), (v, 2 * KC, 2), (qT, 0, 1), (z, None, 1)]
    with K.stage() as st:
        cv = K.sb("dp_cv", [P, 2, 2, T], ctx=st)
        ps = K.ps("dp_ps", [P, 4, 512], st)
        block = st.enter_context(nc.Block())

        @block.tensor
        def _(pe):
            q = 0
            for n, (dst, taps, segs) in enumerate(jobs):
                for t in range(2):
                    w = K.tile(pe, g0 + 2 * n + t, KC)
                    for j in range(4):
                        if q >= 4:
                            pe.wait_ge(conved.sem, conved.at(q - 3))
                        for k in range(KC):
                            mm = pe.matmul(ps[:, q % 4, 0:segs * T], w[:, k, j * P:(j + 1) * P], src[:, k, 0:segs * T],
                                           start=k == 0, stop=k == KC - 1)
                        mm.then_inc(full.sem, full.tick())
                        q += 1
                    K.done_at[g0 + 2 * n + t] = full.count

        @block.scalar
        def _(act):
            q = 0
            for dst, taps, segs in jobs:
                for c in range(KC):
                    act.wait_ge(full.sem, full.at(q + 1))
                    seg = ps[:, q % 4, 0:segs * T].rearrange("p (s t) -> p s t", s=segs)
                    if q >= 2:
                        act.wait_ge(out.sem, out.at(q - 1))
                    scale = 1.0 if taps is None else K.col("conv_a1", taps + c)
                    act.activation(cv[:, q % 2, 0:segs, :], seg, ACT.Copy, scale=scale).then_inc(base.sem, base.tick())
                    act.wait_ge(conved.sem, conved.at(q + 1))
                    act.activation(dst[:, c, 0:segs * T].rearrange("p (s t) -> p s t", s=segs),
                                          cv[:, q % 2, 0:segs, :], ACT.Silu).then_inc(out.sem, out.tick())
                    q += 1

        @block.vector
        def _(dve):
            own = K.own["dve"]
            q = 0
            for dst, taps, segs in jobs:
                for c in range(KC):
                    dve.wait_ge(base.sem, base.at(q + 1))
                    seg = ps[:, q % 4, 0:segs * T].rearrange("p (s t) -> p s t", s=segs)
                    b = cv[:, q % 2, 0:segs, :]
                    if taps is None:
                        dve.tensor_copy(b[:, :, 0:1], b[:, :, 0:1]).then_inc(conved.sem, conved.tick())
                    else:
                        dve.scalar_tensor_tensor(out=b[:, :, 1:T], in0=seg[:, :, 0:T - 1], scalar=K.col("conv_a0", taps + c),
                                                          in1=b[:, :, 1:T], op0=ALU.mult, op1=ALU.add).then_inc(own.sem, own.tick())
                        dve.wait_ge(own.sem, own.count)
                        dve.scalar_tensor_tensor(out=b[:, :, 0:T - 1], in0=seg[:, :, 1:T], scalar=K.col("conv_a2", taps + c),
                                                           in1=b[:, :, 0:T - 1], op0=ALU.mult, op1=ALU.add).then_inc(conved.sem, conved.tick())
                    q += 1

        @block.sync
        def _(sp):
            K.issue(sp, g0 + 8 + RING)
    K.used = g0 + 8


def stage_head_norm(K, S, t, n, scale, eps_scale=1.0, gain=None, times=None):
    nc = K.nc
    squared, summed, rooted, spread, scaled, done = (K.counter(x) for x in (
        "hn_squared", "hn_summed", "hn_rooted", "hn_spread", "hn_scaled", "hn_done"))
    inverted = K.counter("hn_inverted")
    with K.stage() as st:
        sq = K.sb("hn_sq", [P, 2, n], ctx=st)
        r = K.sb("hn_r", [NH, n], ctx=st)
        ps = K.ps("hn_ps", [P, 3, 512], st)
        block = st.enter_context(nc.Block())

        @block.scalar
        def _(act):
            for h in range(NH):
                if h >= 2:
                    act.wait_ge(summed.sem, summed.at(h - 1))
                act.activation(sq[:, h % 2, :], t[:, h, 0:n], ACT.Square, scale=eps_scale ** 0.5).then_inc(squared.sem, squared.tick())
            act.wait_ge(summed.sem, summed.at(NH))
            act.activation(r[:, :], ps[0:NH, 0, 0:n], ACT.Sqrt, bias=K.epsb[0:NH, :]).then_inc(rooted.sem, rooted.tick())

        @block.tensor
        def _(pe):
            for h in range(NH):
                pe.wait_ge(squared.sem, squared.at(h + 1))
                pe.matmul(ps[0:NH, 0, 0:n], S["head_sum"][:, h, :], sq[:, h % 2, :], start=h == 0, stop=h == NH - 1).then_inc(summed.sem, summed.tick())
            pe.wait_ge(inverted.sem, inverted.at(1))
            for h in range(NH):
                if h >= 2:
                    pe.wait_ge(scaled.sem, scaled.at(h - 1))
                pe.matmul(ps[:, 1 + h % 2, 0:n], S["head_row"][:, h, :], r[:, :], start=True, stop=True).then_inc(spread.sem, spread.tick())

        @block.vector
        def _(dve):
            dve.wait_ge(rooted.sem, rooted.at(1))
            dve.reciprocal(r[:, :], r[:, :]).then_inc(inverted.sem, inverted.tick())
            for h in range(NH):
                dve.wait_ge(spread.sem, spread.at(h + 1))
                dve.scalar_tensor_tensor(out=t[:, h, 0:n], in0=t[:, h, 0:n],
                                                   scalar=scale if gain is None else gain, in1=ps[:, 1 + h % 2, 0:n],
                                                   op0=ALU.mult, op1=ALU.mult).then_inc(scaled.sem, scaled.tick())

        if times is not None:
            @block.gpsimd
            def _(pool):
                for h in range(NH):
                    pool.wait_ge(scaled.sem, scaled.at(h + 1))
                    pool.tensor_tensor(t[:, h, 0:n], t[:, h, 0:n], times[:, h, 0:n], ALU.mult).then_inc(done.sem, done.tick())


def delta_setup(K, S):
    loads, made = K.counter("delta_loads", 16), K.counter("delta_made")
    io = K.io

    def program(block):
        @block.gpsimd
        def _(pool):
            w = io["w_in_a_2"][0].rearrange("(k p) n -> p k n", p=P)[:, :, 4 * D:4 * D + 4 * NH]
            pool.dma_start(S["wg"][:, :, :], w).then_inc(loads.sem, loads.tick())
            for i, n in enumerate(("dt_bias_a_2", "a_log_a_2")):
                pool.dma_start(S["rows"][:, i, :], io[n].rearrange("a d h -> a (d h)").broadcast_to([P, 2 * NH])).then_inc(loads.sem, loads.tick())
            pool.dma_start(S["context"][:, :, :], io["ctx_2"][0].rearrange("(a p) d -> p a d", p=P)).then_inc(loads.sem, loads.tick())
            for l in range(2):
                for n, c in (("router_g_2", 0), ("router_e_2", N_GRP)):
                    w = io[n][l].rearrange("(k p) n -> p k n", p=P)
                    pool.dma_start(K.routers[:, l, :, c:c + w.shape[2]], w).then_inc(loads.sem, loads.tick())
            own = K.own["pool"]
            pool.memset(S["head_sum"][:, :, :], 0.0).then_inc(own.sem, own.tick())
            pool.wait_ge(own.sem, own.count)
            pool.memset(S["head_row"][:, :, :], 1.0).then_inc(own.sem, own.tick())
            pool.wait_ge(own.sem, own.count)
            pool.memset(S["level"][:, :, :, :], 0.0).then_inc(own.sem, own.tick())
            pool.wait_ge(own.sem, own.count)
            for h in range(NH):
                pool.memset(S["head_sum"][:, h, h:h + 1], 1.0).then_inc(made.sem, made.tick())
            pool.affine_select(out=S["head_row"][:, :, :], in_=S["head_row"][:, :, :], compare_op=ALU.is_equal, fill=0.0,
                                       base=0, pattern=[[1, NH], [0, P]], channel_multiplier=-1).then_inc(made.sem, made.tick())
            for k in range(7):
                s = 1 << k
                nb = P // (2 * s)
                for d in range(2):
                    m = S["level"][:, d, k, :].rearrange("p (b o i) -> p b o i", o=2, i=s)[:, :, d, :]
                    lo = s if d == 0 else 0
                    pool.memset(m, 1.0).then_inc(own.sem, own.tick())
                    pool.wait_ge(own.sem, own.count)
                    pool.affine_select(out=m, in_=m, compare_op=ALU.is_ge, fill=0.0, base=-lo,
                                                 pattern=[[-2 * s, nb], [0, s]], channel_multiplier=1).then_inc(own.sem, own.tick())
                    pool.wait_ge(own.sem, own.count)
                    pool.affine_select(out=m, in_=m, compare_op=ALU.is_ge, fill=0.0, base=lo + s - 1,
                                               pattern=[[2 * s, nb], [0, s]], channel_multiplier=-1).then_inc(made.sem, made.tick())
            pool.wait_ge(loads.sem, loads.at(8))

    return program


def stage_delta_gates(K, S, src):
    nc = K.nc
    full, took, added, size, gated, sums, out = (K.counter(x) for x in (
        "dg_full", "dg_took", "dg_added", "dg_size", "dg_gated", "dg_sums", "dg_out"))
    with K.stage() as st:
        a = K.sb("dg_a", [P, 2, 4, NH], ctx=st)
        b = K.sb("dg_b", [P, 2, 4, NH], ctx=st)
        ps = K.ps("dg_ps", [P, 2, 512], st)
        block = st.enter_context(nc.Block())
        prod = ps[:, 0, 0:P].rearrange("p (t f d h) -> p f d t h", t=4, f=2, d=2)
        flat = lambda x: x[:, :, :, :].rearrange("p d t h -> p (d t h)")

        @block.tensor
        def _(pe):
            for t in range(4):
                for k in range(KC):
                    mm = pe.matmul(ps[:, 0, 32 * t:32 * t + 32], src[:, k, t * P:(t + 1) * P], S["wg"][:, k, :],
                                   start=k == 0, stop=k == KC - 1)
            mm.then_inc(full.sem, full.tick())
            pe.wait_ge(gated.sem, gated.at(1))
            for d in range(2):
                pe.matmul(ps[:, 1, 32 * d:32 * d + 32], K.incl[:, d, :], a[:, d].rearrange("p t h -> p (t h)"), start=True, stop=True)
            pe.matmul(ps[:, 1, 64:128], K.ones[:, :], flat(a), start=True, stop=True).then_inc(sums.sem, sums.tick())

        @block.scalar
        def _(act):
            act.wait_ge(full.sem, full.at(1))
            for d in range(2):
                act.activation(S["beta"][:, d], prod[:, 0, d], ACT.Sigmoid).then_inc(took.sem, took.tick())
            act.wait_ge(added.sem, added.at(1))
            act.activation(b[:, :], a[:, :], ACT.Abs).then_inc(took.sem, took.tick())
            act.wait_ge(took.sem, took.at(3))
            act.activation(b[:, :], b[:, :], ACT.Exp, scale=-1.0).then_inc(took.sem, took.tick())
            act.wait_ge(took.sem, took.at(4))
            act.activation(b[:, :], b[:, :], ACT.Ln, bias=1.0).then_inc(size.sem, size.tick())
            act.activation(S["rows"][:, 1, :], S["rows"][:, 1, :], ACT.Exp).then_inc(size.sem, size.tick())
            act.wait_ge(out.sem, out.at(3))
            act.activation(S["egl"][:, :], S["gl"][:, :], ACT.Exp)
            act.activation(S["negegc"][:, :], S["gc"][:, :], ACT.Exp).then_inc(took.sem, took.tick())
            act.activation(S["ekd"][:, :], S["ekd"][:, :], ACT.Exp)

        @block.vector
        def _(dve):
            own = K.own["dve"]
            row = lambda i: S["rows"][:, i, :].rearrange("p (d h) -> p d h", d=2)
            dve.wait_ge(took.sem, took.at(2))
            for d in range(2):
                ins = dve.tensor_tensor(a[:, d], prod[:, 1, d], row(0)[:, d, :].unsqueeze(1).broadcast_to([P, 4, NH]), ALU.add)
                if d == 0:
                    ins.then_inc(own.sem, own.tick())
                    dve.wait_ge(own.sem, own.count)
            ins.then_inc(added.sem, added.tick())
            dve.wait_ge(size.sem, size.at(2))
            dve.scalar_tensor_tensor(out=b[:, :], in0=a[:, :], scalar=0.0, in1=b[:, :], op0=ALU.max, op1=ALU.add).then_inc(own.sem, own.tick())
            dve.wait_ge(own.sem, own.count)
            for d in range(2):
                ins = dve.scalar_tensor_tensor(out=a[:, d], in0=b[:, d], scalar=-1.0,
                                               in1=row(1)[:, d, :].unsqueeze(1).broadcast_to([P, 4, NH]), op0=ALU.mult, op1=ALU.mult)
                if d == 0:
                    ins.then_inc(own.sem, own.tick())
                    dve.wait_ge(own.sem, own.count)
            ins.then_inc(gated.sem, gated.tick())
            dve.wait_ge(sums.sem, sums.at(1))
            dve.tensor_copy(flat(S["gc"]), ps[:, 1, 0:64]).then_inc(out.sem, out.tick())
            dve.tensor_copy(flat(S["gl"]), ps[:, 1, 64:128]).then_inc(out.sem, out.tick())
            dve.wait_ge(out.sem, out.at(2))
            dve.tensor_tensor(flat(S["ekd"]), flat(S["gl"]), flat(S["gc"]), ALU.subtract).then_inc(out.sem, out.tick())
            dve.wait_ge(took.sem, took.at(5))
            dve.tensor_scalar(S["negegc"][:, :], S["negegc"][:, :], -1.0, None, ALU.mult)


def stage_turn_values(K, v):
    nc = K.nc
    turned, moved = K.counter("tv_turned"), K.counter("tv_moved")
    with K.stage() as st:
        ps = K.ps("tv_ps", [P, 2, 512], st)
        block = st.enter_context(nc.Block())

        @block.tensor
        def _(pe):
            for h in range(NH):
                if h >= 2:
                    pe.wait_ge(moved.sem, moved.at(h - 1))
                for t in range(4):
                    mm = pe.transpose(ps[:, h % 2, t * P:(t + 1) * P], v[:, h, t * P:(t + 1) * P], K.ident[:, :])
                mm.then_inc(turned.sem, turned.tick())

        @block.scalar
        def _(act):
            for h in range(NH):
                act.wait_ge(turned.sem, turned.at(h + 1))
                act.activation(v[:, h, :], ps[:, h % 2, :], ACT.Copy).then_inc(moved.sem, moved.tick())


CHAIN = ([("new", 0), ("state", 0)] +
         [(what, s) for s in (1, 2, 3) for what in ("read", "new", "state")])
ORDER = ((2, 3, 0, 1), (3, 2, 1, 0))
LEVELS = 7


def stage_delta(K, S, qT, kT, v):
    nc = K.nc
    names = ("gram", "gram_used", "turned", "kd", "diag", "sums", "diff", "masked", "decay", "decay_beta", "sums_used",
             "lt", "qd", "z", "t1", "uv", "x", "first", "chain_read", "rest", "new", "new_done", "state", "state_done", "o_taken")
    dl = {n: K.counter("dl_" + n) for n in names}
    with K.stage() as st:
        kd = K.sb("dl_kd", [P, 2, 2, 4, P], ctx=st)
        E = K.sb("dl_E", [P, 2, 4, P], ctx=st)
        Eb = K.sb("dl_Eb", [P, 2, 4, P], ctx=st)
        LT = K.sb("dl_LT", [P, 2, 4, P], ctx=st)
        X = K.sb("dl_X", [P, 2, 4, P], ctx=st)
        XT = K.sb("dl_XT", [P, 2, 2, 4, P], ctx=st)
        T1 = K.sb("dl_T1", [P, 2, 4, P], ctx=st)
        pt = K.sb("dl_pt", [P, 2, 2, 2, P], ctx=st)
        qd = K.sb("dl_qd", [P, 2, 2, T], ctx=st)
        er = K.sb("dl_er", [P, 2, T], ctx=st)
        Ss = K.sb("dl_S", [P, 2, P], ctx=st)
        res = K.sb("dl_res", [P, 2, P], ctx=st)
        vn = K.sb("dl_vn", [P, 2, P], ctx=st)
        g_ps = K.ps("dl_gram", [P, 4, P], st)
        a_ps = K.ps("dl_a", [P, 2, 4, P], st)
        b_ps = K.ps("dl_b", [P, 2, 4, P], st)
        c_ps = K.ps("dl_c", [P, 2, 4, P], st)
        o_ps = K.ps("dl_o", [P, 4, P], st)
        block = st.enter_context(nc.Block())
        wide = lambda ap, n: ap.unsqueeze(2).broadcast_to([P, n, P])
        col = lambda t, d, tile, h: t[:, d, tile, h:h + 1]
        ident4 = K.ident[:, :].unsqueeze(1).broadcast_to([P, 4, P])

        def schedule():
            yield "keys", 0, None
            yield "sums", 0, None
            for h in range(NH + 1):
                chain = iter(CHAIN if h else ())
                if h < NH:
                    yield "prep", h, None
                for k in range(LEVELS):
                    for what in ("cross", "join"):
                        if k == LEVELS - 1 and h + 1 < NH:
                            yield {"cross": "keys", "join": "sums"}[what], h + 1, None
                        if h < NH:
                            yield what, h, k
                        step = next(chain, None)
                        if step:
                            yield step[0], h - 1, step[1]

        @block.tensor
        def _(pe):
            for what, h, k in schedule():
                if what == "keys":
                    if h:
                        pe.wait_ge(dl["gram_used"].sem, dl["gram_used"].at(2 * h))
                    for t in range(4):
                        mm = pe.transpose(g_ps[:, t, :], kT[:, h, t * P:(t + 1) * P], K.ident[:, :])
                    mm.then_inc(dl["turned"].sem, dl["turned"].tick())
                elif what == "sums":
                    for d in range(2):
                        pe.wait_ge(dl["diag"].sem, dl["diag"].at(2 * h + d + 1))
                        if h:
                            pe.wait_ge(dl["t1"].sem, dl["t1"].at(2 * (LEVELS * h - 1) + d + 1))
                        for t in range(4):
                            mm = pe.matmul(a_ps[:, d, t, :], K.ones[:, :], Eb[:, d, t, :], start=True, stop=True)
                        mm.then_inc(dl["sums"].sem, dl["sums"].tick())
                elif what == "prep":
                    pe.wait_ge(dl["kd"].sem, dl["kd"].at(8 * (h + 1)))
                    for t in range(4):
                        pe.matmul(g_ps[:, t, :], kT[:, h, t * P:(t + 1) * P], kT[:, h, t * P:(t + 1) * P], start=True, stop=True)
                    if h:
                        pe.wait_ge(dl["x"].sem, dl["x"].at(2 * LEVELS * h))
                    for t in range(2):
                        mm = pe.matmul(b_ps[:, 0, t, :], kT[:, h, t * P:(t + 1) * P], qT[:, h, t * P:(t + 1) * P], start=True, stop=True)
                    mm.then_inc(dl["gram"].sem, dl["gram"].tick())
                elif what == "cross":
                    for d in range(2):
                        if k == 0:
                            pe.wait_ge(dl["lt"].sem, dl["lt"].at(2 * h + d + 1))
                            pe.wait_ge(dl["sums_used"].sem, dl["sums_used"].at(2 * h + d + 1))
                        else:
                            pe.wait_ge(dl["x"].sem, dl["x"].at(2 * (LEVELS * h + k - 1) + d + 1))
                        for t in range(4):
                            mm = pe.matmul(a_ps[:, d, t, :], LT[:, d, t, :], K.ident[:, :] if k == 0 else X[:, d, t, :],
                                           start=True, stop=True)
                        mm.then_inc(dl["z"].sem, dl["z"].tick())
                elif what == "join":
                    if k == 0:
                        continue
                    for d in range(2):
                        pe.wait_ge(dl["t1"].sem, dl["t1"].at(2 * (LEVELS * h + k) + d + 1))
                        if k == 1:
                            pe.wait_ge(dl["gram_used"].sem, dl["gram_used"].at(2 * h + 2))
                        for t in range(4):
                            if k < LEVELS - 1:
                                pe.matmul(a_ps[:, d, t, :], XT[:, h % 2, d, t, :], T1[:, d, t, :], start=True, stop=True)
                            mm = pe.matmul(b_ps[:, d, t, :], T1[:, d, t, :], XT[:, h % 2, d, t, :], start=True, stop=True)
                        mm.then_inc(dl["uv"].sem, dl["uv"].tick())
                elif what == "read":
                    for d in range(2):
                        t = ORDER[d][k]
                        pe.wait_ge(dl["state_done"].sem, dl["state_done"].at(2 * (3 * h + k - 1) + d + 1))
                        pe.matmul(c_ps[:, d, 0, :], kT[:, h, t * P:(t + 1) * P], Ss[:, d, :], start=True, stop=True).then_inc(dl["chain_read"].sem, dl["chain_read"].tick())
                elif what == "new":
                    for d in range(2):
                        t = ORDER[d][k]
                        if k == 0:
                            pe.wait_ge(dl["x"].sem, dl["x"].at(2 * (LEVELS * (h + 1) - 1) + d + 1))
                            if h:
                                pe.wait_ge(dl["state_done"].sem, dl["state_done"].at(2 * 3 * h))
                                pe.wait_ge(dl["new_done"].sem, dl["new_done"].at(2 * 4 * h))
                        else:
                            pe.wait_ge(dl["rest"].sem, dl["rest"].at(2 * (3 * h + k - 1) + d + 1))
                        rhs = v[:, h, t * P:(t + 1) * P] if k == 0 else res[:, d, :]
                        pe.matmul(c_ps[:, d, 1, :], XT[:, h % 2, d, t, :], rhs, start=True, stop=True).then_inc(dl["new"].sem, dl["new"].tick())
                elif what == "state":
                    for d in range(2):
                        t = ORDER[d][k]
                        pe.wait_ge(dl["new_done"].sem, dl["new_done"].at(2 * (4 * h + k) + d + 1))
                        if k >= 2:
                            if k == 2 and d == 0:
                                pe.wait_ge(dl["qd"].sem, dl["qd"].at(2 * h + 2))
                                if h:
                                    pe.wait_ge(dl["o_taken"].sem, dl["o_taken"].at(h))
                            pe.matmul(o_ps[:, t, :], Ss[:, d, :], qd[:, h % 2, d, t * P:(t + 1) * P],
                                      start=k == 2 and d == 0, stop=False, skip_group_check=True)
                            mm = pe.matmul(o_ps[:, t, :], vn[:, d, :], pt[:, h % 2, d, t, :],
                                           start=False, stop=k == 3 and d == 1, skip_group_check=True)
                        if k < 3:
                            mm = pe.matmul(c_ps[:, d, 2, :], kd[:, h % 2, d, t, :], vn[:, d, :], start=True, stop=True)
                        mm.then_inc(dl["state"].sem, dl["state"].tick())

        @block.gpsimd
        def _(pool):
            for what, h, k in schedule():
                if what == "sums":
                    for d in range(2):
                        if h:
                            pool.wait_ge(dl["lt"].sem, dl["lt"].at(2 * (h - 1) + d + 1))
                        pool.tensor_tensor(Eb[:, d], ident4, wide(S["gc"][:, d, :, h], 4), ALU.mult).then_inc(dl["diag"].sem, dl["diag"].tick())
                    for d in range(2):
                        pool.wait_ge(dl["diff"].sem, dl["diff"].at(2 * h + d + 1))
                        sign = 1 if d == 0 else -1
                        pool.affine_select(out=E[:, d], in_=E[:, d], compare_op=ALU.is_ge, fill=-BIG, base=0,
                                                           pattern=[[0, 4], [sign, P]], channel_multiplier=-sign).then_inc(dl["masked"].sem, dl["masked"].tick())
                        pool.wait_ge(dl["decay"].sem, dl["decay"].at(2 * h + d + 1))
                        pool.wait_ge(dl["sums_used"].sem, dl["sums_used"].at(2 * h + d + 1))
                        pool.tensor_tensor(Eb[:, d], E[:, d], wide(S["beta"][:, d, :, h], 4), ALU.mult).then_inc(dl["decay_beta"].sem, dl["decay_beta"].tick())
                        pool.tensor_tensor(qd[:, h % 2, d, :], qT[:, h, :], er[:, d, :], ALU.mult).then_inc(dl["qd"].sem, dl["qd"].tick())
                elif what == "join" and k == 0:
                    for d in range(2):
                        pool.wait_ge(dl["z"].sem, dl["z"].at(2 * LEVELS * h + d + 1))
                        mask = S["level"][:, 1 - d, 0, :].unsqueeze(1).broadcast_to([P, 4, P])
                        own = K.own["pool"]
                        pool.tensor_tensor(XT[:, h % 2, d], LT[:, d], mask, ALU.mult).then_inc(own.sem, own.tick())
                        pool.wait_ge(own.sem, own.count)
                        pool.tensor_tensor(XT[:, h % 2, d], ident4, XT[:, h % 2, d], ALU.subtract).then_inc(dl["first"].sem, dl["first"].tick())

        @block.scalar
        def _(act):
            for what, h, k in schedule():
                if what == "keys":
                    act.wait_ge(dl["turned"].sem, dl["turned"].at(h + 1))
                    for d in range(2):
                        for t in range(4):
                            act.activation(kd[:, h % 2, d, t, :], g_ps[:, t, :], ACT.Copy, scale=col(S["ekd"], d, t, h)).then_inc(dl["kd"].sem, dl["kd"].tick())
                elif what == "sums":
                    for d in range(2):
                        act.wait_ge(dl["diff"].sem, dl["diff"].at(2 * h + d + 1))
                        if h:
                            act.wait_ge(dl["qd"].sem, dl["qd"].at(2 * (h - 1) + d + 1))
                        act.activation(er[:, d, :], a_ps[:, d, 0:2, :].rearrange("p t i -> p (t i)"), ACT.Exp).then_inc(dl["sums_used"].sem, dl["sums_used"].tick())
                        act.wait_ge(dl["masked"].sem, dl["masked"].at(2 * h + d + 1))
                        act.activation(E[:, d], E[:, d], ACT.Exp).then_inc(dl["decay"].sem, dl["decay"].tick())
                elif what == "new":
                    for d in range(2):
                        t = ORDER[d][k]
                        act.wait_ge(dl["new"].sem, dl["new"].at(2 * (4 * h + k) + d + 1))
                        act.activation(vn[:, d, :], c_ps[:, d, 1, :], ACT.Copy, scale=col(S["beta"], d, t, h)).then_inc(dl["new_done"].sem, dl["new_done"].tick())
                elif what == "state" and k == 3:
                    act.wait_ge(dl["state"].sem, dl["state"].at(2 * (4 * h + 3) + 2))
                    act.activation(qT[:, h, :], o_ps[:, 0:2, :].rearrange("p t i -> p (t i)"), ACT.Copy).then_inc(dl["o_taken"].sem, dl["o_taken"].tick())

        @block.vector
        def _(dve):
            for what, h, k in schedule():
                if what == "sums":
                    for d in range(2):
                        dve.wait_ge(dl["sums"].sem, dl["sums"].at(2 * h + d + 1))
                        dve.tensor_tensor(E[:, d], a_ps[:, d], wide(S["gc"][:, d, :, h], 4), ALU.subtract).then_inc(dl["diff"].sem, dl["diff"].tick())
                elif what == "prep":
                    dve.wait_ge(dl["gram"].sem, dl["gram"].at(h + 1))
                    for d in range(2):
                        dve.wait_ge(dl["decay_beta"].sem, dl["decay_beta"].at(2 * h + d + 1))
                        dve.tensor_tensor(LT[:, d], g_ps[:, :, :], Eb[:, d], ALU.mult).then_inc(dl["lt"].sem, dl["lt"].tick())
                        dve.tensor_tensor(pt[:, h % 2, d], b_ps[:, 0, 0:2, :], E[:, d, 0:2], ALU.mult).then_inc(dl["gram_used"].sem, dl["gram_used"].tick())
                elif what == "cross":
                    for d in range(2):
                        dve.wait_ge(dl["z"].sem, dl["z"].at(2 * (LEVELS * h + k) + d + 1))
                        mask = S["level"][:, d, k, :].unsqueeze(1).broadcast_to([P, 4, P])
                        dve.tensor_tensor(T1[:, d], a_ps[:, d], mask, ALU.mult).then_inc(dl["t1"].sem, dl["t1"].tick())
                elif what == "join":
                    for d in range(2):
                        if k == 0:
                            dve.wait_ge(dl["t1"].sem, dl["t1"].at(2 * LEVELS * h + d + 1))
                            dve.wait_ge(dl["first"].sem, dl["first"].at(2 * h + d + 1))
                            dve.tensor_tensor(X[:, d], ident4, T1[:, d], ALU.subtract).then_inc(dl["x"].sem, dl["x"].tick())
                        else:
                            dve.wait_ge(dl["uv"].sem, dl["uv"].at(2 * ((LEVELS - 1) * h + k - 1) + d + 1))
                            if k < LEVELS - 1:
                                dve.tensor_tensor(X[:, d], X[:, d], a_ps[:, d], ALU.subtract)
                            dve.tensor_tensor(XT[:, h % 2, d], XT[:, h % 2, d], b_ps[:, d], ALU.subtract).then_inc(dl["x"].sem, dl["x"].tick())
                elif what == "read":
                    for d in range(2):
                        t = ORDER[d][k]
                        dve.wait_ge(dl["chain_read"].sem, dl["chain_read"].at(2 * (3 * h + k - 1) + d + 1))
                        dve.scalar_tensor_tensor(out=res[:, d, :], in0=c_ps[:, d, 0, :], scalar=col(S["negegc"], d, t, h),
                                                               in1=v[:, h, t * P:(t + 1) * P], op0=ALU.mult, op1=ALU.add).then_inc(dl["rest"].sem, dl["rest"].tick())
                elif what == "state" and k < 3:
                    for d in range(2):
                        t = ORDER[d][k]
                        dve.wait_ge(dl["state"].sem, dl["state"].at(2 * (4 * h + k) + d + 1))
                        if k == 0:
                            dve.tensor_copy(Ss[:, d, :], c_ps[:, d, 2, :]).then_inc(dl["state_done"].sem, dl["state_done"].tick())
                        else:
                            dve.scalar_tensor_tensor(out=Ss[:, d, :], in0=Ss[:, d, :], scalar=col(S["egl"], d, t, h),
                                                                         in1=c_ps[:, d, 2, :], op0=ALU.mult, op1=ALU.add).then_inc(dl["state_done"].sem, dl["state_done"].tick())


def stage_grid_conv(K, proj, dst):
    made, conved = K.counter("gc_made"), K.counter("gc_conved")
    with K.stage() as st:
        cv = K.sb("gc_cv", [P, KC, T], ctx=st)
        block = st.enter_context(K.nc.Block())

        @block.gpsimd
        def _(pool):
            for c in range(KC):
                pool.tensor_tensor(proj[:, 2 * KC + c, :], proj[:, KC + c, :], proj[:, 2 * KC + c, :], ALU.mult).then_inc(made.sem, made.tick())

        @block.vector
        def _(dve):
            own = K.own["dve"]
            for c in range(KC):
                dve.wait_ge(made.sem, made.at(c + 1))
                u, o = proj[:, 2 * KC + c, :], cv[:, c, :]
                dve.tensor_scalar(o, u, K.col("conv_b1", c), None, ALU.mult).then_inc(own.sem, own.tick())
                dve.wait_ge(own.sem, own.count)
                if c < KC // 2:
                    u, o = (x.rearrange("p (r w) -> p r w", w=GRID_W) for x in (u, o))
                    parts = ((0, o[:, :, 1:], u[:, :, :-1]), (2, o[:, :, :-1], u[:, :, 1:]))
                else:
                    parts = ((0, o[:, GRID_W:], u[:, :-GRID_W]), (2, o[:, :-GRID_W], u[:, GRID_W:]))
                for tap, to, of in parts:
                    dve.scalar_tensor_tensor(out=to, in0=of, scalar=K.col(f"conv_b{tap}", c), in1=to,
                                                      op0=ALU.mult, op1=ALU.add).then_inc(own.sem, own.tick())
                    dve.wait_ge(own.sem, own.count)
                dve.tensor_tensor(dst[:, c, :], cv[:, c, :], proj[:, c, :], ALU.mult)


def stage_router(K, l, hT, R):
    nc = K.nc
    full, tops, size, exps, chosen, counted, made = (K.counter(x) for x in (
        "rt_full", "rt_tops", "rt_size", "rt_exps", "rt_chosen", "rt_counted", "rt_made"))
    turned, moved = K.counter("rt_turned"), K.counter("rt_moved")
    NG = N_GRP + N_EXP
    with K.stage() as st:
        rw = K.routers[:, l]
        lg = K.sb("rt_lg", [P, TT, 8], ctx=st)
        le = K.sb("rt_le", [P, TT, N_EXP], ctx=st)
        top = K.sb("rt_top", [P, TT, 2, 8], ctx=st)
        idx = K.sb("rt_idx", [P, TT, 2, 8], U32, ctx=st)
        idf = K.sb("rt_idf", [P, TT, 2, 8], ctx=st)
        sel = K.sb("rt_sel", [P, TT, 8], ctx=st)
        ex = K.sb("rt_ex", [P, TT, 8], ctx=st)
        wt = K.sb("rt_wt", [P, TT, 2, N_EXP], ctx=st)
        iota = K.sb("rt_iota", [P, N_EXP], ctx=st)
        hot = K.sb("rt_hot", [P, TT, 3, N_EXP], ctx=st)
        l_ps = K.ps("rt_ps", [P, 512], st)
        c_ps = K.ps("rt_counts", [P, 512], st)
        t_ps = K.ps("rt_turn", [P, 2, 512], st)
        block = st.enter_context(nc.Block())

        @block.gpsimd
        def _(pool):
            pool.memset(lg[:, :, :], -BIG).then_inc(made.sem, made.tick())
            pool.memset(R["place"][:, :, N_EXP:], -1.0).then_inc(made.sem, made.tick())
            pool.memset(R["weight"][:, :, N_EXP:], 0.0).then_inc(made.sem, made.tick())
            pool.iota(iota[:, :], pattern=[[1, N_EXP]], base=0, channel_multiplier=0,
                              allow_small_or_imprecise_dtypes=True).then_inc(made.sem, made.tick())

        @block.tensor
        def _(pe):
            for t in range(TT):
                for k in range(KC):
                    mm = pe.matmul(l_ps[:, t * NG:(t + 1) * NG], hT[:, k, t * P:(t + 1) * P], rw[:, k, :],
                                   start=k == 0, stop=k == KC - 1)
            mm.then_inc(full.sem, full.tick())
            for q in range(TT * KC // 4):
                if q >= 2:
                    pe.wait_ge(moved.sem, moved.at(q - 1))
                a, c = divmod(4 * q, KC)
                for j in range(4):
                    mm = pe.transpose(t_ps[:, q % 2, j * P:(j + 1) * P], hT[:, c + j, a * P:(a + 1) * P], K.ident[:, :])
                mm.then_inc(turned.sem, turned.tick())
            pe.wait_ge(chosen.sem, chosen.at(1))
            pe.matmul(c_ps[:, 0:N_EXP], K.incl[:, 0, :], hot[:, 0, 2, :], start=True, stop=True)
            pe.matmul(c_ps[:, N_EXP:2 * N_EXP], K.incl[:, 0, :], hot[:, 1, 2, :], start=True, stop=False)
            pe.matmul(c_ps[:, N_EXP:2 * N_EXP], K.ones[:, :], hot[:, 0, 2, :], start=False, stop=True)
            pe.matmul(c_ps[:, 2 * N_EXP:3 * N_EXP], K.ones[:, :], hot[:, 0, 2, :], start=True, stop=False)
            pe.matmul(c_ps[:, 2 * N_EXP:3 * N_EXP], K.ones[:, :], hot[:, 1, 2, :], start=False,
                      stop=True).then_inc(counted.sem, counted.tick())

        @block.scalar
        def _(act):
            for q in range(TT * KC // 4):
                act.wait_ge(turned.sem, turned.at(q + 1))
                a, c = divmod(4 * q, KC)
                act.activation(R["tokens"][:, a, c * P:(c + 4) * P], t_ps[:, q % 2, :], ACT.Copy).then_inc(moved.sem, moved.tick())
            act.wait_ge(tops.sem, tops.at(1))
            for t in range(TT):
                act.activation(ex[:, t, 0:N_GRP], lg[:, t, 0:N_GRP], ACT.Exp, bias=sel[:, t, 4:5], accum_out=ex[:, t, 4:5]).then_inc(size.sem, size.tick())
            act.wait_ge(tops.sem, tops.at(2))
            for t in range(TT):
                act.activation(ex[:, t, 5:6], top[:, t, 1, 1:2], ACT.Exp, bias=sel[:, t, 5:6]).then_inc(exps.sem, exps.tick())

        @block.vector
        def _(dve):
            own = K.own["dve"]
            dve.wait_ge(made.sem, made.at(4))
            dve.wait_ge(full.sem, full.at(1))
            logits = l_ps[:, 0:TT * NG].rearrange("p (t n) -> p t n", t=TT)
            dve.tensor_copy(lg[:, :, 0:N_GRP], logits[:, :, 0:N_GRP]).then_inc(own.sem, own.tick())
            dve.wait_ge(own.sem, own.count)
            for t in range(TT):
                dve.max(top[:, t, 0, :], lg[:, t, :]).then_inc(own.sem, own.tick())
                dve.wait_ge(own.sem, own.count)
                dve.max_index(idx[:, t, 0, :], top[:, t, 0, :], lg[:, t, :]).then_inc(own.sem, own.tick())
                dve.wait_ge(own.sem, own.count)
            dve.tensor_copy(idf[:, :, 0, :], idx[:, :, 0, :]).then_inc(own.sem, own.tick())
            dve.wait_ge(own.sem, own.count)
            dve.tensor_scalar(sel[:, :, 4:5], top[:, :, 0, 0:1], -1.0, None, ALU.mult).then_inc(tops.sem, tops.tick())
            for t in range(TT):
                dve.tensor_scalar(sel[:, t, 0:N_GRP], iota[:, 0:N_GRP], idf[:, t, 0, 0:1], None, ALU.is_equal).then_inc(own.sem, own.tick())
                dve.wait_ge(own.sem, own.count)
            dve.tensor_scalar(sel[:, :, 0:N_GRP], sel[:, :, 0:N_GRP], -1.0, BIG, ALU.add, ALU.mult).then_inc(own.sem, own.tick())
            dve.wait_ge(own.sem, own.count)
            for t in range(TT):
                dve.tensor_tensor(le[:, t, :].rearrange("p (g e) -> p g e", g=N_GRP),
                                           logits[:, t, N_GRP:NG].rearrange("p (g e) -> p g e", g=N_GRP),
                                           sel[:, t, 0:N_GRP].unsqueeze(2).broadcast_to([P, N_GRP, E_GRP]), ALU.add).then_inc(own.sem, own.tick())
                dve.wait_ge(own.sem, own.count)
                dve.max(top[:, t, 1, :], le[:, t, :]).then_inc(own.sem, own.tick())
                dve.wait_ge(own.sem, own.count)
                dve.max_index(idx[:, t, 1, :], top[:, t, 1, :], le[:, t, :]).then_inc(own.sem, own.tick())
                dve.wait_ge(own.sem, own.count)
            dve.tensor_copy(idf[:, :, 1, :], idx[:, :, 1, :]).then_inc(own.sem, own.tick())
            dve.wait_ge(own.sem, own.count)
            dve.tensor_scalar(sel[:, :, 5:6], top[:, :, 1, 0:1], -1.0, None, ALU.mult).then_inc(tops.sem, tops.tick())
            dve.wait_ge(exps.sem, exps.at(2))
            dve.tensor_scalar(ex[:, :, 6:7], ex[:, :, 5:6], 1.0, None, ALU.add).then_inc(own.sem, own.tick())
            dve.wait_ge(own.sem, own.count)
            dve.tensor_tensor(ex[:, :, 6:7], ex[:, :, 6:7], ex[:, :, 4:5], ALU.mult).then_inc(own.sem, own.tick())
            dve.wait_ge(own.sem, own.count)
            dve.reciprocal(ex[:, :, 6:7], ex[:, :, 6:7]).then_inc(own.sem, own.tick())
            dve.wait_ge(own.sem, own.count)
            dve.tensor_tensor(ex[:, :, 7:8], ex[:, :, 6:7], ex[:, :, 5:6], ALU.mult).then_inc(own.sem, own.tick())
            dve.wait_ge(own.sem, own.count)
            for t in range(TT):
                for j in range(2):
                    dve.tensor_scalar(hot[:, t, j, :], iota[:, :], idf[:, t, 1, j:j + 1], None,
                                      ALU.is_equal).then_inc(own.sem, own.tick())
                    dve.wait_ge(own.sem, own.count)
                    dve.tensor_scalar(wt[:, t, j, :], hot[:, t, j, :], ex[:, t, 6 + j:7 + j], None,
                                      ALU.mult).then_inc(own.sem, own.tick())
                    dve.wait_ge(own.sem, own.count)
            dve.tensor_tensor(hot[:, :, 2, :], hot[:, :, 0, :], hot[:, :, 1, :], ALU.add).then_inc(chosen.sem, chosen.tick())
            dve.wait_ge(chosen.sem, chosen.at(1))
            dve.tensor_tensor(R["weight"][:, :, 0:N_EXP], wt[:, :, 0, :], wt[:, :, 1, :], ALU.add).then_inc(own.sem, own.tick())
            dve.wait_ge(own.sem, own.count)
            dve.wait_ge(counted.sem, counted.at(1))
            places = c_ps[:, 0:2 * N_EXP].rearrange("p (t e) -> p t e", t=TT)
            dve.tensor_tensor(R["place"][:, :, 0:N_EXP], places, hot[:, :, 2, :], ALU.mult).then_inc(own.sem, own.tick())
            dve.wait_ge(own.sem, own.count)
            dve.tensor_scalar(R["place"][:, :, 0:N_EXP], R["place"][:, :, 0:N_EXP], -1.0, None, ALU.add).then_inc(own.sem, own.tick())
            dve.wait_ge(own.sem, own.count)
            dve.tensor_scalar(R["left"][:, :, 0:N_EXP], R["place"][:, :, 0:N_EXP], float(SLOTS), None, ALU.is_ge).then_inc(own.sem, own.tick())
            dve.wait_ge(own.sem, own.count)
            dve.tensor_tensor(R["left"][:, :, 0:N_EXP], R["left"][:, :, 0:N_EXP], R["weight"][:, :, 0:N_EXP], ALU.mult).then_inc(own.sem, own.tick())
            dve.tensor_reduce(sel[:, 0, 6:7], c_ps[:, 2 * N_EXP:3 * N_EXP], AX.X, ALU.max).then_inc(own.sem, own.tick())
            dve.wait_ge(own.sem, own.count)
            dve.tensor_scalar(R["any_left"][:, :], sel[:, 0, 6:7], float(SLOTS), None, ALU.is_gt).then_inc(own.sem, own.tick())
            dve.wait_ge(own.sem, own.count)


def queue_experts(K, l):
    io = K.io
    for e in range(N_EXP):
        for n in ("w1_2", "w3_2"):
            K.queue((0, (KC, D_EXP), rows_of(io[n][l, e], 0, D_EXP)))
        K.queue((0, (4, D), rows_of(io["w2_2"][l, e], 0, D)))


def routing(K, part):
    R = {n: K.sb("route_" + n, [P, TT, N_EXP + 2], ctx=part) for n in ("place", "weight", "left")}
    R["tokens"] = K.sb("route_tokens", [P, TT, D], ctx=part)
    R["any_left"] = K.sb("route_any_left", [P, 1], I32, ctx=part)
    return R


def stage_experts(K, l, R, gate):
    nc, io = K.nc, K.io
    per, fc, H = 4, D_EXP // P, SLOTS
    rounds = N_EXP // per
    full = K.products
    names = ("cleared", "picked", "rows_moved", "up_moved", "silued", "xt_moved", "hidden", "back_moved", "y_moved", "out_rows")
    cleared, picked, rows_moved, up_moved, silued, xt_moved, hidden, back_moved, y_moved, out_rows = (K.counter("ex_" + x) for x in names)
    g0, tiles = K.used, 3 * per
    UP, ROWS_NEXT, TURN, XT_NEXT, BACK, Y = 1, 2, 3, 4, 5, 6
    EVENTS = 6
    with K.stage() as st:
        iota = K.sb("ex_iota", [P, 2, H], ctx=st)
        pick = K.sb("ex_pick", [P, 2, TT, H], ctx=st)
        give = K.sb("ex_give", [P, 2, TT, 2, H], ctx=st)
        rows = K.sb("ex_rows", [P, 512], ctx=st)
        xt = K.sb("ex_xt", [P, 2, 4, 2 * H], ctx=st)
        up = K.sb("ex_up", [P, 512], ctx=st)
        sil = K.sb("ex_sil", [P, fc, H], ctx=st)
        hid = K.sb("ex_hid", [P, fc, H], ctx=st)
        back = K.sb("ex_back", [P, 2, TT, P], ctx=st)
        ys = K.sb("ex_ys", [P, 2, 512], ctx=st)
        zero = K.sb("ex_zero", [P, 512], ctx=st)
        rows_ps = K.ps("ex_rows_ps", [P, 512], st)
        xt_ps = K.ps("ex_xt_ps", [P, 4, 2 * H], st)
        up_ps = K.ps("ex_up_ps", [P, 512], st)
        hid_ps = K.ps("ex_hid_ps", [P, fc, 2, H], st)
        y_ps = K.ps("ex_y_ps", [P, TT, 2, 512], st)
        block = st.enter_context(nc.Block())
        y_of_expert = hid_ps[:, :, :, :].rearrange("p f a s -> p (f a s)")
        p0 = full.base

        def group(e, n):
            return p0 + 2 + EVENTS * e + n

        for e in range(N_EXP):
            K.done_at[g0 + 3 * e] = K.done_at[g0 + 3 * e + 1] = group(e, UP)
            K.done_at[g0 + 3 * e + 2] = group(e, Y)

        @block.gpsimd
        def _(pool):
            pool.iota(iota[:, :, :], pattern=[[0, 2], [1, H]], base=0, channel_multiplier=0,
                      allow_small_or_imprecise_dtypes=True).then_inc(cleared.sem, cleared.tick())
            pool.memset(zero[:, :], 0.0).then_inc(cleared.sem, cleared.tick())

        @block.tensor
        def _(pe):
            def gather(b):
                for t in range(TT):
                    for n in range(2):
                        mm = pe.matmul(rows_ps[H * n:H * n + H, :], pick[:, b, t, :], R["tokens"][:, t, n * 512:(n + 1) * 512],
                                       start=t == 0, stop=t == TT - 1, skip_group_check=True)
                return mm

            def turn_gathered():
                for c in range(4):
                    mm = pe.transpose(xt_ps[:, c, :], rows[:, c * P:(c + 1) * P], K.ident[:, :])
                return mm

            def to_tokens(b):
                for t in range(TT):
                    for n in range(2):
                        r = slice(H * n, H * n + H)
                        mm = pe.matmul(y_ps[:, t, n, :], back[r, b, t, :], ys[r, b, :], start=False, stop=False, skip_group_check=True)
                return mm

            pe.wait_ge(cleared.sem, cleared.at(2))
            for t in range(TT):
                for n in range(2):
                    pe.matmul(y_ps[:, t, n, :], zero[:, 0:P], zero[:, :], start=True, stop=False, skip_group_check=True)
            pe.wait_ge(picked.sem, picked.at(1))
            gather(0).then_inc(full.sem, 1)
            pe.wait_ge(rows_moved.sem, rows_moved.at(1))
            turn_gathered().then_inc(full.sem, 1)
            with pe.Fori(0, rounds) as it:
                for j in range(per):
                    b, done = j % 2, it * per + j
                    w = [K.ring[(g0 + 3 * j + i) % RING][:, :].rearrange("p (k n) -> p k n", k=KC if i < 2 else fc) for i in range(3)]
                    pe.wait_ge(xt_moved.sem, it * per + xt_moved.at(j + 1))
                    for i in range(2):
                        pe.wait_ge(K.landed[(g0 + 3 * j + i) % RING], it * (16 * tiles // RING) + K.need[g0 + 3 * j + i])
                    for k in range(KC):
                        h = k // 4
                        for i in range(2):
                            mm = pe.matmul(up_ps[H * i:H * i + H, :], xt[:, b, k % 4, H * h:H * h + H], w[i][:, k, :],
                                           start=k == 0, stop=k == KC - 1, skip_group_check=True)
                    mm.then_inc(full.sem, 1)
                    pe.wait_ge(picked.sem, it * per + picked.at(j + 2))
                    pe.wait_ge(back_moved.sem, it * per + back_moved.at(j + 1))
                    gather(1 - b).then_inc(full.sem, 1)
                    pe.wait_ge(y_moved.sem, it * per + y_moved.at(j + 1))
                    to_tokens(1 - b)
                    pe.wait_ge(up_moved.sem, it * per + up_moved.at(j + 1))
                    for f in range(fc):
                        mm = pe.transpose(hid_ps[:, f].rearrange("p a s -> p (a s)"), up[:, f * P:(f + 1) * P], K.ident[:, :])
                    mm.then_inc(full.sem, 1)
                    pe.wait_ge(rows_moved.sem, it * per + rows_moved.at(j + 2))
                    turn_gathered().then_inc(full.sem, 1)
                    for t in range(TT):
                        mm = pe.transpose(rows_ps[:, t * P:(t + 1) * P], give[:, b, t].rearrange("p a s -> p (a s)"), K.ident[:, :])
                    mm.then_inc(full.sem, 1)
                    pe.wait_ge(hidden.sem, it * per + hidden.at(j + 1))
                    pe.wait_ge(K.landed[(g0 + 3 * j + 2) % RING], it * (16 * tiles // RING) + K.need[g0 + 3 * j + 2])
                    for f in range(fc):
                        for n in range(2):
                            mm = pe.matmul(y_of_expert[H * n:H * n + H, :], hid[:, f, :], w[2][:, f, n * 512:(n + 1) * 512],
                                           start=f == 0, stop=f == fc - 1, skip_group_check=True)
                    mm.then_inc(full.sem, 1)
            pe.wait_ge(back_moved.sem, back_moved.at(N_EXP + 1))
            pe.wait_ge(y_moved.sem, y_moved.at(N_EXP + 1))
            to_tokens((N_EXP - 1) % 2).then_inc(full.sem, 1)
            for q in range(TT * 2):
                t, n = divmod(q, 2)
                pe.wait_ge(out_rows.sem, out_rows.at(q + 1))
                for c in range(4):
                    mm = pe.transpose(y_ps[:, t, n, c * P:(c + 1) * P], R["tokens"][:, t, n * 512 + c * P:n * 512 + (c + 1) * P], K.ident[:, :])
                mm.then_inc(full.sem, 1)

        @block.scalar
        def _(act):
            act.wait_ge(cleared.sem, cleared.at(2))
            act.activation(back[:, 1, :, :].rearrange("p t s -> p (t s)"), zero[:, 0:TT * P], ACT.Copy).then_inc(back_moved.sem, 1)
            act.activation(ys[:, 1, :], zero[:, :], ACT.Copy).then_inc(y_moved.sem, 1)
            with act.Fori(0, rounds) as it:
                for j in range(per):
                    b = j % 2
                    act.wait_ge(full.sem, it * (per * EVENTS) + group(j, UP))
                    act.activation(up[:, :], up_ps[:, :], ACT.Copy).then_inc(up_moved.sem, 1)
                    act.wait_ge(full.sem, it * (per * EVENTS) + group(j, TURN))
                    act.activation(sil[:, :, :], hid_ps[:, :, 0, :], ACT.Silu).then_inc(silued.sem, 1)
                    act.wait_ge(full.sem, it * (per * EVENTS) + group(j, BACK))
                    act.activation(back[:, b, :, :].rearrange("p t s -> p (t s)"), rows_ps[:, 0:TT * P], ACT.Copy).then_inc(back_moved.sem, 1)
                    act.wait_ge(full.sem, it * (per * EVENTS) + group(j, Y))
                    act.activation(ys[:, b, :], y_of_expert, ACT.Copy).then_inc(y_moved.sem, 1)
            act.wait_ge(full.sem, group(N_EXP, 1))
            for q in range(TT * 2):
                t, n = divmod(q, 2)
                act.activation(R["tokens"][:, t, n * 512:(n + 1) * 512], y_ps[:, t, n, :], ACT.Copy).then_inc(out_rows.sem, out_rows.tick())

        @block.vector
        def _(dve):
            def make_pick(e, b):
                for t in range(TT):
                    dve.tensor_scalar(pick[:, b, t, :], iota[:, 0, :], R["place"][:, t, e], None, ALU.is_equal)
                for t in range(TT):
                    ins = dve.tensor_scalar(give[:, b, t, :, :], iota[:, :, :], R["place"][:, t, e], R["weight"][:, t, e],
                                            ALU.is_equal, ALU.mult)
                return ins

            dve.wait_ge(cleared.sem, cleared.at(1))
            make_pick(slice(0, 1), 0).then_inc(picked.sem, 1)
            make_pick(slice(1, 2), 1).then_inc(picked.sem, 1)
            dve.wait_ge(full.sem, p0 + 1)
            dve.tensor_copy(rows[:, :], rows_ps[:, :]).then_inc(rows_moved.sem, 1)
            dve.wait_ge(full.sem, p0 + 2)
            dve.tensor_copy(xt[:, 0, :, :], xt_ps[:, :, :]).then_inc(xt_moved.sem, 1)
            with dve.Fori(0, rounds) as it:
                for j in range(per):
                    b = j % 2
                    dve.wait_ge(full.sem, it * (per * EVENTS) + group(j, ROWS_NEXT))
                    dve.tensor_copy(rows[:, :], rows_ps[:, :]).then_inc(rows_moved.sem, 1)
                    dve.wait_ge(silued.sem, it * per + silued.at(j + 1))
                    dve.tensor_tensor(hid[:, :, :], sil[:, :, :], hid_ps[:, :, 1, :], ALU.mult).then_inc(hidden.sem, 1)
                    dve.wait_ge(full.sem, it * (per * EVENTS) + group(j, XT_NEXT))
                    dve.tensor_copy(xt[:, 1 - b, :, :], xt_ps[:, :, :]).then_inc(xt_moved.sem, 1)
                    dve.wait_ge(full.sem, it * (per * EVENTS) + group(j, BACK))
                    make_pick(bass.ds(it * per + j + 2, 1), b).then_inc(picked.sem, 1)
            for q in range(TT * 2):
                t, n = divmod(q, 2)
                dve.wait_ge(full.sem, group(N_EXP, 2 + q))
                for c in range(4):
                    dve.scalar_tensor_tensor(out=K.xT[:, 4 * n + c, t * P:(t + 1) * P], in0=y_ps[:, t, n, c * P:(c + 1) * P],
                                             scalar=gate(4 * n + c), in1=K.xT[:, 4 * n + c, t * P:(t + 1) * P],
                                             op0=ALU.mult, op1=ALU.add)

        @block.sync
        def _(sp):
            K.issue(sp, g0 + RING)
            with sp.Fori(0, rounds - 1) as it:
                for m in range(tiles):
                    n = m + RING
                    e, kind = n // 3, n % 3
                    sp.wait_ge(full.sem, it * (per * EVENTS) + K.done_at[g0 + m])
                    w = io[("w1_2", "w3_2", "w2_2")[kind]][l][bass.ds(it * per + e, 1)]
                    src = w.rearrange("a (k p) n -> p (a k) n", p=P)
                    dst = K.ring[(g0 + n) % RING][:, :].rearrange("p (k n) -> p k n", k=fc if kind == 2 else KC)
                    sp.dma_start(dst, src).then_inc(K.landed[(g0 + n) % RING], 16)
            for m in range(tiles * (rounds - 1)):
                K.landed_count[(g0 + RING + m) % RING] += 16
            K.issued = g0 + RING + tiles * (rounds - 1)
            K.issue(sp, g0 + 3 * N_EXP + RING)

        full.count = group(N_EXP, 1 + TT * 2)
        for c in (up_moved, silued, hidden):
            c.count = c.base + N_EXP
        for c in (back_moved, y_moved, rows_moved, xt_moved):
            c.count = c.base + N_EXP + 1
        picked.count = picked.base + N_EXP + 2
    K.used = g0 + 3 * N_EXP


def stage_experts_left(K, l, hT, R, gate):
    nc, io = K.nc, K.io
    fc = D_EXP // P
    names = ("loads", "diag", "spread", "weights", "gate_up", "silued", "gated", "hidden", "y")
    loads, diag, spread, weights, gate_up, silued, gated, hidden, y_done = (
        K.ctx.enter_context(nc.semaphore(f"left{l}_{n}")) for n in names)
    with K.stage() as st:
        w1 = K.sb("lf_w1", [P, KC, D_EXP], ctx=st)
        w3 = K.sb("lf_w3", [P, KC, D_EXP], ctx=st)
        w2 = K.sb("lf_w2", [P, fc, D], ctx=st)
        dg = K.sb("lf_diag", [P, TT, P], ctx=st)
        wb = K.sb("lf_weights", [P, T], ctx=st)
        sil = K.sb("lf_sil", [P, T], ctx=st)
        hid = K.sb("lf_hid", [P, fc, T], ctx=st)
        zero = K.sb("lf_zero", [P, 512], ctx=st)
        w_ps = K.ps("lf_w_ps", [P, 512], st)
        gu = K.ps("lf_gu", [P, 2, 512], st)
        y = K.ps("lf_y", [P, 4, 512], st)
        block = st.enter_context(nc.Block())

        @block.sync
        def _(sp):
            left = sp.value_load(R["any_left"][0:1, 0:1], min_val=0, max_val=1)
            with sp.If(left > 0):
                with sp.Fori(0, N_EXP) as e:
                    sp.wait_ge(y_done, e + 1)
                    for w, name, k in ((w1, "w1_2", KC), (w3, "w3_2", KC), (w2, "w2_2", fc)):
                        sp.dma_start(w[:, :, :], io[name][l][bass.ds(e, 1)].rearrange("a (k p) n -> p (a k) n", p=P)).then_inc(loads, 16)

        @block.tensor
        def _(pe):
            left = pe.value_load(R["any_left"][0:1, 0:1], min_val=0, max_val=1)
            with pe.If(left > 0):
                pe.wait_ge(gated, 1)
                for b in range(4):
                    mm = pe.matmul(y[:, b, :], zero[:, 0:P], zero[:, :], start=True, stop=False, skip_group_check=True)
                mm.then_inc(y_done, 1)
                with pe.Fori(0, N_EXP) as e:
                    pe.wait_ge(diag, e + 1)
                    pe.matmul(w_ps[:, 0:T], K.ones[:, :], dg[:, :, :].rearrange("p t n -> p (t n)"), start=True, stop=True).then_inc(spread, 1)
                    pe.wait_ge(loads, e * 48 + 48)
                    for f in range(fc):
                        if f >= 2:
                            pe.wait_ge(hidden, e * fc + (f - 1))
                        for i, w in enumerate((w1, w3)):
                            for k in range(KC):
                                mm = pe.matmul(gu[:, f % 2, i * T:(i + 1) * T], w[:, k, f * P:(f + 1) * P], hT[:, k, :],
                                               start=k == 0, stop=k == KC - 1)
                        mm.then_inc(gate_up, 1)
                    pe.wait_ge(hidden, e * fc + fc)
                    for f in range(fc):
                        for c in range(KC):
                            mm = pe.matmul(y[:, c // 2, (c % 2) * T:(c % 2 + 1) * T], w2[:, f, c * P:(c + 1) * P], hid[:, f, :],
                                           start=False, stop=False, skip_group_check=True)
                    mm.then_inc(y_done, 1)

        @block.scalar
        def _(act):
            left = act.value_load(R["any_left"][0:1, 0:1], min_val=0, max_val=1)
            with act.If(left > 0):
                with act.Fori(0, N_EXP) as e:
                    for f in range(fc):
                        act.wait_ge(gated, e * fc + (f + 1))
                        act.wait_ge(gate_up, e * fc + (f + 1))
                        act.activation(sil[:, :], gu[:, f % 2, 0:T], ACT.Silu).then_inc(silued, 1)

        @block.vector
        def _(dve):
            left = dve.value_load(R["any_left"][0:1, 0:1], min_val=0, max_val=1)
            with dve.If(left > 0):
                dve.memset(zero[:, :], 0.0).then_inc(gated, 1)
                with dve.Fori(0, N_EXP) as e:
                    dve.wait_ge(y_done, e + 1)
                    for t in range(TT):
                        ins = dve.tensor_scalar(dg[:, t, :], K.ident[:, :], R["left"][:, t, bass.ds(e, 1)], None, ALU.mult)
                    ins.then_inc(diag, 1)
                    dve.wait_ge(spread, e + 1)
                    dve.tensor_copy(wb[:, :], w_ps[:, 0:T]).then_inc(weights, 1)
                    for f in range(fc):
                        dve.wait_ge(silued, e * fc + (f + 1))
                        dve.tensor_tensor(hid[:, f, :], sil[:, :], gu[:, f % 2, T:2 * T], ALU.mult).then_inc(gated, 1)
                        dve.wait_ge(weights, e + 1)
                        dve.wait_ge(gated, e * fc + (f + 2))
                        dve.tensor_tensor(hid[:, f, :], hid[:, f, :], wb[:, :], ALU.mult).then_inc(hidden, 1)
                dve.wait_ge(y_done, N_EXP + 1)
                for c in range(KC):
                    dve.scalar_tensor_tensor(out=K.xT[:, c, :], in0=y[:, c // 2, (c % 2) * T:(c % 2 + 1) * T], scalar=gate(c),
                                             in1=K.xT[:, c, :], op0=ALU.mult, op1=ALU.add)


def stage_output(K, src, out):
    nc = K.nc
    turned, moved, written = K.counter("out_turned"), K.counter("out_moved"), K.counter("out_written", 16)
    with K.stage() as st:
        rows = K.sb("out_rows", [P, TT, D], ctx=st)
        ps = K.ps("out_ps", [P, 2, 512], st)
        block = st.enter_context(nc.Block())
        quads = TT * KC // 4

        @block.tensor
        def _(pe):
            for q in range(quads):
                if q >= 2:
                    pe.wait_ge(moved.sem, moved.at(q - 1))
                a, c = divmod(4 * q, KC)
                for j in range(4):
                    mm = pe.transpose(ps[:, q % 2, j * P:(j + 1) * P], src[:, c + j, a * P:(a + 1) * P], K.ident[:, :])
                mm.then_inc(turned.sem, turned.tick())

        @block.vector
        def _(dve):
            for q in range(quads):
                dve.wait_ge(turned.sem, turned.at(q + 1))
                a, c = divmod(4 * q, KC)
                dve.tensor_copy(rows[:, a, c * P:(c + 4) * P], ps[:, q % 2, :]).then_inc(moved.sem, moved.tick())

        @block.sync
        def _(sp):
            for a in range(TT):
                sp.wait_ge(moved.sem, moved.at(2 * (a + 1)))
                sp.dma_start(out[0, a * P:(a + 1) * P, :], rows[:, a, :]).then_inc(written.sem, written.tick())
            sp.wait_ge(written.sem, written.at(TT))


def queue_second_block(K):
    io = K.io
    queue_columns(K, io["ada_w_2"][0], 6 * D)
    for c in (D, 2 * D, 0, 3 * D):
        for h in range(2):
            K.queue((0, (KC, 512), rows_of(io["w_in_a_2"][0], c + 512 * h, 512)))
    queue_columns(K, io["w_out_a_2"][0], D)
    queue_experts(K, 0)
    queue_columns(K, io["ada_w_2"][1], 6 * D)
    queue_columns(K, io["w_in_b_2"][0], 3 * D)
    queue_columns(K, io["w_out_b_2"][0], D)
    queue_experts(K, 1)


def second_block(K):
    mods = K.sb("mods", [P, 2, 6 * KC])
    gains = K.sb("gains", [P, 2, 2, KC])
    mod = lambda v, i: (lambda c: mods[:, v, i * KC + c:i * KC + c + 1])
    gain = lambda v, i: (lambda c: gains[:, v, i, c:c + 1])
    K.routers = K.sb("routers", [P, 2, KC, N_GRP + N_EXP])
    with ExitStack() as part:
        kT = K.sb("dn_kT", [P, NH, 2 * T], ctx=part)
        v = K.sb("dn_v", [P, NH, 2 * T], ctx=part)
        qT = K.sb("dn_qT", [P, NH, T], ctx=part)
        S = {n: K.sb("dn_" + n, [P, 2, 4, NH], ctx=part) for n in ("beta", "gc", "gl", "egl", "negegc", "ekd")}
        S["wg"] = K.sb("dn_wg", [P, KC, 4 * NH], ctx=part)
        S["rows"] = K.sb("dn_rows", [P, 2, 2 * NH], ctx=part)
        S["head_sum"] = K.sb("dn_head_sum", [P, NH, NH], ctx=part)
        S["head_row"] = K.sb("dn_head_row", [NH, NH, P], ctx=part)
        S["level"] = K.sb("dn_level", [P, 2, LEVELS, P], ctx=part)
        S["context"] = qT.rearrange("p h t -> p (h t)").rearrange("p (a d) -> p a d", a=TT)
        stage_ada(K, 0, mods, gains, delta_setup(K, S))
        with ExitStack() as K.part:
            src = K.sb("dn_src", [P, KC, 2 * T], ctx=K.part)
            turn_rows(K, None, kT[:, :, 0:T], "ctx", rows=S["context"])
            stage_norm(K, kT[:, :, 0:T], src[:, :, T:2 * T], gain(1, 0), shift=mod(1, 0))
            stage_norm(K, K.xT, src[:, :, 0:T], gain(0, 0), shift=mod(0, 0))
            stage_delta_project(K, src, kT, v, qT, K.hT)
            stage_delta_gates(K, S, src)
        stage_head_norm(K, S, kT, 2 * T, 1.0)
        stage_head_norm(K, S, qT, T, P ** -0.5)
        stage_turn_values(K, v)
        stage_delta(K, S, qT, kT, v)
        stage_head_norm(K, S, qT, T, 1.0, eps_scale=1.0 / P, gain=K.col("onorm"), times=K.hT)
        linear_stage(K, qT, KC, copy_to(kT[:, :, 0:T]))
        stage_add_gated(K, kT, mod(0, 2))
    with ExitStack() as part:
        R = routing(K, part)
        stage_norm(K, K.xT, K.hT, gain(0, 1), shift=mod(0, 3))
        stage_router(K, 0, K.hT, R)
        stage_experts(K, 0, R, mod(0, 5))
        stage_experts_left(K, 0, K.hT, R, mod(0, 5))
    stage_ada(K, 1, mods, gains)
    with ExitStack() as part:
        proj = K.sb("sc_proj", [P, 3 * KC, T], ctx=part)
        stage_norm(K, K.xT, K.hT, gain(0, 0), shift=mod(0, 0))
        linear_stage(K, K.hT, 3 * KC, copy_to(proj))
        stage_grid_conv(K, proj, K.hT)
        linear_stage(K, K.hT, KC, copy_to(proj))
        stage_add_gated(K, proj, mod(0, 2))
    with ExitStack() as part:
        R = routing(K, part)
        stage_norm(K, K.xT, K.hT, gain(0, 1), shift=mod(0, 3))
        stage_router(K, 1, K.hT, R)
        stage_experts(K, 1, R, mod(0, 5))
        stage_experts_left(K, 1, K.hT, R, mod(0, 5))
    stage_norm(K, K.xT, K.hT, lambda c: K.col("final", c))


def two_blocks(nc, io, out):
    with ExitStack() as ctx:
        K = Kit(nc, ctx, io)
        queue_first_block(K)
        queue_second_block(K)
        stage_setup(K)
        first_block(K)
        second_block(K)
        stage_output(K, K.hT, out)


INPUTS = (
    "x", "mem", "norm_mix_pre", "norm_mix_post", "w_in", "b_gate", "ssm_a_re", "ssm_a_im", "ssm_log_dt",
    "ssm_b_re", "ssm_b_im", "ssm_c_re", "ssm_c_im", "ssm_d", "ssm_w_glu", "ssm_b_glu", "w_branch_attn",
    "w_branch_ssm", "w_out", "norm_xa_pre", "norm_xa_post", "norm_mem", "xa_wq", "xa_wk", "xa_wv", "xa_wo",
    "norm_ffn_pre", "norm_ffn_post", "ffn_w_up", "ffn_conv_w", "ffn_conv_b", "ffn_w_down", "c_2", "ctx_2",
    "c_ctx_2", "ada_w_2", "ada_b_2", "norm_mix_2", "norm_ffn_2", "w_in_a_2", "conv_a_2", "a_log_a_2",
    "dt_bias_a_2", "onorm_a_2", "w_out_a_2", "w_in_b_2", "conv_b_2", "w_out_b_2", "router_g_2", "router_e_2",
    "w1_2", "w3_2", "w2_2", "final_norm_2",
)


def kernel(**inputs):
    import numpy as np
    import concourse.bacc as bacc
    from concourse.bass_utils import run_bass_kernel_spmd

    nc = bacc.Bacc("TRN2", target_bir_lowering=False, num_devices=1)
    arrays, io = {}, {}
    for name in INPUTS:
        a = np.ascontiguousarray(inputs[name])
        arrays[f"in_{name}"] = a
        io[name] = nc.dram_tensor(f"in_{name}", a.shape, mybir.dt.from_np(a.dtype), kind="ExternalInput").ap()
    out = nc.dram_tensor("out_0", (1, T, D), F32, kind="ExternalOutput").ap()
    two_blocks(nc, io, out)
    result = run_bass_kernel_spmd(nc, [arrays], core_ids=[0])
    return result.results[0]["out_0"]
```
